# Optimizing a Trainium2 kernel written in Bass

```python
import jax
import jax.numpy as jnp
from jax import lax
import numpy as np
import jax, jax.numpy as jnp

D_MODEL = 1024
BATCH = 1
SEQ = 1024
DEPTH = 1

GRID_W = 64
CTX_LEN = 256
N_MIXERS = 4
EPS = 1e-6
N_MOD = 6

FNET_GROUPS = 4
FNET_GROUP_DIM = D_MODEL // FNET_GROUPS

NA_HEADS = 16
NA_HEAD_DIM = D_MODEL // NA_HEADS
NA_WIN_ROWS = 8
NA_WIN_COLS = 16

SG_CHUNK = 128
SG_GROUPS = 4
SG_DIM = D_MODEL
SG_GROUP_DIM = SG_DIM // SG_GROUPS

ATT_HEADS = 16
ATT_KV_HEADS = 4
ATT_GROUP = ATT_HEADS // ATT_KV_HEADS
ATT_HEAD_DIM = D_MODEL // ATT_HEADS
ATT_Q_BLOCK = 128
ROPE_THETA = 10000.0

FFN_DIM = 2816
FFN_CONV = 3


def _layers_using(m):
    return (DEPTH - m + N_MIXERS - 1) // N_MIXERS

def rms_norm(x, g):
    xf = x.astype(jnp.float32)
    y = xf * lax.rsqrt(jnp.mean(xf * xf, axis=-1, keepdims=True) + EPS)
    return (y * g.astype(jnp.float32)).astype(x.dtype)

def modulate(h, g, shift, scale):
    return rms_norm(h, g) * (1 + scale) + shift

def ada_params(cond, w_mod, b_mod):
    m = jax.nn.silu(cond) @ w_mod + b_mod
    return jnp.split(m[:, None, :], N_MOD, axis=-1)

def depthwise_conv_seq(h, w, b):
    pad = FFN_CONV // 2
    y = lax.conv_general_dilated(h, w[:, None, :].astype(h.dtype), window_strides=(1,),
                                 padding=((pad, FFN_CONV - 1 - pad),),
                                 dimension_numbers=("NWC", "WIO", "NWC"),
                                 feature_group_count=h.shape[-1])
    return y + b

def conv_ffn(h, w_up, w_conv, b_conv, w_down):
    g, v = jnp.split(h @ w_up, 2, axis=-1)
    g = depthwise_conv_seq(g, w_conv, b_conv)
    return (jax.nn.silu(g) * v) @ w_down

def fourier_mix(a, w_out):
    B, L, D = a.shape
    ag = a.reshape(B, L, FNET_GROUPS, FNET_GROUP_DIM).astype(jnp.float32)
    f = jnp.fft.fft2(ag, axes=(1, 3), norm="ortho").real
    return f.astype(a.dtype).reshape(B, L, D) @ w_out

def spatial_gating_mix(a, w_in, g_v, w_s, b_s, w_out):
    B, L, _ = a.shape
    z = jax.nn.gelu(a @ w_in)
    u, v = jnp.split(z, 2, axis=-1)
    v = rms_norm(v, g_v)
    n = L // SG_CHUNK
    vg = v.reshape(B, n, SG_CHUNK, SG_GROUPS, SG_GROUP_DIM)
    mixed = jnp.einsum("gpq,bnqgc->bnpgc", w_s, vg) + b_s.T[None, None, :, :, None]
    return (u * mixed.reshape(B, L, SG_DIM)) @ w_out

def axial_rope(L):
    t = jnp.arange(L)
    row = (t // GRID_W).astype(jnp.float32)
    col = (t % GRID_W).astype(jnp.float32)
    n_freq = ATT_HEAD_DIM // 4
    inv_freq = ROPE_THETA ** (-jnp.arange(n_freq, dtype=jnp.float32) / n_freq)
    ang = jnp.concatenate([row[:, None] * inv_freq, col[:, None] * inv_freq], axis=-1)
    return jnp.cos(ang), jnp.sin(ang)

def apply_rope(x, cos, sin):
    xf = x.astype(jnp.float32)
    x1, x2 = jnp.split(xf, 2, axis=-1)
    c = cos[None, :, None, :]
    s = sin[None, :, None, :]
    return jnp.concatenate([x1 * c - x2 * s, x1 * s + x2 * c], axis=-1).astype(x.dtype)

def _gqa_attend(q, k, v):
    s = jnp.einsum("bqkgd,bskd->bkgqs", q, k).astype(jnp.float32) * (ATT_HEAD_DIM ** -0.5)
    p = jax.nn.softmax(s, axis=-1).astype(v.dtype)
    return jnp.einsum("bkgqs,bskd->bqkgd", p, v)

def gqa_mix(a_lat, a_ctx, w_qkv, g_q, g_k, w_out, need_ctx_out):
    B, L, _ = a_lat.shape
    H, KV, G, Dh = ATT_HEADS, ATT_KV_HEADS, ATT_GROUP, ATT_HEAD_DIM
    q, k, v = jnp.split(a_lat @ w_qkv, [H * Dh, (H + KV) * Dh], axis=-1)
    q = rms_norm(q.reshape(B, L, H, Dh), g_q)
    k = rms_norm(k.reshape(B, L, KV, Dh), g_k)
    v = v.reshape(B, L, KV, Dh)
    cos, sin = axial_rope(L)
    q = apply_rope(q, cos, sin)
    k = apply_rope(k, cos, sin)
    n_ctx = a_ctx.shape[1]
    kc, vc = jnp.split(a_ctx @ w_qkv[:, H * Dh:], 2, axis=-1)
    kc = rms_norm(kc.reshape(B, n_ctx, KV, Dh), g_k)
    vc = vc.reshape(B, n_ctx, KV, Dh)
    k_all = jnp.concatenate([k, kc], axis=1)
    v_all = jnp.concatenate([v, vc], axis=1)
    nblk = L // ATT_Q_BLOCK
    q_blocks = q.reshape(B, nblk, ATT_Q_BLOCK, KV, G, Dh).swapaxes(0, 1)
    o = lax.map(lambda qb: _gqa_attend(qb, k_all, v_all), q_blocks)
    y_lat = o.swapaxes(0, 1).reshape(B, L, H * Dh) @ w_out
    y_ctx = None
    if need_ctx_out:
        qc = rms_norm((a_ctx @ w_qkv[:, :H * Dh]).reshape(B, n_ctx, H, Dh), g_q)
        oc = _gqa_attend(qc.reshape(B, n_ctx, KV, G, Dh), kc, vc)
        y_ctx = oc.reshape(B, n_ctx, H * Dh) @ w_out
    return y_lat, y_ctx

def neighbourhood_mix(a_lat, a_ctx, w_qkv, rpb, w_out, need_ctx_out):
    B, L, D = a_lat.shape
    H, Dh = NA_HEADS, NA_HEAD_DIM
    rows = L // GRID_W
    kh = min(NA_WIN_ROWS, rows)
    kw = NA_WIN_COLS
    scale = Dh ** -0.5
    q, k, v = jnp.split(a_lat @ w_qkv, 3, axis=-1)
    n_ctx = a_ctx.shape[1]
    kc, vc = jnp.split(a_ctx @ w_qkv[:, D:], 2, axis=-1)
    kc = kc.reshape(B, n_ctx, H, Dh)
    vc = vc.reshape(B, n_ctx, H, Dh)
    k_grid = k.reshape(B, rows, GRID_W, H, Dh)
    v_grid = v.reshape(B, rows, GRID_W, H, Dh)
    col = jnp.arange(GRID_W)
    col_start = jnp.clip(col - kw // 2, 0, GRID_W - kw)
    col_idx = col_start[:, None] + jnp.arange(kw)[None, :]
    col_off = col_idx - col[:, None] + (NA_WIN_COLS - 1)
    q_rows = q.reshape(B, rows, GRID_W, H, Dh).swapaxes(0, 1)

    def row_block(args):
        r, q_r = args
        r_start = jnp.clip(r - kh // 2, 0, rows - kh)
        k_r = lax.dynamic_slice_in_dim(k_grid, r_start, kh, axis=1)[:, :, col_idx]
        v_r = lax.dynamic_slice_in_dim(v_grid, r_start, kh, axis=1)[:, :, col_idx]
        row_off = r_start + jnp.arange(kh) - r + (NA_WIN_ROWS - 1)
        bias = rpb[:, row_off[:, None, None], col_off[None, :, :]].astype(jnp.float32)
        s_nb = jnp.einsum("bwhd,bawjhd->bhwaj", q_r, k_r).astype(jnp.float32) * scale
        s_nb = (s_nb + bias.transpose(0, 2, 1, 3)[None]).reshape(B, H, GRID_W, kh * kw)
        s_ctx = jnp.einsum("bwhd,bchd->bhwc", q_r, kc).astype(jnp.float32) * scale
        p = jax.nn.softmax(jnp.concatenate([s_nb, s_ctx], axis=-1), axis=-1).astype(q_r.dtype)
        p_nb = p[..., :kh * kw].reshape(B, H, GRID_W, kh, kw)
        p_ctx = p[..., kh * kw:]
        return (jnp.einsum("bhwaj,bawjhd->bwhd", p_nb, v_r)
                + jnp.einsum("bhwc,bchd->bwhd", p_ctx, vc))

    o = lax.map(row_block, (jnp.arange(rows), q_rows))
    y_lat = o.swapaxes(0, 1).reshape(B, L, D) @ w_out
    y_ctx = None
    if need_ctx_out:
        qc = (a_ctx @ w_qkv[:, :D]).reshape(B, n_ctx, H, Dh)
        s = jnp.einsum("bqhd,bkhd->bhqk", qc, kc).astype(jnp.float32) * scale
        p = jax.nn.softmax(s, axis=-1).astype(vc.dtype)
        y_ctx = jnp.einsum("bhqk,bkhd->bqhd", p, vc).reshape(B, n_ctx, D) @ w_out
    return y_lat, y_ctx

def _normal(k, shape, scale):
    return jax.random.normal(k, shape, jnp.float32) * scale

def first_inputs(seed: int = 0) -> dict:
    key = jax.random.key(seed)
    ks = iter(jax.random.split(key, 32))
    D = D_MODEL
    inv = D ** -0.5
    n_a, n_b, n_c, n_d = (_layers_using(m) for m in range(N_MIXERS))
    qkv_dim = (ATT_HEADS + 2 * ATT_KV_HEADS) * ATT_HEAD_DIM
    return {
        "x": _normal(next(ks), (BATCH, SEQ, D), 1.0),
        "c": _normal(next(ks), (BATCH, D), 1.0),
        "ctx": _normal(next(ks), (BATCH, CTX_LEN, D), 1.0),
        "c_ctx": _normal(next(ks), (D,), 1.0),
        "w_mod": _normal(next(ks), (DEPTH, D, N_MOD * D), 0.5 * inv),
        "b_mod": _normal(next(ks), (DEPTH, N_MOD * D), 0.01),
        "g_norm_mix": 1.0 + _normal(next(ks), (DEPTH, D), 0.02),
        "g_norm_ffn": 1.0 + _normal(next(ks), (DEPTH, D), 0.02),
        "w_ffn_up": _normal(next(ks), (DEPTH, D, 2 * FFN_DIM), inv),
        "w_ffn_conv": _normal(next(ks), (DEPTH, FFN_CONV, FFN_DIM), FFN_CONV ** -0.5),
        "b_ffn_conv": _normal(next(ks), (DEPTH, FFN_DIM), 0.01),
        "w_ffn_down": _normal(next(ks), (DEPTH, FFN_DIM, D), FFN_DIM ** -0.5),
        "w_fnet_out": _normal(next(ks), (n_a, D, D), inv),
        "w_na_qkv": _normal(next(ks), (n_b, D, 3 * D), inv),
        "na_rel_bias": _normal(next(ks), (n_b, NA_HEADS, 2 * NA_WIN_ROWS - 1, 2 * NA_WIN_COLS - 1), 0.1),
        "w_na_out": _normal(next(ks), (n_b, D, D), inv),
        "w_sg_in": _normal(next(ks), (n_c, D, 2 * SG_DIM), inv),
        "g_sg_v": 1.0 + _normal(next(ks), (n_c, SG_DIM), 0.02),
        "w_sg_spatial": _normal(next(ks), (n_c, SG_GROUPS, SG_CHUNK, SG_CHUNK), SG_CHUNK ** -0.5),
        "b_sg_spatial": 1.0 + _normal(next(ks), (n_c, SG_GROUPS, SG_CHUNK), 0.01),
        "w_sg_out": _normal(next(ks), (n_c, SG_DIM, D), SG_DIM ** -0.5),
        "w_att_qkv": _normal(next(ks), (n_d, D, qkv_dim), inv),
        "g_att_q": 1.0 + _normal(next(ks), (n_d, ATT_HEAD_DIM), 0.02),
        "g_att_k": 1.0 + _normal(next(ks), (n_d, ATT_HEAD_DIM), 0.02),
        "w_att_out": _normal(next(ks), (n_d, ATT_HEADS * ATT_HEAD_DIM, D), (ATT_HEADS * ATT_HEAD_DIM) ** -0.5),
        "g_final": 1.0 + _normal(next(ks), (D,), 0.02),
    }

def first_block(x, c, ctx, c_ctx, w_mod, b_mod, g_norm_mix, g_norm_ffn, w_ffn_up, w_ffn_conv, b_ffn_conv,
              w_ffn_down, w_fnet_out, w_na_qkv, na_rel_bias, w_na_out, w_sg_in, g_sg_v, w_sg_spatial,
              b_sg_spatial, w_sg_out, w_att_qkv, g_att_q, g_att_k, w_att_out, g_final):
    h_lat, h_ctx = x, ctx
    for i in range(DEPTH):
        m, j = i % N_MIXERS, i // N_MIXERS
        last = i == DEPTH - 1
        ctx_in_needed = (not last) or m in (1, 3)
        sh1, sc1, gt1, sh2, sc2, gt2 = ada_params(c, w_mod[i], b_mod[i])
        a_lat = modulate(h_lat, g_norm_mix[i], sh1, sc1)
        if ctx_in_needed:
            csh1, csc1, cgt1, csh2, csc2, cgt2 = ada_params(c_ctx[None, :], w_mod[i], b_mod[i])
            a_ctx = modulate(h_ctx, g_norm_mix[i], csh1, csc1)
        if m == 0:
            y_lat = fourier_mix(a_lat, w_fnet_out[j])
            y_ctx = None if last else fourier_mix(a_ctx, w_fnet_out[j])
        elif m == 1:
            y_lat, y_ctx = neighbourhood_mix(a_lat, a_ctx, w_na_qkv[j], na_rel_bias[j], w_na_out[j], not last)
        elif m == 2:
            y_lat = spatial_gating_mix(a_lat, w_sg_in[j], g_sg_v[j], w_sg_spatial[j], b_sg_spatial[j], w_sg_out[j])
            y_ctx = None if last else spatial_gating_mix(a_ctx, w_sg_in[j], g_sg_v[j], w_sg_spatial[j],
                                                         b_sg_spatial[j], w_sg_out[j])
        else:
            y_lat, y_ctx = gqa_mix(a_lat, a_ctx, w_att_qkv[j], g_att_q[j], g_att_k[j], w_att_out[j], not last)
        h_lat = h_lat + gt1 * y_lat
        h_lat = h_lat + gt2 * conv_ffn(modulate(h_lat, g_norm_ffn[i], sh2, sc2),
                                       w_ffn_up[i], w_ffn_conv[i], b_ffn_conv[i], w_ffn_down[i])
        if not last:
            h_ctx = h_ctx + cgt1 * y_ctx
            h_ctx = h_ctx + cgt2 * conv_ffn(modulate(h_ctx, g_norm_ffn[i], csh2, csc2),
                                           w_ffn_up[i], w_ffn_conv[i], b_ffn_conv[i], w_ffn_down[i])
    return rms_norm(h_lat, g_final)


DEPTH_2 = 2

ROPE_BASE = 10000.0
NORM_EPS = 1e-6
MLA_HEADS = D_MODEL // 128
MLA_QK_NOPE = 128
MLA_QK_ROPE = 64
MLA_V_DIM = 128
MLA_Q_LORA = 3 * D_MODEL // 8
MLA_KV_LORA = D_MODEL // 8
ATTN_Q_BLOCK = 128
POOL_WINDOWS = (2, 4, 8, 16)
POOL_GROUPS = len(POOL_WINDOWS)
POOL_GROUP_DIM = D_MODEL // POOL_GROUPS
MIX_A = MLA_HEADS * MLA_V_DIM
MIX_B = POOL_GROUPS * POOL_GROUP_DIM
EVEN_MIX = MIX_A + MIX_B
EVEN_SPLITS = (MLA_Q_LORA, MLA_Q_LORA + MLA_KV_LORA, MLA_Q_LORA + MLA_KV_LORA + MLA_QK_ROPE,
               MLA_Q_LORA + MLA_KV_LORA + MLA_QK_ROPE + MIX_B)
EVEN_IN = EVEN_SPLITS[-1] + EVEN_MIX
RET_HEADS = D_MODEL // 256
RET_DK = 256
RET_DV = 512
RET_CHUNK = 128
RET_QK = RET_HEADS * RET_DK
RET_V = RET_HEADS * RET_DV
ODD_IN = 2 * RET_QK + 2 * RET_V
N_EVEN = (DEPTH_2 + 1) // 2
N_ODD = DEPTH_2 // 2


def rms_norm_2(x, g):
    xf = x.astype(jnp.float32)
    y = xf * lax.rsqrt(jnp.mean(xf * xf, axis=-1, keepdims=True) + NORM_EPS)
    return (y * g.astype(jnp.float32)).astype(x.dtype)

def rope_tables(positions, dim):
    inv = 1.0 / (ROPE_BASE ** (jnp.arange(0, dim, 2, dtype=jnp.float32) / dim))
    ang = positions.astype(jnp.float32)[..., None] * inv
    return jnp.cos(ang)[:, :, None, :], jnp.sin(ang)[:, :, None, :]

def apply_rope_2(x, cos, sin):
    half = x.shape[-1] // 2
    xf = x.astype(jnp.float32)
    x1, x2 = xf[..., :half], xf[..., half:]
    return jnp.concatenate([x1 * cos - x2 * sin, x2 * cos + x1 * sin], axis=-1).astype(x.dtype)

def mla(cq, ckv, kr, cos, sin, q_norm_g, w_uq, kv_norm_g, w_ukv):
    B_, T, _ = cq.shape
    dqk = MLA_QK_NOPE + MLA_QK_ROPE
    q = (rms_norm_2(cq, q_norm_g) @ w_uq).reshape(B_, T, MLA_HEADS, dqk)
    q = jnp.concatenate([q[..., :MLA_QK_NOPE], apply_rope_2(q[..., MLA_QK_NOPE:], cos, sin)], axis=-1)
    kv = (rms_norm_2(ckv, kv_norm_g) @ w_ukv).reshape(B_, T, MLA_HEADS, MLA_QK_NOPE + MLA_V_DIM)
    k_rope = apply_rope_2(kr[:, :, None, :], cos, sin)
    k = jnp.concatenate([kv[..., :MLA_QK_NOPE],
                         jnp.broadcast_to(k_rope, (B_, T, MLA_HEADS, MLA_QK_ROPE))], axis=-1)
    v = kv[..., MLA_QK_NOPE:]
    nb = T // ATTN_Q_BLOCK
    qb = q.reshape(B_, nb, ATTN_Q_BLOCK, MLA_HEADS, dqk).transpose(1, 0, 2, 3, 4)
    scale = dqk ** -0.5

    def attend(q_blk):
        s = jnp.einsum('bqhd,bkhd->bhqk', q_blk, k, preferred_element_type=jnp.float32) * scale
        p = jax.nn.softmax(s, axis=-1).astype(v.dtype)
        return jnp.einsum('bhqk,bkhd->bqhd', p, v)

    o = lax.map(attend, qb)
    return o.transpose(1, 0, 2, 3, 4).reshape(B_, T, MIX_A)

def multiscale_pool(u, pool_w, pool_scale):
    B_, T, _ = u.shape
    uf = u.reshape(B_, T, POOL_GROUPS, POOL_GROUP_DIM).astype(jnp.float32)
    cs = jnp.concatenate([jnp.zeros_like(uf[:, :1]), jnp.cumsum(uf, axis=1)], axis=1)
    t = jnp.arange(T)
    outs = []
    for g, w in enumerate(POOL_WINDOWS):
        left = w // 2
        right = w - 1 - left
        lo = jnp.clip(t - left, 0, T - 1)
        hi = jnp.clip(t + right, 0, T - 1)
        csg = cs[:, :, g]
        s = jnp.take(csg, hi + 1, axis=1) - jnp.take(csg, lo, axis=1)
        cnt = (hi - lo + 1).astype(jnp.float32)
        outs.append(s / cnt[None, :, None] - uf[:, :, g])
    d = jnp.stack(outs, axis=2).astype(u.dtype)
    y = jnp.einsum('btgc,gcd->btgd', d, pool_w) * pool_scale.reshape(POOL_GROUPS, POOL_GROUP_DIM)
    return y.reshape(B_, T, MIX_B)

def hybrid_attn_pool_layer(x, cos_a, sin_a, norm_g, w_in, q_norm_g, w_uq, kv_norm_g, w_ukv,
                           pool_w, pool_scale, w_out):
    h = rms_norm_2(x, norm_g)
    proj = h @ w_in
    cq, ckv, kr, u, gate = jnp.split(proj, list(EVEN_SPLITS), axis=-1)
    a = mla(cq, ckv, kr, cos_a, sin_a, q_norm_g, w_uq, kv_norm_g, w_ukv)
    b = multiscale_pool(u, pool_w, pool_scale)
    y = jnp.concatenate([a, b], axis=-1) * jax.nn.silu(gate)
    return y @ w_out

def retention_chunkwise(q, k, v, log_g, include_diag):
    B_, T, H, dk = q.shape
    dv = v.shape[-1]
    C = RET_CHUNK
    N = T // C
    to_chunks = lambda a: a.reshape(B_, N, C, H, a.shape[-1]).transpose(1, 0, 3, 2, 4)
    qc, kc, vc = to_chunks(q), to_chunks(k), to_chunks(v)
    idx = jnp.arange(C).astype(jnp.float32)
    diff = idx[:, None] - idx[None, :]
    mask = (diff >= 0) if include_diag else (diff > 0)
    dmat = jnp.where(mask[None], jnp.exp(jnp.where(mask, diff, 0.0)[None] * log_g[:, None, None]), 0.0)
    xi = jnp.exp((idx + 1.0)[None, :] * log_g[:, None])[None, :, :, None]
    zeta = jnp.exp((C - 1.0 - idx)[None, :] * log_g[:, None])[None, :, :, None]
    chunk_decay = jnp.exp(C * log_g)[None, :, None, None]

    def step(state, inp):
        q_i, k_i, v_i = inp
        scores = jnp.einsum('bhid,bhjd->bhij', q_i, k_i) * dmat
        o_in = jnp.einsum('bhij,bhjv->bhiv', scores, v_i)
        o_cross = jnp.einsum('bhid,bhdv->bhiv', q_i, state) * xi
        state = state * chunk_decay + jnp.einsum('bhjd,bhjv->bhdv', k_i * zeta, v_i)
        return state, o_in + o_cross

    s0 = jnp.zeros((B_, H, dk, dv), jnp.float32)
    _, o = lax.scan(step, s0, (qc, kc, vc))
    return o.transpose(1, 0, 3, 2, 4).reshape(B_, T, H, dv)

def retention_layer(x, cos_r, sin_r, norm_g, w_in, decay_fwd, decay_bwd, gn_g, w_out):
    B_, T, _ = x.shape
    h = rms_norm_2(x, norm_g)
    proj = h @ w_in
    q, k, v, gate = jnp.split(proj, [RET_QK, 2 * RET_QK, 2 * RET_QK + RET_V], axis=-1)
    q = apply_rope_2(q.reshape(B_, T, RET_HEADS, RET_DK), cos_r, sin_r).astype(jnp.float32)
    k = apply_rope_2(k.reshape(B_, T, RET_HEADS, RET_DK), cos_r, sin_r).astype(jnp.float32) * (RET_DK ** -0.5)
    v = v.reshape(B_, T, RET_HEADS, RET_DV).astype(jnp.float32)
    lf = jax.nn.log_sigmoid(decay_fwd.astype(jnp.float32))
    lb = jax.nn.log_sigmoid(decay_bwd.astype(jnp.float32))
    o_f = retention_chunkwise(q, k, v, lf, True)
    o_b = jnp.flip(retention_chunkwise(jnp.flip(q, 1), jnp.flip(k, 1), jnp.flip(v, 1), lb, False), 1)
    o = o_f + o_b
    mu = jnp.mean(o, axis=-1, keepdims=True)
    var = jnp.mean(jnp.square(o - mu), axis=-1, keepdims=True)
    o = ((o - mu) * lax.rsqrt(var + NORM_EPS)).reshape(B_, T, RET_V) * gn_g.astype(jnp.float32)
    y = o.astype(x.dtype) * jax.nn.silu(gate)
    return y @ w_out

def second_inputs(seed: int = 0) -> dict:
    key = jax.random.key(seed)
    ks = jax.random.split(key, 24)
    f32 = jnp.float32
    nrm = lambda k, shape, scale: jax.random.normal(k, shape, f32) * scale
    gain = lambda k, shape: 1.0 + 0.05 * jax.random.normal(k, shape, f32)
    x = jax.random.normal(ks[0], (BATCH, SEQ, D_MODEL), f32)
    positions = (jnp.arange(SEQ, dtype=jnp.int32)[None, :]
                 + jax.random.randint(ks[1], (BATCH, 1), 0, 4096, dtype=jnp.int32))
    base_decay = jnp.log(2.0 ** (5.0 + jnp.arange(RET_HEADS, dtype=f32)) - 1.0)
    return {
        'x': x,
        'positions': positions,
        'a_norm_g': gain(ks[2], (N_EVEN, D_MODEL)),
        'a_w_in': nrm(ks[3], (N_EVEN, D_MODEL, EVEN_IN), D_MODEL ** -0.5),
        'a_q_norm_g': gain(ks[4], (N_EVEN, MLA_Q_LORA)),
        'a_w_uq': nrm(ks[5], (N_EVEN, MLA_Q_LORA, MLA_HEADS * (MLA_QK_NOPE + MLA_QK_ROPE)), MLA_Q_LORA ** -0.5),
        'a_kv_norm_g': gain(ks[6], (N_EVEN, MLA_KV_LORA)),
        'a_w_ukv': nrm(ks[7], (N_EVEN, MLA_KV_LORA, MLA_HEADS * (MLA_QK_NOPE + MLA_V_DIM)), MLA_KV_LORA ** -0.5),
        'a_pool_w': nrm(ks[8], (N_EVEN, POOL_GROUPS, POOL_GROUP_DIM, POOL_GROUP_DIM), POOL_GROUP_DIM ** -0.5),
        'a_pool_scale': 1.0 + 0.1 * jax.random.normal(ks[9], (N_EVEN, MIX_B), f32),
        'a_w_out': nrm(ks[10], (N_EVEN, EVEN_MIX, D_MODEL), EVEN_MIX ** -0.5),
        'r_norm_g': gain(ks[11], (N_ODD, D_MODEL)),
        'r_w_in': nrm(ks[12], (N_ODD, D_MODEL, ODD_IN), D_MODEL ** -0.5),
        'r_decay_fwd': base_decay[None, :] + 0.1 * jax.random.normal(ks[13], (N_ODD, RET_HEADS), f32),
        'r_decay_bwd': base_decay[None, :] + 0.1 * jax.random.normal(ks[14], (N_ODD, RET_HEADS), f32),
        'r_gn_g': gain(ks[15], (N_ODD, RET_V)),
        'r_w_out': nrm(ks[16], (N_ODD, RET_V, D_MODEL), RET_V ** -0.5),
        'final_norm_g': gain(ks[17], (D_MODEL,)),
    }

def second_block(x, positions, a_norm_g, a_w_in, a_q_norm_g, a_w_uq, a_kv_norm_g, a_w_ukv,
              a_pool_w, a_pool_scale, a_w_out, r_norm_g, r_w_in, r_decay_fwd, r_decay_bwd,
              r_gn_g, r_w_out, final_norm_g):
    cos_a, sin_a = rope_tables(positions, MLA_QK_ROPE)
    cos_r, sin_r = rope_tables(positions, RET_DK)
    for layer in range(DEPTH_2):
        i = layer // 2
        if layer % 2 == 0:
            x = x + hybrid_attn_pool_layer(x, cos_a, sin_a, a_norm_g[i], a_w_in[i], a_q_norm_g[i],
                                           a_w_uq[i], a_kv_norm_g[i], a_w_ukv[i], a_pool_w[i],
                                           a_pool_scale[i], a_w_out[i])
        else:
            x = x + retention_layer(x, cos_r, sin_r, r_norm_g[i], r_w_in[i], r_decay_fwd[i],
                                    r_decay_bwd[i], r_gn_g[i], r_w_out[i])
    return rms_norm_2(x, final_norm_g)


def setup_inputs(seed=0):
    out = dict(first_inputs(seed))
    for name, value in second_inputs(seed + 1).items():
        if name != "x":
            out[name + "_2"] = value
    return out


def reference(
    x, c, ctx, c_ctx, w_mod, b_mod, g_norm_mix, g_norm_ffn, w_ffn_up, w_ffn_conv, b_ffn_conv,
    w_ffn_down, w_fnet_out, w_na_qkv, na_rel_bias, w_na_out, w_sg_in, g_sg_v, w_sg_spatial,
    b_sg_spatial, w_sg_out, w_att_qkv, g_att_q, g_att_k, w_att_out, g_final, positions_2,
    a_norm_g_2, a_w_in_2, a_q_norm_g_2, a_w_uq_2, a_kv_norm_g_2, a_w_ukv_2, a_pool_w_2,
    a_pool_scale_2, a_w_out_2, r_norm_g_2, r_w_in_2, r_decay_fwd_2, r_decay_bwd_2, r_gn_g_2,
    r_w_out_2, final_norm_g_2,
):
    x = first_block(
        x, c, ctx, c_ctx, w_mod, b_mod, g_norm_mix, g_norm_ffn, w_ffn_up, w_ffn_conv,
        b_ffn_conv, w_ffn_down, w_fnet_out, w_na_qkv, na_rel_bias, w_na_out, w_sg_in, g_sg_v,
        w_sg_spatial, b_sg_spatial, w_sg_out, w_att_qkv, g_att_q, g_att_k, w_att_out, g_final,
    )
    return second_block(
        x, positions_2, a_norm_g_2, a_w_in_2, a_q_norm_g_2, a_w_uq_2, a_kv_norm_g_2, a_w_ukv_2,
        a_pool_w_2, a_pool_scale_2, a_w_out_2, r_norm_g_2, r_w_in_2, r_decay_fwd_2,
        r_decay_bwd_2, r_gn_g_2, r_w_out_2, final_norm_g_2,
    )


_drawn_inputs = setup_inputs


def setup_inputs(seed=0):
    import zlib

    import numpy as np

    out = dict(_drawn_inputs(seed))
    spreads = {}
    factors = {'b_mod': 3.636,
     'g_norm_mix': 8.0,
     'g_norm_ffn': 6.438,
     'b_ffn_conv': 8.0,
     'a_q_norm_g_2': 8.0,
     'a_kv_norm_g_2': 8.0,
     'a_pool_scale_2': 4.788,
     'r_norm_g_2': 2.993,
     'r_gn_g_2': 6.817}
    for name, (base, spread) in spreads.items():
        noise = np.random.default_rng([zlib.crc32(name.encode()), seed]).standard_normal(out[name].shape)
        drawn = base * np.exp(spread * noise) if base else spread * noise
        out[name] = jnp.asarray(drawn.astype(out[name].dtype))
    for name, factor in factors.items():
        out[name] = (out[name] * factor).astype(out[name].dtype)
    return out
```

```python
from contextlib import ExitStack

import numpy as np

import concourse.bass as bass
from concourse import mybir

F32 = mybir.dt.float32
F32R = mybir.dt.float32r
I32 = mybir.dt.int32
ALU = mybir.AluOpType
ACT = mybir.ActivationFunctionType
AX_X = mybir.AxisListType.X

P = 128
D = 1024
L = 1024
KT = D // P
HALF = 512
EPS = 1e-6

FNET_G, FNET_C = 4, 256
FFN = 2816
FFN_T = FFN // P
Q_LORA, KV_LORA = 384, 128
HEADS, NOPE, ROPE, VDIM = 8, 128, 64, 128
ATT_SCALE = float((NOPE + ROPE) ** -0.5)
POOL_G, POOL_C = 4, 256
MIX = 2048
R_HEADS, R_DK, R_DV = 4, 256, 512
IB = 256
MASK_W = 2 * L - P

N_DFT, N_CDFT, N_FNET = 16, 1, KT
N_FFN = FFN_T // 2 * 6
N_A1 = 5 + KT + POOL_G
N_A2 = HEADS
N_MIX = MIX // P * 2
N_R2 = R_HEADS * 8
COUNTS = [N_DFT, N_CDFT, N_FNET, N_FFN, N_A1, N_A2, N_MIX, N_R2, N_MIX]
B_DFT, B_CDFT, B_FNET, B_FFN, B_A1, B_A2, B_A3, B_R2, B_R3, N_PANELS = [sum(COUNTS[:i]) for i in range(10)]

_COLS = [("c", KT), ("b_mod", 48), ("g_mix", KT), ("g_ffn", KT), ("conv", 3 * FFN_T), ("b_conv", FFN_T),
         ("g_final1", KT), ("a_norm", KT), ("q_norm", 3), ("kv_norm", 1), ("pool_scale", KT),
         ("r_norm", KT), ("gn", 16), ("final", KT), ("decay", 8),
         ("inv_a", 1), ("turn_a", 1), ("rad_a", 1), ("inv_r", 1), ("edge", 26)]
COL = {}
N_COL = 0
for _name, _n in _COLS:
    COL[_name] = N_COL
    N_COL += _n

TWO_PI = 2.0 * np.pi
C1 = 6.28125
C2 = float(np.float32(np.round((TWO_PI - C1) * 2.0 ** 21) / 2.0 ** 21))
C3 = float(np.float32(TWO_PI - C1 - C2))
ROUND = 1.5 * 2.0 ** 23
PI_IN = float(np.nextafter(np.float32(np.pi), np.float32(0)))

NORM_T = [KT, KT, KT, 3, 1, KT, KT]
NORM_N = [D, D, D, Q_LORA, KV_LORA, D, D]
SPLIT_T = [KT, KT, 3, 1, KT, KT]


def pool_window(g):
    return 2 << g


def pool_levels(g):
    out, lo, hi = [], 0, L
    for lv in range(g, -1, -1):
        a, b = (1, 0) if lv == 0 else (1 << (lv - 1), 1 << (lv - 1))
        out.append((a, b, lo, hi))
        lo, hi = lo - a, hi + b
    return out[::-1]


def edge_cols(g):
    at = COL["edge"] + sum(pool_window(q) - 1 for q in range(g))
    w = pool_window(g)
    return at, w // 2, w // 2 - 1


def pool_out(q):
    return (q // 2 + 1) % 2


def build(nc, xt_d, x_d, pan_d, wm_d, par_d, pos_d, ident_d, diff_d, out_d):
    ctx = ExitStack()
    with ctx:
        def place(name, shape, dt, at):
            with ExitStack() as s:
                if at:
                    s.enter_context(nc.sbuf_tensor(f"under_{name}", [P, at // 4], F32))
                return s.enter_context(nc.sbuf_tensor(name, shape, dt))

        def sem(name):
            return ctx.enter_context(nc.semaphore(name))

        K = 1024
        stage = place("stage", [P, 2, D], F32, 0)
        wh = place("wh", [P, 2, D], F32R, 8 * K)
        wl = place("wl", [P, 2, D], F32R, 16 * K)
        x = place("x", [P, KT, L], F32, 24 * K)
        hh = place("hh", [P, KT, L], F32R, 56 * K)
        hl = place("hl", [P, KT, L], F32R, 88 * K)
        par = place("par", [P, N_COL], F32, 120 * K)
        modc = place("modc", [P, 48], F32, 120 * K + 1200)
        s1 = place("s1", [P, KT], F32, 120 * K + 1392)
        s2 = place("s2", [P, KT], F32, 120 * K + 1424)
        sh2x = place("sh2x", [P, KT], F32, 120 * K + 1456)
        silu_c = place("silu_c", [P, KT], F32, 120 * K + 1488)
        rr = place("rr", [P, 8, KT], F32, 120 * K + 1520)
        stat = place("stat", [P, 64], F32, 120 * K + 1776)
        lgam = place("lgam", [P, 40], F32, 120 * K + 2032)
        nothing = place("nothing", [P, 1], F32, 120 * K + 3216)
        ident = place("ident", [P, P], F32, 120 * K + 2192)
        ones = place("ones", [P, P], F32, 120 * K + 2704)
        rb = place("rb", [P, L], F32, 124 * K)
        trig_a = place("trig_a", [P, L], F32, 128 * K)
        sqb = place("sqb", [P, 2, L], F32, 132 * K)
        nacc = place("nacc", [P, L], F32, 140 * K)
        diag = place("diag", [P, KT, P], F32, 144 * K)
        tt = place("tt", [P, 2, L], F32, 148 * K)
        WMC = 384
        wm = place("wm", [P, 2, KT * WMC], F32, 124 * K)
        macc = place("macc", [P, 6 * D], F32, 148 * K)
        pq = place("pq", [P, 16, HALF], F32, 172 * K)
        pqh = place("pqh", [P, 2, 2, D], F32R, 124 * K)
        pql = place("pql", [P, 2, 2, D], F32R, 140 * K)
        zt = place("zt", [P, 2, L], F32, 156 * K)
        vs = place("vs", [P, HALF], F32, 164 * K)
        posi = place("posi", [P, L], I32, 172 * K)
        posf = place("posf", [P, L], F32, 176 * K)
        ang = place("ang", [P, L], F32, 180 * K)
        turns = place("turns", [P, L], F32, 203 * K + 512)
        hidh = place("hidh", [P, 2, 2, L], F32R, 164 * K)
        hidl = place("hidl", [P, 2, 2, L], F32R, 180 * K)
        gbuf = place("gbuf", [P, L + 2], F32, 132 * K)
        conv = place("conv", [P, L], F32, 137 * K)
        act_g = place("act_g", [P, L], F32, 141 * K)
        hid = place("hid", [P, L], F32, 145 * K)
        cqh = place("cqh", [P, 3, L], F32R, 24 * K)
        cql = place("cql", [P, 3, L], F32R, 36 * K)
        ckh = place("ckh", [P, 1, L], F32R, 48 * K)
        ckl = place("ckl", [P, 1, L], F32R, 52 * K)
        krh = place("krh", [P, L], F32R, 156 * K)
        krl = place("krl", [P, L], F32R, 160 * K)
        cqf = place("cqf", [P, 4, L], F32, 164 * K)
        dh = place("dh", [P, 2, L], F32R, 164 * K)
        dl = place("dl", [P, 2, L], F32R, 172 * K)
        PADW = L + 16
        ub = [place(f"ub{i}", [P, PADW], F32, 180 * K + i * 4160) for i in range(4)]
        kt_t = place("kt_t", [P, L], F32, 180 * K + 4 * 4160)
        ks_t = place("ks_t", [P, L], F32, 180 * K + 4 * 4160 + 4096)
        yp = place("yp", [P, 2, L], F32, 180 * K + 4 * 4160)
        qnh = place("qnh", [P, 2, L], F32R, 56 * K)
        qnl = place("qnl", [P, 2, L], F32R, 64 * K)
        qrh = place("qrh", [P, 2, L], F32R, 72 * K)
        qrl = place("qrl", [P, 2, L], F32R, 80 * K)
        knh = place("knh", [P, 2, L], F32R, 88 * K)
        knl = place("knl", [P, 2, L], F32R, 96 * K)
        vvh = place("vvh", [P, 2, L], F32R, 104 * K)
        vvl = place("vvl", [P, 2, L], F32R, 112 * K)
        prob = place("prob", [P, 4, L], F32, 132 * K)
        osb = place("osb", [P, 2, 256], F32, 148 * K)
        rt = place("rt", [P, 2, HALF], F32, 150 * K)
        pth = place("pth", [P, 2, KT, 256], F32R, 164 * K)
        ptl = place("ptl", [P, 2, KT, 256], F32R, 180 * K)
        rs_t = place("rs_t", [P, 2, HALF], F32, 196 * K)
        rf_t = place("rf_t", [P, 2, HALF], F32, 200 * K)
        ybuf = place("ybuf", [P, 2, 2, L], F32, 132 * K)
        sg = place("sg", [P, L], F32, 196 * K)
        yg = place("yg", [P, L], F32, 200 * K)
        vrh = place("vrh", [P, KT, R_DV], F32R, 24 * K)
        vrl = place("vrl", [P, KT, R_DV], F32R, 40 * K)
        rqh = place("rqh", [P, 2, L], F32R, 132 * K)
        rql = place("rql", [P, 2, L], F32R, 140 * K)
        rkh = place("rkh", [P, 2, L], F32R, 148 * K)
        rkl = place("rkl", [P, 2, L], F32R, 156 * K)
        rph = place("rph", [P, KT, IB], F32R, 164 * K)
        rpl = place("rpl", [P, KT, IB], F32R, 172 * K)
        cos_r = place("cos_r", [P, L], F32, 187 * K + 512)
        sin_r = place("sin_r", [P, L], F32, 191 * K + 512)
        mask = place("mask", [P, MASK_W], F32, 180 * K)
        rta = place("rta", [P, 4, HALF], F32, 195 * K + 512)
        mtmp = place("mtmp", [P, MASK_W], F32, 195 * K + 512)
        rsm = place("rsm", [P, 2, IB], F32, 124 * K)
        roa = place("roa", [P, IB], F32, 126 * K)
        rinv = place("rinv", [P, IB], F32, 127 * K)
        rsq = place("rsq", [P, 2, IB], F32, 128 * K)
        rstd = place("rstd", [P, IB], F32, 130 * K)
        ro = place("ro", [P, 4, IB], F32, 203 * K + 512)

        ps = ctx.enter_context(nc.psum_tensor("ps", [P, 8, HALF], F32))
        xs_d = nc.dram_tensor("x_spill", (P, KT, L), F32).ap()
        y_d = nc.dram_tensor("y_spill", (16, P, L), F32).ap()

        panel_in = [sem("panel_in0"), sem("panel_in1")]
        nothing_set, w_hi, w_ready, w_used = sem("nothing_set"), sem("w_hi"), sem("w_ready"), sem("w_used")
        wm_in = [sem("wm_in0"), sem("wm_in1")]
        xt_in = [sem(f"xt_in{i}") for i in range(4)]
        par_in, ident_in, x_in, pos_in = sem("par_in"), sem("ident_in"), sem("x_in"), sem("pos_in")
        ones_set, zero_set, c_ready = sem("ones_set"), sem("zero_set"), sem("c_ready")
        row_ss, row_std, row_inv, xh_done, xl_done = [sem(n) for n in ("row_ss", "row_std", "row_inv", "xh_done", "xl_done")]
        mod_step, pq_ev, mod_mm, mod_ready, mod_s = [sem(n) for n in ("mod_step", "pq_ev", "mod_mm", "mod_ready", "mod_s")]
        pq_scaled, pq_hi, pq_lo, c_mm, v_copied, z_ev, z_hi, z_lo = [
            sem(n) for n in ("pq_scaled", "pq_hi", "pq_lo", "c_mm", "v_copied", "z_ev", "z_hi", "z_lo")]
        pos_float, trig_step, trig_sin = sem("pos_float"), sem("trig_step"), sem("trig_sin")
        fnet_ev = sem("fnet_ev")
        nm_sq, nm_acc, nm_ss, nm_std, nm_r, nm_dg, nm_rb, nm_rbs = [
            sem(n) for n in ("nm_sq", "nm_acc", "nm_ss", "nm_std", "nm_r", "nm_dg", "nm_rb", "nm_rbs")]
        sp_t, sp_hi, sp_lo = sem("sp_t"), sem("sp_hi"), sem("sp_lo")
        g_ev, cv_step, silu_done, hid_done, hid_hi, hid_lo, dn_mm, dn_ev = [
            sem(n) for n in ("g_ev", "cv_step", "silu_done", "hid_done", "hid_hi", "hid_lo", "dn_mm", "dn_ev")]
        x3_done, spilled = sem("x3_done"), sem("spilled")
        a_ev, pw_mm, kr_dve, kr_act, pool_step, pool_d, pool_hi, pool_lo = [
            sem(n) for n in ("a_ev", "pw_mm", "kr_dve", "kr_act", "pool_step", "pool_d", "pool_hi", "pool_lo")]
        yp_out = [sem("yp_out0"), sem("yp_out1")]
        aux_mm, aux_ev, ax_hi, rope_shift, rope_sum, rope_hi, rope_lo = [
            sem(n) for n in ("aux_mm", "aux_ev", "ax_hi", "rope_shift", "rope_sum", "rope_hi", "rope_lo")]
        sc_mm, row_max, row_bias, exp_done, sum_inv, prob_ok, tp_mm, tp_hi, tp_lo = [
            sem(n) for n in ("sc_mm", "row_max", "row_bias", "exp_done", "sum_inv", "prob_ok", "tp_mm", "tp_hi", "tp_lo")]
        o_out = [sem("o_out0"), sem("o_out1")]
        y_in = [sem("y_in0"), sem("y_in1")]
        diff_in, gam_step, gam_exp, mask_step, mask_exp = [
            sem(n) for n in ("diff_in", "gam_step", "gam_exp", "mask_step", "mask_exp")]
        r_ev, r_sum, r_hi, r_lo, v_sum, v_mean, v_hi, v_lo = [
            sem(n) for n in ("r_ev", "r_sum", "r_hi", "r_lo", "v_sum", "v_mean", "v_hi", "v_lo")]
        s_mm, s_ev, p_hi, p_lo, o_mm, o_ev, o_sq, o_acc, var_mm, var_std, var_inv, o_normed, r_out = [
            sem(n) for n in ("s_mm", "s_ev", "p_hi", "p_lo", "o_mm", "o_ev", "o_sq", "o_acc", "var_mm", "var_std",
                             "var_inv", "o_normed", "r_out")]
        done = sem("done")
        block = ctx.enter_context(nc.Block())

        def col(name, i=0, n=1):
            return par[:, COL[name] + i:COL[name] + i + n]

        def slot_of(panel):
            return panel % 2

        @block.sync
        def _(sp):
            for n in range(N_DFT):
                if n >= 2:
                    sp.wait_ge(w_ready, n - 1)
                sp.dma_start(stage[:, n % 2], pan_d[n]).then_inc(panel_in[n % 2], 16)
                if n >= 2:
                    sp.wait_ge(mod_step, KT * (n - 1))
                sp.dma_start(wm[:, n % 2], wm_d[n]).then_inc(wm_in[n % 2], 16)
            with sp.Fori(N_DFT // 2, N_PANELS // 2) as i:
                for j in range(2):
                    sp.wait_ge(w_ready, 2 * i + j - 1)
                    sp.dma_start(stage[:, j], pan_d[bass.ds(2 * i + j, 1)].rearrange("a p n -> p (a n)")
                                 ).then_inc(panel_in[j], 16)
            sp.wait_ge(done, 16 * KT)

        @block.gpsimd
        def _(pool):
            def split(n, j, landed):
                pool.wait_ge(panel_in[j], landed)
                nc.gpsimd.tensor_tensor(wh[:, j], stage[:, j], nothing[:].to_broadcast([P, D]), ALU.add).then_inc(w_hi, 1)
                pool.wait_ge(w_hi, n + 1)
                nc.gpsimd.tensor_tensor(wl[:, j], stage[:, j], wh[:, j].bitcast(F32),
                                        ALU.subtract).then_inc(w_ready, 1)

            nc.gpsimd.memset(nothing[:], 0.0).then_inc(nothing_set, 1)
            pool.wait_ge(nothing_set, 1)
            for j in range(2):
                split(j, j, 16)
            with pool.Fori(1, N_PANELS // 2) as i:
                for j in range(2):
                    pool.wait_ge(w_used, 2 * i + j - 1)
                    split(2 * i + j, j, 16 * i + 16)

        nb = [sum(NORM_T[:m]) for m in range(len(NORM_T))]
        sb = [sum(SPLIT_T[:q]) for q in range(len(SPLIT_T))]
        x_tiles = [x[:, k] for k in range(KT)]

        u_panel = [B_A1 + 5 + q + (q >= 4) + (q >= 6) for q in range(KT)]
        u_unit = [5 + q + 2 * (q >= 4) + 2 * (q >= 6) for q in range(KT)]
        pw_panel = [B_A1 + n for n in (9, 12, 15, 16)]
        pw_unit = [9, 13, 17, 19]

        def pv_unit(h, j, last):
            return 8 + 12 * h + j + (8 if j >= 2 and not last else 0)

        def pv_count(h, j, last):
            return 7 + 11 * h + j + 1 + (7 if j >= 2 and not last else 0)

        def proj_unit(h):
            return 0 if isinstance(h, int) and h == 0 else 12 * h - 2

        N_MC = MIX // P // 2

        @block.tensor
        def _(pe):
            def mm3(out, a_hi, a_lo, b_hi, b_lo, first, last):
                nc.tensor.matmul(out, a_hi, b_lo, start=first, stop=False)
                nc.tensor.matmul(out, a_lo, b_hi, start=False, stop=False)
                return nc.tensor.matmul(out, a_hi, b_hi, start=False, stop=last)

            def linear(slot, bank, rhs_hi, rhs_lo, tiles=KT, blk=0, width=P):
                for h in range(2):
                    for k in range(tiles):
                        c = (blk + k) * P
                        last = mm3(ps[:width, bank + h], wh[:, slot, c:c + width], wl[:, slot, c:c + width],
                                   rhs_hi(k)[:, h * HALF:(h + 1) * HALF], rhs_lo(k)[:, h * HALF:(h + 1) * HALF],
                                   k == 0, k == tiles - 1)
                return last

            def norm_sums(m):
                pe.wait_ge(nm_acc, nb[m] + NORM_T[m])
                for t in range(KT):
                    last = nc.tensor.matmul(ps[:, 7, t:t + 1], nacc[:, t * P:(t + 1) * P], ones[:, 0:1],
                                            start=True, stop=True)
                last.then_inc(nm_ss, 1)

            def norm_spread(s):
                pe.wait_ge(nm_dg, KT * (s + 1))
                if s:
                    pe.wait_ge(nm_rbs, s)
                for t in range(KT):
                    last = nc.tensor.matmul(ps[:, 5 + t // 4, (t % 4) * P:(t % 4 + 1) * P], ones[:], diag[:, t],
                                            start=True, stop=True)
                last.then_inc(nm_rb, 1)

            def wait_split(q):
                pe.wait_ge(sp_lo, sb[q] + SPLIT_T[q])

            h_hi, h_lo = (lambda k: hh[:, k]), (lambda k: hl[:, k])

            for f0 in (0, 4):
                for t in range(KT):
                    n = f0 * 2 + t
                    pe.wait_ge(w_ready, n + 1)
                    if f0 == 0:
                        pe.wait_ge(xl_done, t + 1)
                    for f in range(4):
                        for c in range(2):
                            if f0 and t == 0:
                                pe.wait_ge(pq_ev, 2 * f + c + 1)
                            a = slice((f0 + f) * P, (f0 + f + 1) * P)
                            b = slice(c * HALF, (c + 1) * HALF)
                            last = mm3(ps[:, 2 * f + c], hh[:, t, a], hl[:, t, a], wh[:, n % 2, b], wl[:, n % 2, b],
                                       t == 0, t == KT - 1)
                    last.then_inc(w_used, 1)
            pe.wait_ge(mod_step, N_DFT * KT)
            pe.wait_ge(ones_set, 1)
            pe.wait_ge(pq_ev, 16)
            for c in range(48):
                last = nc.tensor.matmul(ps[:, 7, c:c + 1], macc[:, c * P:(c + 1) * P], ones[:, 0:1],
                                        start=True, stop=True)
            last.then_inc(mod_mm, 1)
            sc = slot_of(B_CDFT)
            pe.wait_ge(w_ready, B_CDFT + 1)
            for n in range(KT):
                g, m = n // 2, n % 2
                pe.wait_ge(pq_lo, 2 * g + 2)
                if n >= 3:
                    pe.wait_ge(z_ev, n - 2)
                for c in range(2):
                    for k in range(2):
                        blk = slice((c * 4 + m * 2 + k) * P, (c * 4 + m * 2 + k + 1) * P)
                        mm3(ps[:, 2 * (n % 3) + c], wh[:, sc, blk], wl[:, sc, blk],
                            pqh[:, g % 2, k, c * HALF:(c + 1) * HALF], pql[:, g % 2, k, c * HALF:(c + 1) * HALF],
                            k == 0, k == 1)
                if n >= 2:
                    pe.wait_ge(z_ev, n - 1)
                for k in range(2):
                    blk = slice((m * 2 + k) * P, (m * 2 + k + 1) * P)
                    last = mm3(ps[:, 6 + n % 2, 0:2], wh[:, sc, blk], wl[:, sc, blk],
                               pqh[:, g % 2, k, HALF:HALF + 2], pql[:, g % 2, k, HALF:HALF + 2], k == 0, k == 1)
                last.then_inc(w_used if n == KT - 1 else c_mm, 1)
            pe.wait_ge(z_lo, KT)
            with pe.Fori(0, KT // 2) as i:
                for j in range(2):
                    pe.wait_ge(w_ready, B_FNET + 1 + 2 * i + j)
                    pe.wait_ge(fnet_ev, 2 * i + j + 1)
                    linear(slot_of(B_FNET + j), 2 * j, h_hi, h_lo).then_inc(w_used, 1)
            norm_sums(0)
            norm_spread(0)
            wait_split(0)

            def up(c, base, first=False):
                for q in range(2):
                    T = 2 * c + q
                    for v in range(2):
                        pe.wait_ge(w_ready, base + 2 * q + v + 1)
                        if not (first and q == 0):
                            pe.wait_ge(hid_done if v else g_ev, T)
                        linear(slot_of(B_FFN + 2 * q + v), 2 * v, h_hi, h_lo).then_inc(w_used, 1)

            def down(c, par_c, base, slot0, Tb=0):
                pe.wait_ge(hid_lo, Tb + 2 * c + 2)
                for m in range(KT):
                    d, mm = m // 4, m % 4
                    if mm == 0:
                        pe.wait_ge(w_ready, base + d + 1)
                    pe.wait_ge(dn_ev, dn_base + 8 * c + m + 1)
                    last = linear((slot0 + d) % 2, 4 + 2 * (m % 2), lambda k: hidh[:, par_c, k],
                                  lambda k: hidl[:, par_c, k], tiles=2, blk=2 * mm)
                    last.then_inc(w_used if mm == 3 else dn_mm, 1)

            dn_base = 0
            up(0, B_FFN, first=True)
            with pe.Fori(0, FFN_T // 4) as i:
                for cc in range(2):
                    at = B_FFN + 4 + 12 * i + 6 * cc
                    up(2 * i + cc + 1, at)
                    down(2 * i + cc, cc, at + 4, slot_of(B_FFN))
            down(FFN_T // 2 - 1, 0, B_A1 - 2, slot_of(B_FFN))
            norm_sums(1)
            norm_spread(1)
            norm_sums(2)
            norm_spread(2)
            wait_split(1)

            def a1_unit(n, panel, **kw):
                if n >= 2:
                    pe.wait_ge(a_ev, n - 1)
                return linear(slot_of(panel), 2 * (n % 2), **kw)

            def a1_panel(n, panel):
                pe.wait_ge(w_ready, panel + 1)
                a1_unit(n, panel, rhs_hi=h_hi, rhs_lo=h_lo).then_inc(w_used, 1)

            def pool_mix(g):
                pe.wait_ge(w_ready, pw_panel[g] + 1)
                pe.wait_ge(pool_lo, 2 * g + 2)
                for m in range(2):
                    a1_unit(pw_unit[g] + m, pw_panel[g], rhs_hi=lambda k: dh[:, k], rhs_lo=lambda k: dl[:, k],
                            tiles=2, blk=2 * m).then_inc(w_used if m else pw_mm, 1)

            for n in range(5):
                a1_panel(n, B_A1 + n)
            a1_panel(u_unit[0], u_panel[0])
            norm_sums(3)
            a1_panel(u_unit[1], u_panel[1])
            norm_spread(3)
            a1_panel(u_unit[2], u_panel[2])
            norm_sums(4)
            norm_spread(4)
            a1_panel(u_unit[3], u_panel[3])
            pool_mix(0)
            for g in (1, 2):
                a1_panel(u_unit[2 * g + 2], u_panel[2 * g + 2])
                a1_panel(u_unit[2 * g + 3], u_panel[2 * g + 3])
                pool_mix(g)
            pool_mix(3)

            pe.sem_inc(tp_mm, 4)
            wait_split(3)
            pe.wait_ge(kr_dve, 3)
            pe.wait_ge(nm_rbs, 5)
            pe.wait_ge(a_ev, 21)

            def bank_of(a):
                if not (isinstance(a, int) and a < 2):
                    pe.wait_ge(aux_ev, a - 1)

            def project(h, b):
                a0 = proj_unit(h)
                slot = slot_of(B_A2 + b)
                pe.wait_ge(w_ready, B_A2 + 1 + h)
                for u in range(8):
                    kind, f = u // 2, u % 2
                    bank_of(a0 + u)
                    out = ps[:, 6 + u % 2]
                    tok = slice(f * HALF, (f + 1) * HALF)
                    if kind < 2:
                        for k in range(3):
                            c = slice((3 * kind + k) * P, (3 * kind + k + 1) * P)
                            last = mm3(out, wh[:, slot, c], wl[:, slot, c], cqh[:, k, tok], cql[:, k, tok],
                                       k == 0, k == 2)
                    elif kind == 2:
                        c = slice(6 * P, 7 * P)
                        last = mm3(out, wh[:, slot, c], wl[:, slot, c], ckh[:, 0, tok], ckl[:, 0, tok], True, True)
                    else:
                        c = slice(7 * P, 8 * P)
                        for t in range(4):
                            at = slice((4 * f + t) * P, (4 * f + t + 1) * P)
                            last = mm3(out[:, t * P:(t + 1) * P], ckh[:, 0, at], ckl[:, 0, at],
                                       wh[:, slot, c], wl[:, slot, c], True, True)
                    last.then_inc(w_used if u == 7 else aux_mm, 1)

            def scores(h, b, t):
                pe.wait_ge(exp_done, 8 * h + t + 1)
                q = slice(t * P, (t + 1) * P)
                for f in range(2):
                    out = ps[:, 2 * (t % 2) + f]
                    key = slice(f * HALF, (f + 1) * HALF)
                    mm3(out, qnh[:, b, q], qnl[:, b, q], knh[:, b, key], knl[:, b, key], True, False)
                    last = mm3(out, qrh[:ROPE, b, q], qrl[:ROPE, b, q], krh[:ROPE, key], krl[:ROPE, key], False, True)
                last.then_inc(sc_mm, 1)

            def turn_probs(h, t):
                pe.wait_ge(prob_ok, 8 * h + t + 1)
                pe.wait_ge(tp_lo, 8 * h + t + 1)
                for k in range(KT):
                    last = nc.tensor.transpose(ps[:, 4 + k // 4, (k % 4) * P:(k % 4 + 1) * P],
                                               prob[:, t % 4, k * P:(k + 1) * P], ident[:])
                last.then_inc(tp_mm, 1)

            def attend(h, b, j, last_head):
                pe.wait_ge(tp_lo, 8 * h + 2 * j + 3)
                bank_of(pv_unit(h, j, last_head))
                for k in range(KT):
                    v = slice(k * P, (k + 1) * P)
                    last = mm3(ps[:, 6 + j % 2, 0:256], vvh[:, b, v], vvl[:, b, v], pth[:, j % 2, k], ptl[:, j % 2, k],
                               k == 0, k == KT - 1)
                last.then_inc(aux_mm, 1)

            def head(h, b, last_head=False):
                pe.wait_ge(rope_lo, 2 * h + 2)
                pe.wait_ge(aux_ev, 12 * h + 6)
                scores(h, b, 0)
                scores(h, b, 1)
                for t in range(2, 8):
                    scores(h, b, t)
                    if t in (4, 6):
                        attend(h, b, t // 2 - 2, last_head)
                    turn_probs(h, t - 2)
                if not last_head:
                    project(h + 1, 1 - b)
                attend(h, b, 2, last_head)
                turn_probs(h, 6)
                turn_probs(h, 7)
                attend(h, b, 3, last_head)

            project(0, 0)
            pe.wait_ge(aux_ev, 8)
            with pe.Fori(0, HEADS // 2 - 1) as i:
                head(2 * i, 0)
                head(2 * i + 1, 1)
            head(HEADS - 2, 0)
            head(HEADS - 1, 1, last_head=True)

            def gate(c, base, Tb, first=False):
                for q in range(2):
                    pe.wait_ge(w_ready, base + q + 1)
                    if not first:
                        pe.wait_ge(silu_done, Tb + 2 * c + q - 1)
                    linear(q, 2 * q, h_hi, h_lo).then_inc(w_used, 1)

            def mix(f, B):
                nonlocal dn_base
                Tb, dn_base = FFN_T + 16 * f, 8 * (FFN_T // 2 + N_MC * f)
                gate(0, B, Tb, first=True)
                with pe.Fori(0, N_MC // 2 - 1) as i:
                    for cc in range(2):
                        c = 2 * i + cc
                        gate(c + 1, B + 2 + 4 * c, Tb)
                        down(c, cc, B + 4 + 4 * c, 0, Tb)
                gate(N_MC - 1, B + 4 * N_MC - 6, Tb)
                down(N_MC - 2, 0, B + 4 * N_MC - 4, 0, Tb)
                down(N_MC - 1, 1, B + 4 * N_MC - 2, 0, Tb)

            pe.wait_ge(aux_ev, pv_unit(HEADS - 1, 3, True) + 1)
            norm_spread(5)
            wait_split(4)
            mix(0, B_A3)
            norm_sums(5)
            norm_spread(6)
            wait_split(5)
            pe.wait_ge(nm_rbs, 7)

            def r_scores(h, ib):
                q = slice(ib * IB, (ib + 1) * IB)
                for j in range(KT):
                    s = ib * KT + j
                    if s < 3:
                        pe.wait_ge(v_lo, 8 * h + s + 1)
                    else:
                        pe.wait_ge(s_ev, 32 * h + s - 2)
                    key = slice(j * P, (j + 1) * P)
                    for k in range(2):
                        last = mm3(ps[:, s % 3, 0:IB], rkh[:, k, key], rkl[:, k, key], rqh[:, k, q], rql[:, k, q],
                                   k == 0, k == 1)
                    last.then_inc(s_mm, 1)

            def r_values(h, ib):
                if ib == 0:
                    pe.wait_ge(v_lo, 8 * h + 8)
                else:
                    pe.wait_ge(o_ev, 16 * h + 4 * ib)
                for j in range(KT):
                    pe.wait_ge(p_lo, 32 * h + 8 * ib + j + 1)
                    for m in range(4):
                        v = slice(m * P, (m + 1) * P)
                        last = mm3(ps[:, 4 + m, 0:IB], vrh[:, j, v], vrl[:, j, v], rph[:, j], rpl[:, j],
                                   j == 0, j == KT - 1)
                last.then_inc(o_mm, 1)

            def r_variance(h, ib):
                pe.wait_ge(o_acc, 16 * h + 4 * ib + 4)
                nc.tensor.matmul(ps[:, 3, 0:IB], ones[:], roa[:], start=True, stop=True).then_inc(var_mm, 1)

            with pe.Fori(0, R_HEADS) as h:
                base = B_R2 + 8 * h
                for n in range(4):
                    pe.wait_ge(w_ready, base + n + 1)
                    linear(n % 2, 2 * n, h_hi, h_lo).then_inc(w_used, 1)
                for n in range(4):
                    pe.wait_ge(w_ready, base + 4 + n + 1)
                    for t in range(KT):
                        if n == 0:
                            pe.wait_ge(r_ev, 4 * h + (2 if t < 4 else 4))
                        tok = slice(t * P, (t + 1) * P)
                        for kk in range(2):
                            c = slice(kk * R_DV, (kk + 1) * R_DV)
                            last = mm3(ps[:, t], hh[:, 2 * n + kk, tok], hl[:, 2 * n + kk, tok],
                                       wh[:, n % 2, c], wl[:, n % 2, c], n + kk == 0, n + kk == 4)
                    last.then_inc(w_used, 1)
                pe.wait_ge(r_lo, 8 * h + 8)
                r_scores(h, 0)
                for ib in range(L // IB):
                    r_values(h, ib)
                    if ib + 1 < L // IB:
                        r_scores(h, ib + 1)
                    r_variance(h, ib)
                pe.wait_ge(s_ev, 32 * h + 32)
                pe.wait_ge(var_std, 4 * h + 4)
                pe.wait_ge(o_ev, 16 * h + 16)
            mix(1, B_R3)
            norm_sums(6)
            norm_spread(7)

        @block.scalar
        def _(act):
            def copy(out, in_, **kw):
                return nc.scalar.activation(out, in_, ACT.Copy, **kw)

            def norm_squares(m, src):
                for k in range(NORM_T[m]):
                    if k >= 2:
                        act.wait_ge(nm_acc, nb[m] + k - 1)
                    nc.scalar.activation(sqb[:, k % 2], src[k], ACT.Square).then_inc(nm_sq, 1)

            def norm_std(m):
                act.wait_ge(nm_ss, m + 1)
                nc.scalar.activation(stat[:, 0:KT], ps[:, 7, 0:KT], ACT.Sqrt, bias=stat[:, 60:61],
                                     scale=1.0 / NORM_N[m]).then_inc(nm_std, 1)

            def norm_bring(s):
                act.wait_ge(nm_rb, s + 1)
                copy(rb[:].rearrange("p (a n) -> p a n", a=2), ps[:, 5:7]).then_inc(nm_rbs, 1)

            def split_hi(q, dst, shift=None):
                for k in range(SPLIT_T[q]):
                    act.wait_ge(sp_t, sb[q] + k + 1)
                    if shift is None:
                        copy(dst(k), tt[:, k % 2]).then_inc(sp_hi, 1)
                    else:
                        nc.scalar.activation(dst(k), tt[:, k % 2], ACT.Identity, bias=shift(k)).then_inc(sp_hi, 1)

            h_dst = lambda k: hh[:, k]

            act.dma_start(par[:], par_d).then_inc(par_in, 16)
            for i in range(4):
                act.dma_start(x[:, 2 * i:2 * i + 2], xt_d[:, 2 * i:2 * i + 2]).then_inc(xt_in[i], 16)
            act.dma_start(ident[:], ident_d).then_inc(ident_in, 16)
            act.wait_ge(par_in, 16)
            nc.scalar.activation(silu_c[:], col("c", 0, KT), ACT.Silu).then_inc(c_ready, 1)
            for t in range(KT):
                if t % 2 == 0:
                    act.wait_ge(xt_in[t // 2], 16)
                if t >= 1:
                    act.wait_ge(row_ss, t)
                nc.scalar.activation(pq[:, 0:2].rearrange("p a n -> p (a n)"), x[:, t], ACT.Square,
                                     accum_out=stat[:, 8 + t:9 + t]).then_inc(row_ss, 1)
            act.wait_ge(row_ss, KT)
            act.wait_ge(zero_set, 3)
            nc.scalar.activation(stat[:, 16:24], stat[:, 8:16], ACT.Sqrt, bias=stat[:, 60:61],
                                 scale=1.0 / D).then_inc(row_std, 1)
            act.wait_ge(row_inv, 1)
            for t in range(KT):
                copy(hh[:, t], x[:, t], scale=rr[:, 7, t:t + 1]).then_inc(xh_done, 1)
            act.wait_ge(xl_done, KT)
            act.dma_start(x[:], x_d).then_inc(x_in, 16)
            for f0 in (0, 4):
                act.wait_ge(w_used, 2 * f0 + KT)
                for f in range(4):
                    for c in range(2):
                        copy(pq[:, 2 * (f0 + f) + c], ps[:, 2 * f + c]).then_inc(pq_ev, 1)

            def pq_split(f):
                act.wait_ge(pq_scaled, 3 * (f + 1))
                if f >= 4:
                    act.wait_ge(c_mm, 2 * (f // 2) - 2)
                copy(pqh[:, f // 2 % 2, f % 2], pq[:, 2 * f:2 * f + 2].rearrange("p a n -> p (a n)")).then_inc(pq_hi, 1)

            def v_copy(n):
                if n == KT - 1:
                    act.wait_ge(w_used, B_CDFT + 1)
                else:
                    act.wait_ge(c_mm, n + 1)
                if n >= 1:
                    act.wait_ge(z_ev, n)
                copy(vs[:], ps[:, 2 * (n % 3) + 1]).then_inc(v_copied, 1)

            def z_hi_copy(n):
                act.wait_ge(z_ev, n + 1)
                copy(hh[:, n], zt[:, n % 2]).then_inc(z_hi, 1)

            for f in range(2):
                pq_split(f)
            for g in range(4):
                if g < 3:
                    pq_split(2 * g + 2)
                    pq_split(2 * g + 3)
                for n in (2 * g, 2 * g + 1):
                    v_copy(n)
                    if n:
                        z_hi_copy(n - 1)
            z_hi_copy(KT - 1)
            act.wait_ge(z_lo, KT)
            act.dma_start(posi[:], pos_d).then_inc(pos_in, 16)
            act.wait_ge(trig_step, 8)
            nc.scalar.activation(trig_a[:], ang[:], ACT.Sin).then_inc(trig_sin, 1)

            act.wait_ge(fnet_ev, 2 + KT)
            norm_squares(0, x_tiles)
            norm_std(0)
            norm_bring(0)
            split_hi(0, h_dst, lambda k: modc[:, 24 + k:25 + k])

            act.wait_ge(zero_set, 4)

            def ffn_act(c, base, first=False):
                for q in range(2):
                    T = 2 * c + q
                    act.wait_ge(w_used, base + 2 * q + 1)
                    if not (first and q == 0):
                        act.wait_ge(cv_step, 3 * T)
                    copy(gbuf[:, 1:L + 1].rearrange("p (a n) -> p a n", a=2), ps[:, 0:2]).then_inc(g_ev, 1)
                    act.wait_ge(cv_step, 3 * T + 3)
                    nc.scalar.activation(act_g[:], conv[:], ACT.Silu).then_inc(silu_done, 1)
                    act.wait_ge(hid_done, T + 1)
                    yield T, q

            def ffn_hi(T, q, par_c):
                copy(hidh[:, par_c, q], hid[:]).then_inc(hid_hi, 1)

            for T, q in ffn_act(0, B_FFN, first=True):
                ffn_hi(T, q, 0)
            for T, q in ffn_act(1, B_FFN + 4):
                ffn_hi(T, q, 1)
            with act.Fori(1, FFN_T // 4) as i:
                for cc in range(2):
                    at = B_FFN - 2 + 12 * i + 6 * cc
                    for T, q in ffn_act(2 * i + cc, at):
                        act.wait_ge(w_used, at)
                        ffn_hi(T, q, cc)
            at = B_FFN - 2 + 6 * (FFN_T // 2 - 1)
            for T, q in ffn_act(FFN_T // 2 - 1, at):
                act.wait_ge(w_used, at)
                ffn_hi(T, q, 0)
            act.wait_ge(dn_ev, 2 + 8 * (FFN_T // 2))
            norm_squares(1, x_tiles)
            norm_std(1)
            norm_bring(1)
            act.wait_ge(x3_done, KT)
            act.dma_start(xs_d, x[:]).then_inc(spilled, 16)
            norm_squares(2, x_tiles)
            norm_std(2)
            norm_bring(2)
            split_hi(1, h_dst)

            def bring(n, panel, out, **kw):
                act.wait_ge(w_used, panel + 1)
                copy(out.rearrange("p (a n) -> p a n", a=2), ps[:, 2 * (n % 2):2 * (n % 2) + 2], **kw).then_inc(a_ev, 1)

            def bring_u(q):
                if q >= 2:
                    act.wait_ge(pool_lo, q - 1)
                bring(u_unit[q], u_panel[q], ub[q % 2][:, 8:8 + L])

            def pool_hi_copy(q):
                act.wait_ge(pool_d, q + 1)
                if q >= 2:
                    act.wait_ge(w_used, pw_panel[q // 2 - 1] + 1)
                copy(dh[:, q % 2], ub[2 + pool_out(q)][:, 8:8 + L]).then_inc(pool_hi, 1)

            def pool_store(g):
                for m in range(2):
                    if m == 0:
                        act.wait_ge(pw_mm, g + 1)
                    if g:
                        act.wait_ge(yp_out[m], 16 * g)
                    bring(pw_unit[g] + m, pw_panel[g] + m - 1, yp[:, m], scale=col("pool_scale", 2 * g + m))
                    act.wait_ge(a_ev, pw_unit[g] + m + 1)
                    act.dma_start(y_d[8 + 2 * g + m], yp[:, m]).then_inc(yp_out[m], 16)

            for n in range(4):
                bring(n, B_A1 + n, cqf[:, n])
            bring(4, B_A1 + 4, kt_t[:])
            act.wait_ge(spilled, 16)
            act.wait_ge(a_ev, 4)
            norm_squares(3, [cqf[:, k] for k in range(3)])
            act.wait_ge(kr_dve, 1)
            copy(ks_t[:ROPE], kt_t[ROPE:]).then_inc(kr_act, 1)
            act.wait_ge(kr_dve, 2)
            copy(krh[:ROPE], kt_t[:ROPE]).then_inc(kr_act, 1)
            act.wait_ge(zero_set, 5)
            bring_u(0)
            norm_std(3)
            bring_u(1)
            norm_bring(3)
            split_hi(2, lambda k: cqh[:, k])
            norm_squares(4, [cqf[:, 3]])
            pool_hi_copy(0)
            bring_u(2)
            norm_std(4)
            norm_bring(4)
            split_hi(3, lambda k: ckh[:, 0])
            pool_hi_copy(1)
            bring_u(3)
            pool_store(0)
            for g in (1, 2):
                pool_hi_copy(2 * g)
                bring_u(2 * g + 2)
                pool_hi_copy(2 * g + 1)
                bring_u(2 * g + 3)
                pool_store(g)
            pool_hi_copy(6)
            pool_hi_copy(7)
            pool_store(3)

            act.sem_inc(exp_done, 2)
            for s in o_out:
                act.sem_inc(s, 16)

            def project_act(h, b, m0):
                def hi(u, dst, panel=None):
                    if panel is None:
                        act.wait_ge(aux_mm, m0 + u + 1)
                    else:
                        act.wait_ge(w_used, panel)
                    copy(dst[:, b, (u % 2) * HALF:(u % 2 + 1) * HALF], ps[:, 6 + u % 2]).then_inc(ax_hi, 1)

                def shift(f):
                    act.wait_ge(aux_ev, proj_unit(h) + 3 + f)
                    copy(rs_t[:ROPE, f], rt[ROPE:, f]).then_inc(rope_shift, 1)

                def rot_hi(f):
                    act.wait_ge(rope_sum, 2 * h + f + 1)
                    copy(qrh[:ROPE, b, f * HALF:(f + 1) * HALF], rf_t[:ROPE, f]).then_inc(rope_hi, 1)

                hi(0, qnh)
                hi(1, qnh)
                shift(0)
                shift(1)
                hi(4, knh)
                rot_hi(0)
                hi(5, knh)
                rot_hi(1)
                hi(6, vvh)
                hi(7, vvh, B_A2 + 1 + h)

            def exp_row(h, t):
                act.wait_ge(row_bias, 8 * h + t + 1)
                act.wait_ge(tp_mm, 8 * h + t + 1)
                nc.scalar.activation(prob[:, t % 4].rearrange("p (a n) -> p a n", a=2),
                                     ps[:, 2 * (t % 2):2 * (t % 2) + 2], ACT.Exp, bias=stat[:, 28 + t % 4:29 + t % 4],
                                     scale=ATT_SCALE, accum_out=stat[:, 48 + t % 4:49 + t % 4]).then_inc(exp_done, 1)

            def turned_hi(h, t):
                j = t // 2
                act.wait_ge(tp_mm, 8 * h + t + 5)
                act.wait_ge(aux_mm, 11 * h + 6 + j)
                copy(pth[:, j % 2, :, (t % 2) * P:(t % 2 + 1) * P],
                     ps[:, 4:6].rearrange("p a (b n) -> p (a b) n", n=P)).then_inc(tp_hi, 1)

            def store_o(h, j, last_head):
                act.wait_ge(aux_ev, pv_unit(h, j, last_head) + 1)
                dst = y_d[h] if isinstance(h, int) else y_d[bass.ds(h, 1)].rearrange("a p n -> p (a n)")
                act.dma_start(dst[:, j * 256:(j + 1) * 256], osb[:, j % 2]).then_inc(o_out[j % 2], 16)

            def head_act(h, b, last_head=False):
                exp_row(h, 0)
                exp_row(h, 1)
                for t in range(2, 8):
                    exp_row(h, t)
                    turned_hi(h, t - 2)
                    if t in (5, 7):
                        store_o(h, (t - 5) // 2, last_head)
                if not last_head:
                    project_act(h + 1, 1 - b, 9 + 11 * h)
                turned_hi(h, 6)
                store_o(h, 2, last_head)
                turned_hi(h, 7)
                store_o(h, 3, last_head)

            for s in yp_out:
                act.wait_ge(s, 16 * POOL_G)
            project_act(0, 0, 0)
            with act.Fori(0, HEADS // 2 - 1) as i:
                head_act(2 * i, 0)
                head_act(2 * i + 1, 1)
            head_act(HEADS - 2, 0)
            act.wait_ge(w_used, B_A3)
            act.dma_start(x[:], xs_d).then_inc(x_in, 16)
            head_act(HEADS - 1, 1, last_head=True)

            for s in o_out:
                act.wait_ge(s, 16 + 16 * 2 * HEADS)
            for s in yp_out:
                act.wait_ge(s, 16 * POOL_G)
            norm_bring(5)
            split_hi(4, h_dst)

            def gate_act(c, b, base, Tb, used=None):
                if used is not None:
                    act.wait_ge(hid_done, Tb + 2 * c - 2)
                src = y_d[2 * c:2 * c + 2] if isinstance(c, int) else y_d[bass.ds(2 * c, 2)]
                act.dma_start(ybuf[:, b], src.rearrange("a p n -> p a n")).then_inc(y_in[b], 16)
                for q in range(2):
                    T = 2 * c + q
                    act.wait_ge(w_used, base + q + 1)
                    act.wait_ge(hid_done, Tb + T)
                    nc.scalar.activation(sg[:].rearrange("p (a n) -> p a n", a=2), ps[:, 2 * q:2 * q + 2],
                                         ACT.Silu).then_inc(silu_done, 1)
                    act.wait_ge(hid_done, Tb + T + 1)
                    if used is not None:
                        act.wait_ge(w_used, used)
                    copy(hidh[:, b, q], yg[:]).then_inc(hid_hi, 1)

            def mix_act(f, B):
                Tb = FFN_T + 16 * f
                gate_act(0, 0, B, Tb)
                gate_act(1, 1, B + 2, Tb)
                with act.Fori(1, N_MC // 2) as i:
                    for cc in range(2):
                        at = B - 2 + 8 * i + 4 * cc
                        gate_act(2 * i + cc, cc, at, Tb, used=at)
                act.wait_ge(dn_ev, 2 + 8 * (FFN_T // 2 + N_MC * (f + 1)))

            mix_act(0, B_A3)
            act.dma_start(posi[:], pos_d).then_inc(pos_in, 16)
            act.dma_start(xs_d, x[:]).then_inc(spilled, 16)
            norm_squares(5, x_tiles)
            norm_std(5)
            norm_bring(6)
            split_hi(5, h_dst)

            act.wait_ge(trig_step, 16)
            nc.scalar.activation(cos_r[:], ang[:], ACT.Sin).then_inc(trig_sin, 1)
            act.wait_ge(trig_step, 24)
            nc.scalar.activation(sin_r[:], ang[:], ACT.Sin).then_inc(trig_sin, 1)
            act.wait_ge(gam_step, 1)
            nc.scalar.activation(lgam[:, 8:16], lgam[:, 0:8], ACT.Exp, scale=-1.0).then_inc(gam_exp, 1)
            act.wait_ge(spilled, 32)

            def r_probs_hi(h, ib):
                for j in range(KT):
                    act.wait_ge(s_ev, 32 * h + 8 * ib + j + 1)
                    copy(rph[:, j], rsm[:, j % 2]).then_inc(p_hi, 1)

            act.wait_ge(trig_sin, 3)
            with act.Fori(0, R_HEADS) as h:
                base = B_R2 + 8 * h
                act.dma_start(mask[:], diff_d).then_inc(diff_in, 16)
                act.wait_ge(mask_step, 2 * h + 2)
                nc.scalar.activation(mask[:], mask[:], ACT.Exp).then_inc(mask_exp, 1)
                for u in range(4):
                    dst, f = (rqh, rkh)[u // 2], u % 2
                    for m in range(2):
                        act.wait_ge(r_sum, 8 * h + 2 * u + m + 1)
                        copy(dst[:, m, f * HALF:(f + 1) * HALF], rta[:, 2 * m]).then_inc(r_hi, 1)
                act.wait_ge(w_used, base + 8)
                act.wait_ge(r_lo, 8 * h + 8)
                for t in range(KT + 1):
                    if t < KT:
                        if t >= 2:
                            act.wait_ge(v_sum, 8 * h + t - 1)
                        copy(rta[:, t % 2], ps[:, t], accum_out=stat[:, 8 + t:9 + t]).then_inc(v_sum, 1)
                    if t:
                        act.wait_ge(v_mean, 8 * h + t)
                        nc.scalar.activation(vrh[:, t - 1], ps[:, t - 1], ACT.Identity,
                                             bias=stat[:, 31 + t:32 + t]).then_inc(v_hi, 1)
                r_probs_hi(h, 0)
                for ib in range(L // IB):
                    act.wait_ge(o_mm, 4 * h + ib + 1)
                    if ib:
                        act.wait_ge(r_out, 16 * (4 * h + ib))
                    for m in range(4):
                        copy(ro[:, m], ps[:, 4 + m, 0:IB]).then_inc(o_ev, 1)
                    for m in range(4):
                        n = 4 * ib + m
                        act.wait_ge(o_ev, 16 * h + n + 1)
                        if m >= 2:
                            act.wait_ge(o_acc, 16 * h + n - 1)
                        nc.scalar.activation(rsq[:, m % 2], ro[:, m], ACT.Square).then_inc(o_sq, 1)
                    if ib + 1 < L // IB:
                        r_probs_hi(h, ib + 1)
                    act.wait_ge(var_mm, 4 * h + ib + 1)
                    nc.scalar.activation(rstd[:], ps[:, 3, 0:IB], ACT.Sqrt, bias=stat[:, 60:61],
                                         scale=1.0 / R_DV).then_inc(var_std, 1)
                    act.wait_ge(o_normed, 16 * h + 4 * ib + 4)
                    act.dma_start(y_d[bass.ds(4 * h, 4)].rearrange("a p n -> p a n")[:, :, ib * IB:(ib + 1) * IB],
                                  ro[:]).then_inc(r_out, 16)
                act.wait_ge(s_ev, 32 * h + 32)
                act.wait_ge(r_out, 16 * (4 * h + 4))
            act.wait_ge(w_used, B_R3)
            act.wait_ge(o_mm, 4 * R_HEADS)
            act.dma_start(x[:], xs_d).then_inc(x_in, 16)
            mix_act(1, B_R3)
            norm_squares(6, x_tiles)
            norm_std(6)
            norm_bring(7)
            for k in range(KT):
                act.wait_ge(x3_done, KT + k + 1)
                act.dma_start(out_d[:, k], x[:, k]).then_inc(done, 16)

        @block.vector
        def _(dve):
            V = nc.vector

            spread = [0]

            def lo_of(out, value, hi):
                return V.tensor_tensor(out, value, hi.bitcast(F32), ALU.subtract)

            def norm_add(m):
                for k in range(NORM_T[m]):
                    dve.wait_ge(nm_sq, nb[m] + k + 1)
                    if k == 0:
                        V.tensor_copy(nacc[:], sqb[:, 0]).then_inc(nm_acc, 1)
                    else:
                        dve.wait_ge(nm_acc, nb[m] + k)
                        V.tensor_tensor(nacc[:], nacc[:], sqb[:, k % 2], ALU.add).then_inc(nm_acc, 1)

            def norm_invert(m):
                dve.wait_ge(nm_std, m + 1)
                V.reciprocal(rr[:, m], stat[:, 0:KT]).then_inc(nm_r, 1)
                dve.wait_ge(nm_r, m + 1)

            def norm_diag(m):
                if spread[0]:
                    dve.wait_ge(nm_dg, KT * spread[0])
                spread[0] += 1
                for t in range(KT):
                    V.tensor_scalar(diag[:, t], ident[:], rr[:, m, t:t + 1], None, ALU.mult).then_inc(nm_dg, 1)

            def split(q, src, scale, dst, shift=None):
                for k in range(SPLIT_T[q] + 1):
                    if k < SPLIT_T[q]:
                        if sb[q] + k >= 2:
                            dve.wait_ge(sp_lo, sb[q] + k - 1)
                        V.scalar_tensor_tensor(tt[:, k % 2], src(k), scale(k), rb[:], ALU.mult,
                                               ALU.mult).then_inc(sp_t, 1)
                    if k:
                        j = k - 1
                        dve.wait_ge(sp_hi, sb[q] + j + 1)
                        if shift is None:
                            lo_of(dst(j)[1], tt[:, j % 2], dst(j)[0]).then_inc(sp_lo, 1)
                        else:
                            V.scalar_tensor_tensor(dst(j)[1], tt[:, j % 2], shift(j), dst(j)[0].bitcast(F32),
                                                   ALU.add, ALU.subtract).then_inc(sp_lo, 1)

            h_dst = lambda k: (hh[:, k], hl[:, k])

            dve.sem_inc(fnet_ev, 2)
            dve.sem_inc(dn_ev, 2)
            V.memset(stat[:, 60:61], EPS).then_inc(zero_set, 1)
            V.memset(stat[:, 61:62], 0.0).then_inc(zero_set, 1)
            V.memset(stat[:, 62:63], 0.0).then_inc(zero_set, 1)
            V.memset(ones[:], 1.0).then_inc(ones_set, 1)
            dve.wait_ge(row_std, 1)
            V.reciprocal(rr[:, 7], stat[:, 16:24]).then_inc(row_inv, 1)
            dve.wait_ge(row_inv, 1)
            for t in range(KT):
                dve.wait_ge(xh_done, t + 1)
                V.scalar_tensor_tensor(hl[:, t], x[:, t], rr[:, 7, t:t + 1], hh[:, t].bitcast(F32), ALU.mult,
                                       ALU.subtract).then_inc(xl_done, 1)
            dve.wait_ge(c_ready, 1)
            with dve.Fori(0, N_DFT // 2) as i:
                for j in range(2):
                    dve.wait_ge(wm_in[j], 16 * i + 16)
                    out = macc[:, bass.ds((2 * i + j) * WMC, WMC)]
                    for k in range(KT):
                        w = wm[:, j, k * WMC:(k + 1) * WMC]
                        if k == 0:
                            V.tensor_scalar(out, w, silu_c[:, 0:1], None, ALU.mult).then_inc(mod_step, 1)
                        else:
                            dve.wait_ge(mod_step, (2 * i + j) * KT + k)
                            V.scalar_tensor_tensor(out, w, silu_c[:, k:k + 1], out, ALU.mult,
                                                   ALU.add).then_inc(mod_step, 1)
            dve.wait_ge(mod_mm, 1)
            V.tensor_tensor(modc[:], ps[:, 7, 0:48], col("b_mod", 0, 48), ALU.add).then_inc(mod_ready, 1)
            dve.wait_ge(mod_ready, 1)
            V.scalar_tensor_tensor(s1[:], modc[:, 8:16], 1.0, col("g_mix", 0, KT), ALU.add, ALU.mult).then_inc(mod_s, 1)
            V.scalar_tensor_tensor(s2[:], modc[:, 32:40], 1.0, col("g_ffn", 0, KT), ALU.add, ALU.mult).then_inc(mod_s, 1)
            V.tensor_scalar(sh2x[:], modc[:, 0:8], L / 512.0, None, ALU.mult).then_inc(mod_s, 1)
            dve.wait_ge(mod_s, 3)
            dve.wait_ge(pq_ev, 16)

            def pq_scale(f):
                for c in range(2):
                    V.tensor_scalar(pq[:, 2 * f + c], pq[:, 2 * f + c], s1[:, f:f + 1], None,
                                    ALU.mult).then_inc(pq_scaled, 1)
                dve.wait_ge(pq_scaled, 3 * f + 1)
                V.tensor_tensor(pq[:, 2 * f, 0:1], pq[:, 2 * f, 0:1], sh2x[:, f:f + 1], ALU.add).then_inc(pq_scaled, 1)

            def pq_low(f):
                dve.wait_ge(pq_hi, f + 1)
                lo_of(pql[:, f // 2 % 2, f % 2], pq[:, 2 * f:2 * f + 2].rearrange("p a n -> p (a n)"),
                      pqh[:, f // 2 % 2, f % 2]).then_inc(pq_lo, 1)

            def z_make(n):
                dve.wait_ge(v_copied, n + 1)
                if n >= 2:
                    dve.wait_ge(z_lo, n - 1)
                u, b = ps[:, 2 * (n % 3)], n % 2
                V.tensor_tensor(zt[:, b, 1:HALF], u[:, 1:HALF], vs[:, 1:HALF], ALU.subtract)
                V.tensor_tensor(zt[:, b, L - 1:HALF:-1], u[:, 1:HALF], vs[:, 1:HALF], ALU.add)
                V.tensor_copy(zt[:, b, 0:1], u[:, 0:1])
                V.tensor_copy(zt[:, b, HALF:HALF + 1], ps[:, 6 + n % 2, 0:1]).then_inc(z_ev, 1)

            def z_low(n):
                dve.wait_ge(z_hi, n + 1)
                lo_of(hl[:, n], zt[:, n % 2], hh[:, n]).then_inc(z_lo, 1)

            pq_scale(0)
            pq_scale(1)
            pq_low(0)
            pq_low(1)
            for g in range(4):
                if g < 3:
                    pq_scale(2 * g + 2)
                    pq_scale(2 * g + 3)
                    pq_low(2 * g + 2)
                    pq_low(2 * g + 3)
                for n in (2 * g, 2 * g + 1):
                    z_make(n)
                    if n:
                        z_low(n - 1)
            z_low(KT - 1)

            def angles(inv, turn, rad, s0):
                step = [s0]

                def then(ins):
                    ins.then_inc(trig_step, 1)
                    step[0] += 1
                    dve.wait_ge(trig_step, step[0])

                then(V.tensor_scalar(ang[:], posf[:], inv, None, ALU.mult))
                then(V.tensor_scalar(turns[:], ang[:], 1.0 / TWO_PI, turn, ALU.mult, ALU.add))
                then(V.tensor_scalar(turns[:], turns[:], ROUND, ROUND, ALU.add, ALU.subtract))
                then(V.scalar_tensor_tensor(ang[:], turns[:], -C1, ang[:], ALU.mult, ALU.add))
                then(V.scalar_tensor_tensor(ang[:], turns[:], -C2, ang[:], ALU.mult, ALU.add))
                then(V.scalar_tensor_tensor(ang[:], turns[:], -C3, ang[:], ALU.mult, ALU.add))
                then(V.tensor_scalar(ang[:], ang[:], rad, PI_IN, ALU.add, ALU.min))

            dve.wait_ge(pos_in, 16)
            V.tensor_copy(posf[:], posi[:]).then_inc(pos_float, 1)
            dve.wait_ge(pos_float, 1)
            angles(col("inv_a"), col("turn_a"), col("rad_a"), 0)
            V.tensor_scalar(ang[:], ang[:], -PI_IN, None, ALU.max).then_inc(trig_step, 1)

            dve.wait_ge(x_in, 16)
            with dve.Fori(0, KT // 2) as i:
                for j in range(2):
                    dve.wait_ge(w_used, B_FNET + 1 + 2 * i + j)
                    xm = x[:, bass.ds(2 * i + j, 1)].rearrange("p a (b n) -> p (a b) n", b=2)
                    V.scalar_tensor_tensor(xm, ps[:, 2 * j:2 * j + 2], modc[:, bass.ds(16 + 2 * i + j, 1)], xm,
                                           ALU.mult, ALU.add).then_inc(fnet_ev, 1)
            dve.wait_ge(ident_in, 16)
            norm_add(0)
            norm_invert(0)
            norm_diag(0)
            dve.wait_ge(nm_rbs, 1)
            split(0, lambda k: x[:, k], lambda k: s2[:, k:k + 1], h_dst, lambda k: modc[:, 24 + k:25 + k])

            V.memset(gbuf[:, 0:1], 0.0)
            V.memset(gbuf[:, L + 1:L + 2], 0.0).then_inc(zero_set, 1)

            def hidden(c, base, par_c, first=False):
                for q in range(2):
                    T = 2 * c + q
                    tap = lambda j: par[:, bass.ds(COL["conv"] + j * FFN_T + T, 1)]
                    dve.wait_ge(g_ev, T + 1)
                    V.tensor_scalar(conv[:], gbuf[:, 1:L + 1], tap(1), par[:, bass.ds(COL["b_conv"] + T, 1)],
                                    ALU.mult, ALU.add).then_inc(cv_step, 1)
                    dve.wait_ge(cv_step, 3 * T + 1)
                    V.scalar_tensor_tensor(conv[:], gbuf[:, 0:L], tap(0), conv[:], ALU.mult,
                                           ALU.add).then_inc(cv_step, 1)
                    dve.wait_ge(cv_step, 3 * T + 2)
                    V.scalar_tensor_tensor(conv[:], gbuf[:, 2:L + 2], tap(2), conv[:], ALU.mult,
                                           ALU.add).then_inc(cv_step, 1)
                    dve.wait_ge(silu_done, T + 1)
                    dve.wait_ge(w_used, base + 2 * q + 2)
                    if not (first and q == 0):
                        dve.wait_ge(hid_lo, T)
                    V.tensor_tensor(hid[:].rearrange("p (a n) -> p a n", a=2), ps[:, 2:4],
                                    act_g[:].rearrange("p (a n) -> p a n", a=2), ALU.mult).then_inc(hid_done, 1)
                    dve.wait_ge(hid_hi, T + 1)
                    dve.wait_ge(hid_done, T + 1)
                    lo_of(hidl[:, par_c, q], hid[:], hidh[:, par_c, q]).then_inc(hid_lo, 1)

            def add_down(c, base, mm_base, gate=None):
                for m in range(KT):
                    d, mm = m // 4, m % 4
                    if mm == 3:
                        dve.wait_ge(w_used, base + d + 1)
                    else:
                        dve.wait_ge(dn_mm, mm_base + 6 * c + 3 * d + mm + 1)
                    dve.wait_ge(dn_ev, dn_base + 8 * c + m + 2)
                    xm = x[:, m].rearrange("p (a n) -> p a n", a=2)
                    out = ps[:, 4 + 2 * (m % 2):6 + 2 * (m % 2)]
                    if gate is None:
                        V.tensor_tensor(xm, out, xm, ALU.add).then_inc(dn_ev, 1)
                    else:
                        V.scalar_tensor_tensor(xm, out, gate(m), xm, ALU.mult, ALU.add).then_inc(dn_ev, 1)

            dn_base = 0
            gt2 = lambda m: modc[:, 40 + m:41 + m]
            hidden(0, B_FFN, 0, first=True)
            with dve.Fori(0, FFN_T // 4) as i:
                for cc in range(2):
                    at = B_FFN + 4 + 12 * i + 6 * cc
                    hidden(2 * i + cc + 1, at, 1 - cc)
                    add_down(2 * i + cc, at + 4, 0, gt2)
            add_down(FFN_T // 2 - 1, B_A1 - 2, 0, gt2)
            norm_add(1)
            norm_invert(1)
            norm_diag(1)
            dve.wait_ge(nm_rbs, 2)
            for k in range(KT):
                V.scalar_tensor_tensor(x[:, k], x[:, k], col("g_final1", k), rb[:], ALU.mult,
                                       ALU.mult).then_inc(x3_done, 1)
            for i in range(2):
                V.memset(ub[i][:, 0:8], 0.0)
                last = V.memset(ub[i][:, 8 + L:PADW], 0.0)
            last.then_inc(zero_set, 1)
            norm_add(2)
            norm_invert(2)
            norm_diag(2)
            dve.wait_ge(nm_rbs, 3)
            dve.wait_ge(x3_done, KT)
            split(1, lambda k: x[:, k], lambda k: col("a_norm", k), h_dst)
            norm_add(3)
            dve.wait_ge(a_ev, 5)
            dve.wait_ge(trig_sin, 1)
            V.tensor_tensor(kt_t[:], kt_t[:], trig_a[:], ALU.mult).then_inc(kr_dve, 1)
            dve.wait_ge(kr_act, 1)
            dve.wait_ge(kr_dve, 1)
            V.tensor_tensor(kt_t[:ROPE], kt_t[:ROPE], ks_t[:ROPE], ALU.add).then_inc(kr_dve, 1)
            dve.wait_ge(kr_act, 2)
            dve.wait_ge(kr_dve, 2)
            lo_of(krl[:ROPE], kt_t[:ROPE], krh[:ROPE]).then_inc(kr_dve, 1)
            norm_invert(3)
            norm_diag(3)
            dve.wait_ge(nm_rbs, 4)
            dve.wait_ge(spilled, 16)
            split(2, lambda k: cqf[:, k], lambda k: col("q_norm", k), lambda k: (cqh[:, k], cql[:, k]))
            norm_add(4)
            pstep = [0]

            def pool_tile(q):
                g = q // 2
                w = pool_window(g)

                def then(ins):
                    ins.then_inc(pool_step, 1)
                    pstep[0] += 1
                    dve.wait_ge(pool_step, pstep[0])

                dve.wait_ge(a_ev, u_unit[q] + 1)
                if q:
                    dve.wait_ge(pool_lo, q)
                u = ub[q % 2]
                src, b = u, 0
                for left, right, lo, hi in pool_levels(g):
                    dst = ub[2 + b]
                    then(V.tensor_tensor(dst[:, 8 + lo:8 + hi], src[:, 8 + lo - left:8 + hi - left],
                                         src[:, 8 + lo + right:8 + hi + right], ALU.add))
                    src, b = dst, 1 - b
                d = ub[2 + b]
                then(V.scalar_tensor_tensor(d[:, 8:8 + L], src[:, 8:8 + L], 1.0 / w, u[:, 8:8 + L], ALU.mult,
                                            ALU.subtract))
                at, left, right = edge_cols(g)
                then(V.tensor_tensor(stat[:, 32:32 + left], src[:, 8:8 + left], par[:, at:at + left], ALU.mult))
                if right:
                    then(V.tensor_tensor(stat[:, 40:40 + right], src[:, 8 + L - right:8 + L],
                                         par[:, at + left:at + left + right], ALU.mult))
                    then(V.tensor_tensor(d[:, 8 + L - right:8 + L], stat[:, 40:40 + right],
                                         u[:, 8 + L - right:8 + L], ALU.subtract))
                V.tensor_tensor(d[:, 8:8 + left], stat[:, 32:32 + left], u[:, 8:8 + left],
                                ALU.subtract).then_inc(pool_d, 1)
                dve.wait_ge(pool_hi, q + 1)
                dve.wait_ge(pool_d, q + 1)
                lo_of(dl[:, q % 2], d[:, 8:8 + L], dh[:, q % 2]).then_inc(pool_lo, 1)

            pool_tile(0)
            norm_invert(4)
            norm_diag(4)
            dve.wait_ge(nm_rbs, 5)
            split(3, lambda k: cqf[:, 3], lambda k: col("kv_norm"), lambda k: (ckh[:, 0], ckl[:, 0]))
            for q in range(1, KT):
                pool_tile(q)

            dve.sem_inc(tp_lo, 1)

            def project_dve(h, b, m0):
                def low(u, hi_n, hi_t, lo_t):
                    dve.wait_ge(ax_hi, 6 * h + hi_n)
                    f = slice((u % 2) * HALF, (u % 2 + 1) * HALF)
                    lo_of(lo_t[:, b, f], ps[:, 6 + u % 2], hi_t[:, b, f]).then_inc(aux_ev, 1)

                low(0, 1, qnh, qnl)
                low(1, 2, qnh, qnl)
                for f in range(2):
                    dve.wait_ge(aux_mm, m0 + 3 + f)
                    if not (isinstance(h, int) and h == 0):
                        dve.wait_ge(rope_lo, 2 * h)
                    V.tensor_tensor(rt[:, f], ps[:, 6 + f], trig_a[:, f * HALF:(f + 1) * HALF],
                                    ALU.mult).then_inc(aux_ev, 1)
                for f in range(2):
                    dve.wait_ge(rope_shift, 2 * h + f + 1)
                    dve.wait_ge(aux_ev, proj_unit(h) + 3 + f)
                    V.tensor_tensor(rf_t[:ROPE, f], rt[:ROPE, f], rs_t[:ROPE, f], ALU.add).then_inc(rope_sum, 1)
                low(4, 3, knh, knl)
                low(5, 4, knh, knl)
                for f in range(2):
                    dve.wait_ge(rope_hi, 2 * h + f + 1)
                    dve.wait_ge(rope_sum, 2 * h + f + 1)
                    at = slice(f * HALF, (f + 1) * HALF)
                    lo_of(qrl[:ROPE, b, at], rf_t[:ROPE, f], qrh[:ROPE, b, at]).then_inc(rope_lo, 1)
                low(6, 5, vvh, vvl)
                low(7, 6, vvh, vvl)

            def row_maximum(h, t):
                dve.wait_ge(sc_mm, 8 * h + t + 1)
                m, n = stat[:, 24 + t % 4:25 + t % 4], stat[:, 28 + t % 4:29 + t % 4]
                V.tensor_reduce(m, ps[:, 2 * (t % 2):2 * (t % 2) + 2].rearrange("p a n -> p (a n)"), AX_X,
                                ALU.max).then_inc(row_max, 1)
                dve.wait_ge(row_max, 8 * h + t + 1)
                V.tensor_scalar(n, m, -ATT_SCALE, None, ALU.mult).then_inc(row_bias, 1)

            def normalise(h, t):
                dve.wait_ge(exp_done, 8 * h + t + 3)
                r = stat[:, 52 + t % 4:53 + t % 4]
                V.reciprocal(r, stat[:, 48 + t % 4:49 + t % 4]).then_inc(sum_inv, 1)
                dve.wait_ge(sum_inv, 8 * h + t + 1)
                V.tensor_scalar(prob[:, t % 4], prob[:, t % 4], r, None, ALU.mult).then_inc(prob_ok, 1)

            def turned_lo(h, t):
                j = t // 2
                dve.wait_ge(tp_hi, 8 * h + t + 1)
                at = slice((t % 2) * P, (t % 2 + 1) * P)
                lo_of(ptl[:, j % 2, :, at], ps[:, 4:6].rearrange("p a (b n) -> p (a b) n", n=P),
                      pth[:, j % 2, :, at]).then_inc(tp_lo, 1)

            def bring_o(h, j, last_head):
                dve.wait_ge(aux_mm, pv_count(h, j, last_head))
                dve.wait_ge(o_out[j % 2], 16 * (2 * h + j // 2 + 1))
                V.tensor_copy(osb[:, j % 2], ps[:, 6 + j % 2, 0:256]).then_inc(aux_ev, 1)

            def head_dve(h, b, last_head=False):
                row_maximum(h, 0)
                row_maximum(h, 1)
                normalise(h, 0)
                for t in range(2, 8):
                    row_maximum(h, t)
                    normalise(h, t - 1)
                    if t in (4, 6):
                        bring_o(h, t // 2 - 2, last_head)
                    turned_lo(h, t - 2)
                normalise(h, 7)
                if not last_head:
                    project_dve(h + 1, 1 - b, 9 + 11 * h)
                bring_o(h, 2, last_head)
                turned_lo(h, 6)
                turned_lo(h, 7)
                bring_o(h, 3, last_head)

            project_dve(0, 0, 0)
            with dve.Fori(0, HEADS // 2 - 1) as i:
                head_dve(2 * i, 0)
                head_dve(2 * i + 1, 1)
            head_dve(HEADS - 2, 0)
            head_dve(HEADS - 1, 1, last_head=True)

            dve.wait_ge(tp_mm, 4 + 8 * HEADS)
            norm_diag(2)
            dve.wait_ge(nm_rbs, 6)
            dve.wait_ge(x_in, 32)
            for s in o_out:
                dve.wait_ge(s, 16 + 16 * 2 * HEADS)
            dve.wait_ge(aux_mm, pv_count(HEADS - 1, 3, True))
            split(4, lambda k: x[:, k], lambda k: col("a_norm", k), h_dst)

            def gate_dve(c, b, base, Tb, y_count):
                dve.wait_ge(y_in[b], y_count)
                for q in range(2):
                    T = 2 * c + q
                    dve.wait_ge(silu_done, Tb + T + 1)
                    dve.wait_ge(hid_lo, Tb + T)
                    V.tensor_tensor(yg[:], sg[:], ybuf[:, b, q], ALU.mult).then_inc(hid_done, 1)
                    dve.wait_ge(hid_hi, Tb + T + 1)
                    dve.wait_ge(hid_done, Tb + T + 1)
                    lo_of(hidl[:, b, q], yg[:], hidh[:, b, q]).then_inc(hid_lo, 1)

            def mix_dve(f, B):
                nonlocal dn_base
                Tb, dn_base = FFN_T + 16 * f, 8 * (FFN_T // 2 + N_MC * f)
                mb, y0 = 6 * (FFN_T // 2 + N_MC * f), 16 * (N_MC // 2) * f
                gate_dve(0, 0, B, Tb, y0 + 16)
                with dve.Fori(0, N_MC // 2 - 1) as i:
                    gate_dve(2 * i + 1, 1, B, Tb, y0 + 16 * i + 16)
                    add_down(2 * i, B + 4 + 8 * i, mb)
                    gate_dve(2 * i + 2, 0, B, Tb, y0 + 16 * i + 32)
                    add_down(2 * i + 1, B + 8 + 8 * i, mb)
                gate_dve(N_MC - 1, 1, B, Tb, y0 + 16 * (N_MC // 2))
                add_down(N_MC - 2, B + 4 * N_MC - 4, mb)
                add_down(N_MC - 1, B + 4 * N_MC - 2, mb)

            mix_dve(0, B_A3)
            dve.wait_ge(pos_in, 32)
            V.tensor_copy(posf[:], posi[:]).then_inc(pos_float, 1)
            dve.wait_ge(pos_float, 2)
            norm_add(5)
            norm_invert(5)
            norm_diag(5)
            dve.wait_ge(nm_rbs, 7)
            dve.wait_ge(dn_ev, 2 + 8 * (FFN_T // 2 + N_MC))
            split(5, lambda k: x[:, k], lambda k: col("r_norm", k), h_dst)

            angles(col("inv_r"), 0.25, float(np.pi / 2), 8)
            V.tensor_scalar(ang[:], ang[:], -PI_IN, None, ALU.max).then_inc(trig_step, 1)
            dve.wait_ge(trig_sin, 2)
            dve.wait_ge(trig_step, 16)
            angles(col("inv_r"), 0.0, 0.0, 16)
            V.tensor_scalar(ang[:], ang[:], -PI_IN, None, ALU.max).then_inc(trig_step, 1)

            g_abs, g_e, g_z, g_z2, g_p = [lgam[:, 8 * i:8 * i + 8] for i in range(5)]
            gstep = [0]

            def then(ins):
                ins.then_inc(gam_step, 1)
                gstep[0] += 1
                dve.wait_ge(gam_step, gstep[0])

            dec = col("decay", 0, 8)
            then(V.scalar_tensor_tensor(g_abs, dec, -1.0, dec, ALU.mult, ALU.max))
            dve.wait_ge(gam_exp, 1)
            then(V.tensor_scalar(g_p, g_e, 2.0, None, ALU.add))
            then(V.reciprocal(g_z, g_p))
            then(V.tensor_tensor(g_z, g_z, g_e, ALU.mult))
            then(V.tensor_tensor(g_z2, g_z, g_z, ALU.mult))
            then(V.tensor_scalar(g_p, g_z2, 1.0 / 19, None, ALU.mult))
            for n in range(17, 1, -2):
                then(V.scalar_tensor_tensor(g_p, g_p, 1.0 / n, g_z2, ALU.add, ALU.mult))
            then(V.scalar_tensor_tensor(g_p, g_p, 1.0, g_z, ALU.add, ALU.mult))
            then(V.tensor_scalar(g_abs, dec, 0.0, None, ALU.min))
            then(V.scalar_tensor_tensor(g_abs, g_p, -2.0, g_abs, ALU.mult, ALU.add))
            then(V.tensor_scalar(g_e, g_abs, -1.0, None, ALU.mult))
            dve.wait_ge(spilled, 32)
            dve.wait_ge(trig_sin, 3)

            def r_block(h, ib):
                for j in range(KT + 1):
                    n = 32 * h + 8 * ib + j
                    if j < KT:
                        s = ib * KT + j
                        dve.wait_ge(s_mm, n + 1)
                        if s >= 2:
                            dve.wait_ge(p_lo, n - 1)
                        at = ib * IB - j * P + L - P
                        V.scalar_tensor_tensor(rsm[:, j % 2], ps[:, s % 3, 0:IB], R_DK ** -0.5,
                                               mask[:, at:at + IB], ALU.mult, ALU.mult).then_inc(s_ev, 1)
                    if j:
                        dve.wait_ge(p_hi, n)
                        dve.wait_ge(s_ev, n)
                        lo_of(rpl[:, j - 1], rsm[:, (j - 1) % 2], rph[:, j - 1]).then_inc(p_lo, 1)

            with dve.Fori(0, R_HEADS) as h:
                base = B_R2 + 8 * h
                dve.wait_ge(diff_in, 16 * h + 16)
                V.tensor_scalar(mtmp[:], mask[:], lgam[:, bass.ds(h + 12, 1)], None, ALU.mult).then_inc(mask_step, 1)
                dve.wait_ge(mask_step, 2 * h + 1)
                V.scalar_tensor_tensor(mask[:], mask[:], lgam[:, bass.ds(h, 1)], mtmp[:], ALU.mult,
                                       ALU.min).then_inc(mask_step, 1)
                dve.wait_ge(mask_step, 2 * h + 2)
                for u in range(4):
                    hi_t, lo_t = ((rqh, rql), (rkh, rkl))[u // 2]
                    b0, f = 4 * (u // 2), u % 2
                    dve.wait_ge(w_used, base + 2 * (u // 2) + 2)
                    if u:
                        dve.wait_ge(r_lo, 8 * h + 2 * u)
                    tok = slice(f * HALF, (f + 1) * HALF)
                    x1, x2 = ps[:, b0 + f], ps[:, b0 + 2 + f]
                    V.tensor_tensor(rta[:, 0], x1, cos_r[:, tok], ALU.mult)
                    V.tensor_tensor(rta[:, 1], x2, sin_r[:, tok], ALU.mult)
                    V.tensor_tensor(rta[:, 2], x2, cos_r[:, tok], ALU.mult)
                    V.tensor_tensor(rta[:, 3], x1, sin_r[:, tok], ALU.mult).then_inc(r_ev, 1)
                    dve.wait_ge(r_ev, 4 * h + u + 1)
                    V.tensor_tensor(rta[:, 0], rta[:, 0], rta[:, 1], ALU.subtract).then_inc(r_sum, 1)
                    V.tensor_tensor(rta[:, 2], rta[:, 2], rta[:, 3], ALU.add).then_inc(r_sum, 1)
                    for m in range(2):
                        dve.wait_ge(r_hi, 8 * h + 2 * u + m + 1)
                        dve.wait_ge(r_sum, 8 * h + 2 * u + m + 1)
                        lo_of(lo_t[:, m, tok], rta[:, 2 * m], hi_t[:, m, tok]).then_inc(r_lo, 1)
                for t in range(KT + 1):
                    if t < KT:
                        dve.wait_ge(v_sum, 8 * h + t + 1)
                        V.tensor_scalar(stat[:, 32 + t:33 + t], stat[:, 8 + t:9 + t], -1.0 / R_DV, None,
                                        ALU.mult).then_inc(v_mean, 1)
                    if t:
                        dve.wait_ge(v_hi, 8 * h + t)
                        dve.wait_ge(v_mean, 8 * h + t)
                        V.scalar_tensor_tensor(vrl[:, t - 1], ps[:, t - 1], stat[:, 31 + t:32 + t],
                                               vrh[:, t - 1].bitcast(F32), ALU.add, ALU.subtract).then_inc(v_lo, 1)
                dve.wait_ge(mask_exp, h + 1)
                r_block(h, 0)
                for ib in range(L // IB):
                    for m in range(4):
                        n = 16 * h + 4 * ib + m
                        dve.wait_ge(o_sq, n + 1)
                        if m == 0:
                            V.tensor_copy(roa[:], rsq[:, 0]).then_inc(o_acc, 1)
                        else:
                            dve.wait_ge(o_acc, n)
                            V.tensor_tensor(roa[:], roa[:], rsq[:, m % 2], ALU.add).then_inc(o_acc, 1)
                    if ib + 1 < L // IB:
                        r_block(h, ib + 1)
                    dve.wait_ge(var_std, 4 * h + ib + 1)
                    V.reciprocal(rinv[:], rstd[:]).then_inc(var_inv, 1)
                    dve.wait_ge(var_inv, 4 * h + ib + 1)
                    for m in range(4):
                        V.scalar_tensor_tensor(ro[:, m], ro[:, m], par[:, bass.ds(COL["gn"] + m + 4 * h, 1)], rinv[:],
                                               ALU.mult, ALU.mult).then_inc(o_normed, 1)
            dve.wait_ge(x_in, 48)
            mix_dve(1, B_R3)
            norm_add(6)
            norm_invert(6)
            norm_diag(6)
            dve.wait_ge(nm_rbs, 8)
            dve.wait_ge(dn_ev, 2 + 8 * (FFN_T // 2 + 2 * N_MC))
            for k in range(KT):
                V.scalar_tensor_tensor(x[:, k], x[:, k], col("final", k), rb[:], ALU.mult,
                                       ALU.mult).then_inc(x3_done, 1)


def host_panels(a):
    pan = np.zeros((N_PANELS, P, D), np.float32)
    at = [0]

    def put(*parts):
        pan[at[0]] = np.concatenate(parts, axis=1)
        at[0] += 1

    def cols(w, c0, k0=0, kn=KT, width=P):
        return np.concatenate([w[(k0 + k) * P:(k0 + k + 1) * P, c0:c0 + width] for k in range(kn)], axis=1)

    def down(w, c):
        for d in range(2):
            put(*[cols(w, (4 * d + m) * P, 2 * c, 2) for m in range(4)])

    n = np.arange(L)
    turn = np.outer(n, np.arange(HALF)) % L
    cos = (np.cos(2 * np.pi * turn / L) / 512).astype(np.float32)
    sin = (np.sin(2 * np.pi * turn / L) / 512).astype(np.float32)
    sin[:, 0] = np.where(n % 2 == 0, 1.0, -1.0) / 512
    for _ in range(2):
        for t in range(KT):
            put(cos[t * P:(t + 1) * P], sin[t * P:(t + 1) * P])
    m = np.arange(FNET_C)
    turn = np.outer(m, m) % FNET_C
    cc = np.cos(2 * np.pi * turn / FNET_C).astype(np.float32)
    ss = np.sin(2 * np.pi * turn / FNET_C).astype(np.float32)
    put(*[cols(w, q * P, 0, 2) for w in (cc, ss) for q in range(2)])
    w = a["w_fnet_out"][0]
    for q in range(KT):
        put(cols(w, q * P))
    assert at[0] == B_FFN
    w, wd = a["w_ffn_up"][0], a["w_ffn_down"][0]

    def up(c):
        for q in range(2):
            put(cols(w, (2 * c + q) * P))
            put(cols(w, FFN + (2 * c + q) * P))

    up(0)
    for c in range(FFN_T // 2 - 1):
        up(c + 1)
        down(wd, c)
    down(wd, FFN_T // 2 - 1)
    assert at[0] == B_A1
    w = a["a_w_in_2"][0]
    o_kv, o_kr = Q_LORA, Q_LORA + KV_LORA
    o_u = o_kr + ROPE
    o_g = o_u + POOL_G * POOL_C
    for q in range(3):
        put(cols(w, q * P))
    put(cols(w, o_kv))
    kr = w[:, o_kr:o_kr + ROPE]
    put(cols(np.concatenate([kr, kr[:, 32:], kr[:, :32]], axis=1), 0))
    pw = a["a_pool_w_2"][0]

    def put_pool(g):
        put(cols(pw[g], 0, 0, 2), cols(pw[g], P, 0, 2), np.zeros((P, HALF), np.float32))

    for q in range(KT):
        put(cols(w, o_u + q * P))
        if q in (3, 5):
            put_pool((q - 3) // 2)
    put_pool(2)
    put_pool(3)
    assert at[0] == B_A2
    wq, wkv = a["a_w_uq_2"][0], a["a_w_ukv_2"][0]
    for h in range(HEADS):
        q = wq[:, h * 192:(h + 1) * 192]
        r = q[:, NOPE:]
        put(cols(q, 0, 0, 3), cols(np.concatenate([r, r[:, 32:], r[:, :32]], axis=1), 0, 0, 3),
            wkv[:, h * 256:(h + 1) * 256])
    assert at[0] == B_A3

    def mix(w_gate, w_out):
        def gate(c):
            for q in range(2):
                put(cols(w_gate, (2 * c + q) * P))

        gate(0)
        for c in range(MIX // P // 2 - 1):
            gate(c + 1)
            down(w_out, c)
        down(w_out, MIX // P // 2 - 1)

    mix(w[:, o_g:], a["a_w_out_2"][0])
    assert at[0] == B_R2
    w = a["r_w_in_2"][0]
    for h in range(R_HEADS):
        for o in (0, R_HEADS * R_DK):
            for q in range(2):
                put(cols(w, o + h * R_DK + q * P))
        v = w[:, 2 * R_HEADS * R_DK + h * R_DV:2 * R_HEADS * R_DK + (h + 1) * R_DV]
        for k in range(0, KT, 2):
            put(v[k * P:(k + 1) * P], v[(k + 1) * P:(k + 2) * P])
    assert at[0] == B_R3
    mix(w[:, 2 * R_HEADS * R_DK + R_HEADS * R_DV:], a["r_w_out_2"][0])
    assert at[0] == N_PANELS
    return pan


def host_params(a):
    t = np.zeros((P, N_COL), np.float32)

    def put(name, v, i=0):
        v = np.asarray(v, np.float32).reshape(-1, P).T
        t[:, COL[name] + i:COL[name] + i + v.shape[1]] = v

    put("c", a["c"][0])
    put("b_mod", a["b_mod"][0])
    put("g_mix", a["g_norm_mix"][0])
    put("g_ffn", a["g_norm_ffn"][0])
    put("conv", a["w_ffn_conv"][0].reshape(-1))
    put("b_conv", a["b_ffn_conv"][0])
    put("g_final1", a["g_final"])
    put("a_norm", a["a_norm_g_2"][0])
    put("q_norm", a["a_q_norm_g_2"][0])
    put("kv_norm", a["a_kv_norm_g_2"][0])
    put("pool_scale", a["a_pool_scale_2"][0])
    put("r_norm", a["r_norm_g_2"][0])
    put("gn", a["r_gn_g_2"][0])
    put("final", a["final_norm_g_2"])
    t[:, COL["decay"]:COL["decay"] + 4] = a["r_decay_fwd_2"]
    t[:, COL["decay"] + 4:COL["decay"] + 8] = a["r_decay_bwd_2"]
    f32 = np.float32
    inv_a = f32(1.0) / (10000.0 ** (np.arange(0, ROPE, 2) / ROPE)).astype(f32)
    inv_r = f32(1.0) / (10000.0 ** (np.arange(0, R_DK, 2) / R_DK)).astype(f32)
    t[:, COL["inv_a"]] = np.concatenate([inv_a, inv_a, -inv_a, inv_a])
    t[:64, COL["turn_a"]] = 0.25
    t[:64, COL["rad_a"]] = np.pi / 2
    t[:, COL["inv_r"]] = inv_r
    for g in range(POOL_G):
        at, left, right = edge_cols(g)
        n = np.concatenate([np.arange(left) + left, left * 2 - 1 - np.arange(right)])
        t[:, at:at + left + right] = (1.0 / n).astype(f32)
    return t


def kernel(**inputs):
    import concourse.bacc as bacc
    from concourse.bass_utils import run_bass_kernel_spmd

    a = {k: np.asarray(v) for k, v in inputs.items()}
    xm = a["x"][0]
    wm = a["w_mod"][0].reshape(KT, P, 16, 384).transpose(2, 1, 0, 3).reshape(16, P, KT * 384)
    arrays = {
        "xt": np.ascontiguousarray(xm.reshape(KT, P, D).transpose(1, 0, 2)),
        "xf": np.ascontiguousarray(xm.T.reshape(KT, P, L).transpose(1, 0, 2)),
        "panels": host_panels(a),
        "w_mod_chunks": np.ascontiguousarray(wm),
        "params": host_params(a),
        "positions": np.ascontiguousarray(np.broadcast_to(a["positions_2"].reshape(1, L), (P, L))),
        "ident_c": np.eye(P, dtype=np.float32),
        "diff_c": (np.arange(MASK_W)[None, :] - (L - P) - np.arange(P)[:, None]).astype(np.float32),
    }
    nc = bacc.Bacc("TRN2", target_bir_lowering=False, num_devices=1)
    args = [nc.dram_tensor(k, v.shape, mybir.dt.from_np(v.dtype), kind="ExternalInput").ap() for k, v in arrays.items()]
    out = nc.dram_tensor("out", (P, KT, L), F32, kind="ExternalOutput").ap()
    build(nc, *args, out)
    r = run_bass_kernel_spmd(nc, [arrays], core_ids=[0])
    y = r.results[0]["out"]
    return np.ascontiguousarray(y.transpose(1, 0, 2).reshape(D, L).T).reshape(1, L, D)
```

```python
from contextlib import ExitStack

import numpy as np

import concourse.bass as bass
from concourse import mybir

F32 = mybir.dt.float32
F32R = mybir.dt.float32r
I32 = mybir.dt.int32
ALU = mybir.AluOpType
ACT = mybir.ActivationFunctionType
AX_X = mybir.AxisListType.X

P = 128
D = 1024
L = 1024
KT = D // P
HALF = 512
EPS = 1e-6

FNET_G, FNET_C = 4, 256
FFN = 2816
FFN_T = FFN // P
Q_LORA, KV_LORA = 384, 128
HEADS, NOPE, ROPE, VDIM = 8, 128, 64, 128
ATT_SCALE = float((NOPE + ROPE) ** -0.5)
POOL_G, POOL_C = 4, 256
MIX = 2048
R_HEADS, R_DK, R_DV = 4, 256, 512
IB = 256
R_BLOCKS = L // IB
R_AHEAD = KT - 2
MASK_W = 2 * L - P

N_DFT, N_CDFT, N_FNET = 16, 1, KT
N_FFN = FFN_T // 2 * 6
N_A1 = 5 + KT + POOL_G
N_A2 = HEADS
N_MIX = MIX // P * 2
N_R2 = R_HEADS * 8
COUNTS = [N_DFT, N_CDFT, N_FNET, N_FFN, N_A1, N_A2, N_MIX, N_R2, N_MIX]
B_DFT, B_CDFT, B_FNET, B_FFN, B_A1, B_A2, B_A3, B_R2, B_R3, N_PANELS = [sum(COUNTS[:i]) for i in range(10)]

_COLS = [("c", KT), ("b_mod", 48), ("g_mix", KT), ("g_ffn", KT), ("conv", 3 * FFN_T), ("b_conv", FFN_T),
         ("g_final1", KT), ("a_norm", KT), ("q_norm", 3), ("kv_norm", 1), ("pool_scale", KT),
         ("r_norm", KT), ("gn", 16), ("final", KT), ("decay", 8),
         ("inv_a", 1), ("turn_a", 1), ("rad_a", 1), ("inv_r", 1), ("edge", 26)]
COL = {}
N_COL = 0
for _name, _n in _COLS:
    COL[_name] = N_COL
    N_COL += _n

TWO_PI = 2.0 * np.pi
C1 = 6.28125
C2 = float(np.float32(np.round((TWO_PI - C1) * 2.0 ** 21) / 2.0 ** 21))
C3 = float(np.float32(TWO_PI - C1 - C2))
ROUND = 1.5 * 2.0 ** 23
PI_IN = float(np.nextafter(np.float32(np.pi), np.float32(0)))

NORM_T = [KT, KT, KT, 3, 1, KT, KT]
NORM_N = [D, D, D, Q_LORA, KV_LORA, D, D]
SPLIT_T = [KT, KT, 3, 1, KT, KT]


def pool_window(g):
    return 2 << g


def pool_levels(g):
    out, lo, hi = [], 0, L
    for lv in range(g, -1, -1):
        a, b = (1, 0) if lv == 0 else (1 << (lv - 1), 1 << (lv - 1))
        out.append((a, b, lo, hi))
        lo, hi = lo - a, hi + b
    return out[::-1]


def edge_cols(g):
    at = COL["edge"] + sum(pool_window(q) - 1 for q in range(g))
    w = pool_window(g)
    return at, w // 2, w // 2 - 1


def pool_out(q):
    return (q // 2 + 1) % 2


def build(nc, xt_d, x_d, pan_d, wm_d, par_d, pos_d, ident_d, diff_d, out_d):
    ctx = ExitStack()
    with ctx:
        def place(name, shape, dt, at):
            with ExitStack() as s:
                if at:
                    s.enter_context(nc.sbuf_tensor(f"under_{name}", [P, at // 4], F32))
                return s.enter_context(nc.sbuf_tensor(name, shape, dt))

        def sem(name):
            return ctx.enter_context(nc.semaphore(name))

        K = 1024
        stage = place("stage", [P, 2, D], F32, 0)
        wh = place("wh", [P, 2, D], F32R, 8 * K)
        wl = place("wl", [P, 2, D], F32R, 16 * K)
        x = place("x", [P, KT, L], F32, 24 * K)
        hh = place("hh", [P, KT, L], F32R, 56 * K)
        hl = place("hl", [P, KT, L], F32R, 88 * K)
        par = place("par", [P, N_COL], F32, 120 * K)
        modc = place("modc", [P, 48], F32, 120 * K + 1200)
        s1 = place("s1", [P, KT], F32, 120 * K + 1392)
        s2 = place("s2", [P, KT], F32, 120 * K + 1424)
        sh2x = place("sh2x", [P, KT], F32, 120 * K + 1456)
        silu_c = place("silu_c", [P, KT], F32, 120 * K + 1488)
        rr = place("rr", [P, 8, KT], F32, 120 * K + 1520)
        stat = place("stat", [P, 64], F32, 120 * K + 1776)
        lgam = place("lgam", [P, 40], F32, 120 * K + 2032)
        nothing = place("nothing", [P, 1], F32, 120 * K + 3232)
        ga = place("ga", [P, KT], F32, 120 * K + 3264)
        ident = place("ident", [P, P], F32, 120 * K + 2192)
        ones = place("ones", [P, P], F32, 120 * K + 2704)
        rb = place("rb", [P, L], F32, 124 * K)
        trig_a = place("trig_a", [P, L], F32, 128 * K)
        sqb = place("sqb", [P, 2, L], F32, 132 * K)
        nacc = place("nacc", [P, L], F32, 140 * K)
        diag = place("diag", [P, KT, P], F32, 144 * K)
        sqb0 = place("sqb0", [P, 2, L], F32, 188 * K)
        nacc0 = place("nacc0", [P, L], F32, 196 * K)
        sqb2 = place("sqb2", [P, 2, L], F32, 148 * K)
        nacc2 = place("nacc2", [P, L], F32, 156 * K)
        rb2 = place("rb2", [P, L], F32, 160 * K)
        tt = place("tt", [P, 2, L], F32, 148 * K)
        WMC = 384
        wm = place("wm", [P, 2, KT * WMC], F32, 124 * K)
        macc = place("macc", [P, 3 * D], F32, 148 * K)
        wm_b = place("wm_b", [P, 2, KT * WMC], F32, 132 * K)
        macc_b = place("macc_b", [P, 3 * D], F32, 156 * K)
        pq = place("pq", [P, 16, HALF], F32, 172 * K)
        pqh = place("pqh", [P, 2, 2, D], F32R, 124 * K)
        pql = place("pql", [P, 2, 2, D], F32R, 140 * K)
        zt = place("zt", [P, 2, L], F32, 156 * K)
        vs = place("vs", [P, HALF], F32, 164 * K)
        posi = place("posi", [P, L], I32, 172 * K)
        posf = place("posf", [P, L], F32, 176 * K)
        ang = place("ang", [P, L], F32, 180 * K)
        turns = place("turns", [P, L], F32, 203 * K + 512)
        hidh = place("hidh", [P, 2, 2, L], F32R, 164 * K)
        hidl = place("hidl", [P, 2, 2, L], F32R, 180 * K)
        gbuf = place("gbuf", [P, L + 2], F32, 132 * K)
        conv = place("conv", [P, L], F32, 137 * K)
        act_g = place("act_g", [P, L], F32, 141 * K)
        hid = place("hid", [P, L], F32, 145 * K)
        cqh = place("cqh", [P, 3, L], F32R, 24 * K)
        cql = place("cql", [P, 3, L], F32R, 36 * K)
        ckh = place("ckh", [P, 1, L], F32R, 48 * K)
        ckl = place("ckl", [P, 1, L], F32R, 52 * K)
        krh = place("krh", [P, L], F32R, 156 * K)
        krl = place("krl", [P, L], F32R, 160 * K)
        cqf = place("cqf", [P, 4, L], F32, 164 * K)
        dh = place("dh", [P, 2, L], F32R, 164 * K)
        dl = place("dl", [P, 2, L], F32R, 172 * K)
        PADW = L + 16
        ub = [place(f"ub{i}", [P, PADW], F32, 180 * K + i * 4160) for i in range(4)]
        kt_t = place("kt_t", [P, L], F32, 180 * K + 4 * 4160)
        ks_t = place("ks_t", [P, L], F32, 180 * K + 4 * 4160 + 4096)
        yp = place("yp", [P, 2, L], F32, 180 * K + 4 * 4160)
        qnh = place("qnh", [P, 2, L], F32R, 56 * K)
        qnl = place("qnl", [P, 2, L], F32R, 64 * K)
        qrh = place("qrh", [P, 2, L], F32R, 72 * K)
        qrl = place("qrl", [P, 2, L], F32R, 80 * K)
        knh = place("knh", [P, 2, L], F32R, 88 * K)
        knl = place("knl", [P, 2, L], F32R, 96 * K)
        vvh = place("vvh", [P, 2, L], F32R, 104 * K)
        vvl = place("vvl", [P, 2, L], F32R, 112 * K)
        prob = place("prob", [P, 4, L], F32, 132 * K)
        osb = place("osb", [P, 2, 256], F32, 148 * K)
        rt = place("rt", [P, 2, HALF], F32, 150 * K)
        pth = place("pth", [P, 2, KT, 256], F32R, 164 * K)
        ptl = place("ptl", [P, 2, KT, 256], F32R, 180 * K)
        rs_t = place("rs_t", [P, 2, HALF], F32, 196 * K)
        rf_t = place("rf_t", [P, 2, HALF], F32, 200 * K)
        ybuf = place("ybuf", [P, 2, 2, L], F32, 132 * K)
        sg = place("sg", [P, L], F32, 196 * K)
        yg = place("yg", [P, L], F32, 200 * K)
        vrh = place("vrh", [P, KT, R_DV], F32R, 24 * K)
        vrl = place("vrl", [P, KT, R_DV], F32R, 40 * K)
        rqh = place("rqh", [P, 2, L], F32R, 132 * K)
        rql = place("rql", [P, 2, L], F32R, 140 * K)
        rkh = place("rkh", [P, 2, L], F32R, 148 * K)
        rkl = place("rkl", [P, 2, L], F32R, 156 * K)
        rph = place("rph", [P, KT, IB], F32R, 164 * K)
        rpl = place("rpl", [P, KT, IB], F32R, 172 * K)
        cos_r = place("cos_r", [P, L], F32, 187 * K + 512)
        sin_r = place("sin_r", [P, L], F32, 191 * K + 512)
        mask = place("mask", [P, MASK_W], F32, 180 * K)
        rta = place("rta", [P, 4, HALF], F32, 195 * K + 512)
        mtmp = place("mtmp", [P, MASK_W], F32, 195 * K + 512)
        rsm = place("rsm", [P, 2, IB], F32, 124 * K)
        roa = place("roa", [P, IB], F32, 126 * K)
        rinv = place("rinv", [P, IB], F32, 127 * K)
        rsq = place("rsq", [P, 2, IB], F32, 128 * K)
        rstd = place("rstd", [P, IB], F32, 130 * K)
        ro = place("ro", [P, 4, IB], F32, 203 * K + 512)

        ps = ctx.enter_context(nc.psum_tensor("ps", [P, 8, HALF], F32))
        xs_d = nc.dram_tensor("x_spill", (P, KT, L), F32).ap()
        y_d = nc.dram_tensor("y_spill", (16, P, L), F32).ap()

        panel_in = [sem("panel_in0"), sem("panel_in1")]
        nothing_set, w_hi, w_ready, w_used = sem("nothing_set"), sem("w_hi"), sem("w_ready"), sem("w_used")
        wm_in = [sem("wm_in0"), sem("wm_in1")]
        xt_in = [sem(f"xt_in{i}") for i in range(4)]
        par_in, ident_in, x_in, pos_in = sem("par_in"), sem("ident_in"), sem("x_in"), sem("pos_in")
        ones_set, zero_set, c_ready = sem("ones_set"), sem("zero_set"), sem("c_ready")
        row_ss, row_std, row_inv, xh_done, xl_done = [sem(n) for n in ("row_ss", "row_std", "row_inv", "xh_done", "xl_done")]
        mod_step, pq_ev, mod_mm, mod_ready, mod_s = [sem(n) for n in ("mod_step", "pq_ev", "mod_mm", "mod_ready", "mod_s")]
        ga_set = sem("ga_set")
        pq_scaled, pq_hi, pq_lo, c_mm, v_copied, z_ev, z_hi, z_lo = [
            sem(n) for n in ("pq_scaled", "pq_hi", "pq_lo", "c_mm", "v_copied", "z_ev", "z_hi", "z_lo")]
        pos_float, trig_step, trig_sin = sem("pos_float"), sem("trig_step"), sem("trig_sin")
        fnet_ev = sem("fnet_ev")
        nm_sq, nm_acc, nm_ss, nm_std, nm_r, nm_dg, nm_rb, nm_rbs = [
            sem(n) for n in ("nm_sq", "nm_acc", "nm_ss", "nm_std", "nm_r", "nm_dg", "nm_rb", "nm_rbs")]
        sp_t, sp_hi, sp_lo = sem("sp_t"), sem("sp_hi"), sem("sp_lo")
        g_ev, cv_step, silu_done, hid_done, hid_hi, hid_lo, dn_mm, dn_ev = [
            sem(n) for n in ("g_ev", "cv_step", "silu_done", "hid_done", "hid_hi", "hid_lo", "dn_mm", "dn_ev")]
        x3_done, spilled = sem("x3_done"), sem("spilled")
        a_ev, pw_mm, kr_dve, kr_act, pool_step, pool_d, pool_hi, pool_lo = [
            sem(n) for n in ("a_ev", "pw_mm", "kr_dve", "kr_act", "pool_step", "pool_d", "pool_hi", "pool_lo")]
        yp_out = [sem("yp_out0"), sem("yp_out1")]
        aux_mm, aux_ev, ax_hi, rope_shift, rope_sum, rope_hi, rope_lo = [
            sem(n) for n in ("aux_mm", "aux_ev", "ax_hi", "rope_shift", "rope_sum", "rope_hi", "rope_lo")]
        sc_mm, row_max, row_bias, exp_done, sum_inv, prob_ok, tp_mm, tp_hi, tp_lo = [
            sem(n) for n in ("sc_mm", "row_max", "row_bias", "exp_done", "sum_inv", "prob_ok", "tp_mm", "tp_hi", "tp_lo")]
        o_out = [sem("o_out0"), sem("o_out1")]
        y_in = [sem("y_in0"), sem("y_in1")]
        diff_in, gam_step, gam_exp, mask_step, mask_exp = [
            sem(n) for n in ("diff_in", "gam_step", "gam_exp", "mask_step", "mask_exp")]
        r_ev, r_sum, r_hi, r_lo, v_sum, v_mean, v_hi, v_lo = [
            sem(n) for n in ("r_ev", "r_sum", "r_hi", "r_lo", "v_sum", "v_mean", "v_hi", "v_lo")]
        s_mm, s_ev, p_hi, p_lo, o_mm, o_ev, o_sq, o_acc, var_mm, var_std, var_inv, o_normed, r_out = [
            sem(n) for n in ("s_mm", "s_ev", "p_hi", "p_lo", "o_mm", "o_ev", "o_sq", "o_acc", "var_mm", "var_std",
                             "var_inv", "o_normed", "r_out")]
        done = sem("done")
        block = ctx.enter_context(nc.Block())

        def col(name, i=0, n=1):
            return par[:, COL[name] + i:COL[name] + i + n]

        def slot_of(panel):
            return panel % 2

        @block.sync
        def _(sp):
            for n in range(B_FFN + 1):
                if n >= 2:
                    sp.wait_ge(w_ready, n - 1)
                sp.dma_start(stage[:, n % 2], pan_d[n]).then_inc(panel_in[n % 2], 16)
                if n < N_DFT and n % 2:
                    c, dst = n // 2, wm
                elif n >= B_FNET:
                    c, dst = 8 + n - B_FNET, wm_b
                else:
                    continue
                if c == 8:
                    sp.wait_ge(w_used, B_FNET)
                if c >= 2:
                    sp.wait_ge(mod_step, KT * (c - 1))
                if c < 16:
                    sp.dma_start(dst[:, c % 2], wm_d[c]).then_inc(wm_in[c % 2], 16)
            with sp.Fori((B_FFN + 1) // 2, N_PANELS // 2) as i:
                for j in range(2):
                    sp.wait_ge(w_ready, 2 * i + j - 1)
                    sp.dma_start(stage[:, j], pan_d[bass.ds(2 * i + j, 1)].rearrange("a p n -> p (a n)")
                                 ).then_inc(panel_in[j], 16)
            sp.wait_ge(done, 16 * KT)

        @block.gpsimd
        def _(pool):
            def split(n, j, landed):
                pool.wait_ge(panel_in[j], landed)
                nc.gpsimd.tensor_tensor(wh[:, j], stage[:, j], nothing[:].to_broadcast([P, D]), ALU.add).then_inc(w_hi, 1)
                pool.wait_ge(w_hi, n + 1)
                nc.gpsimd.tensor_tensor(wl[:, j], stage[:, j], wh[:, j].bitcast(F32),
                                        ALU.subtract).then_inc(w_ready, 1)

            nc.gpsimd.memset(nothing[:], 0.0).then_inc(nothing_set, 1)
            pool.wait_ge(nothing_set, 1)
            for j in range(2):
                split(j, j, 16)
            with pool.Fori(1, N_PANELS // 2) as i:
                for j in range(2):
                    pool.wait_ge(w_used, 2 * i + j - 1)
                    split(2 * i + j, j, 16 * i + 16)

        nb = [sum(NORM_T[:m]) for m in range(len(NORM_T))]
        sb = [sum(SPLIT_T[:q]) for q in range(len(SPLIT_T))]
        x_tiles = [x[:, k] for k in range(KT)]

        u_panel = [B_A1 + 5 + q + (q >= 4) + (q >= 6) for q in range(KT)]
        u_unit = [5 + q + 2 * (q >= 4) + 2 * (q >= 6) for q in range(KT)]
        pw_panel = [B_A1 + n for n in (9, 12, 15, 16)]
        pw_unit = [9, 13, 17, 19]

        def pv_unit(h, j, last):
            return 8 + 12 * h + j + (8 if j >= 2 and not last else 0)

        def pv_count(h, j, last):
            return 7 + 11 * h + j + 1 + (7 if j >= 2 and not last else 0)

        def proj_unit(h):
            return 0 if isinstance(h, int) and h == 0 else 12 * h - 2

        N_MC = MIX // P // 2

        @block.tensor
        def _(pe):
            def mm3(out, a_hi, a_lo, b_hi, b_lo, first, last):
                nc.tensor.matmul(out, a_hi, b_lo, start=first, stop=False)
                nc.tensor.matmul(out, a_lo, b_hi, start=False, stop=False)
                return nc.tensor.matmul(out, a_hi, b_hi, start=False, stop=last)

            def linear(slot, bank, rhs_hi, rhs_lo, tiles=KT, blk=0, width=P):
                for h in range(2):
                    for k in range(tiles):
                        c = (blk + k) * P
                        last = mm3(ps[:width, bank + h], wh[:, slot, c:c + width], wl[:, slot, c:c + width],
                                   rhs_hi(k)[:, h * HALF:(h + 1) * HALF], rhs_lo(k)[:, h * HALF:(h + 1) * HALF],
                                   k == 0, k == tiles - 1)
                return last

            def norm_sums(m, src=(nacc,)):
                n = m + len(src) - 1
                pe.wait_ge(nm_acc, nb[n] + NORM_T[n])
                for i, acc in enumerate(src):
                    for t in range(KT):
                        last = nc.tensor.matmul(ps[:, 7, i * KT + t:i * KT + t + 1], acc[:, t * P:(t + 1) * P],
                                                ones[:, 0:1], start=True, stop=True)
                last.then_inc(nm_ss, len(src))

            def norm_spread(s):
                pe.wait_ge(nm_dg, KT * (s + 1))
                if s:
                    pe.wait_ge(nm_rbs, s)
                for t in range(KT):
                    last = nc.tensor.matmul(ps[:, 5 + t // 4, (t % 4) * P:(t % 4 + 1) * P], ones[:], diag[:, t],
                                            start=True, stop=True)
                last.then_inc(nm_rb, 1)

            def wait_split(q):
                pe.wait_ge(sp_lo, sb[q] + SPLIT_T[q])

            def linear_pair(q, slot0, bank0, bank1):
                for k in range(KT):
                    pe.wait_ge(sp_lo, sb[q] + k + 1)
                    for n, bank in enumerate((bank0, bank1)):
                        slot, c = (slot0 + n) % 2, k * P
                        for h in range(2):
                            at = slice(h * HALF, (h + 1) * HALF)
                            last = mm3(ps[:, bank + h], wh[:, slot, c:c + P], wl[:, slot, c:c + P],
                                       hh[:, k, at], hl[:, k, at], k == 0, k == KT - 1)
                        if k == KT - 1:
                            last.then_inc(w_used, 1)

            h_hi, h_lo = (lambda k: hh[:, k]), (lambda k: hl[:, k])

            for f0 in (0, 4):
                for t in range(KT):
                    n = f0 * 2 + t
                    pe.wait_ge(w_ready, n + 1)
                    if f0 == 0:
                        pe.wait_ge(xl_done, t + 1)
                    for f in range(4):
                        for c in range(2):
                            if f0 and t == 0:
                                pe.wait_ge(pq_ev, 2 * f + c + 1)
                            a = slice((f0 + f) * P, (f0 + f + 1) * P)
                            b = slice(c * HALF, (c + 1) * HALF)
                            last = mm3(ps[:, 2 * f + c], hh[:, t, a], hl[:, t, a], wh[:, n % 2, b], wl[:, n % 2, b],
                                       t == 0, t == KT - 1)
                    last.then_inc(w_used, 1)
            def mod_sums(half, bank, src):
                pe.wait_ge(mod_step, 8 * KT * (half + 1))
                for c in range(24):
                    last = nc.tensor.matmul(ps[:, bank, c:c + 1], src[:, c * P:(c + 1) * P], ones[:, 0:1],
                                            start=True, stop=True)
                last.then_inc(mod_mm, 1)

            pe.wait_ge(ones_set, 1)
            pe.wait_ge(pq_ev, 16)
            mod_sums(0, 7, macc)
            sc = slot_of(B_CDFT)
            pe.wait_ge(w_ready, B_CDFT + 1)
            for n in range(KT):
                g, m = n // 2, n % 2
                pe.wait_ge(pq_lo, 2 * g + 2)
                if n >= 3:
                    pe.wait_ge(z_ev, n - 2)
                for c in range(2):
                    for k in range(2):
                        blk = slice((c * 4 + m * 2 + k) * P, (c * 4 + m * 2 + k + 1) * P)
                        mm3(ps[:, 2 * (n % 3) + c], wh[:, sc, blk], wl[:, sc, blk],
                            pqh[:, g % 2, k, c * HALF:(c + 1) * HALF], pql[:, g % 2, k, c * HALF:(c + 1) * HALF],
                            k == 0, k == 1)
                if n >= 2:
                    pe.wait_ge(z_ev, n - 1)
                for k in range(2):
                    blk = slice((m * 2 + k) * P, (m * 2 + k + 1) * P)
                    last = mm3(ps[:, 6 + n % 2, 0:2], wh[:, sc, blk], wl[:, sc, blk],
                               pqh[:, g % 2, k, HALF:HALF + 2], pql[:, g % 2, k, HALF:HALF + 2], k == 0, k == 1)
                last.then_inc(w_used if n == KT - 1 else c_mm, 1)
            pe.wait_ge(z_lo, KT)
            with pe.Fori(0, KT // 2) as i:
                for j in range(2):
                    pe.wait_ge(w_ready, B_FNET + 1 + 2 * i + j)
                    pe.wait_ge(fnet_ev, 2 * i + j + 1)
                    linear(slot_of(B_FNET + j), 2 * j, h_hi, h_lo).then_inc(w_used, 1)
            mod_sums(1, 4, macc_b)
            norm_sums(0, (nacc0,))
            norm_spread(0)
            def up(c, base, first=False):
                if first:
                    pe.wait_ge(w_ready, base + 2)
                    linear_pair(0, slot_of(B_FFN), 0, 2)
                for q in range(1 if first else 0, 2):
                    T = 2 * c + q
                    for v in range(2):
                        pe.wait_ge(w_ready, base + 2 * q + v + 1)
                        pe.wait_ge(hid_done if v else g_ev, T)
                        linear(slot_of(B_FFN + 2 * q + v), 2 * v, h_hi, h_lo).then_inc(w_used, 1)

            def down(c, par_c, base, slot0, Tb=0):
                pe.wait_ge(hid_lo, Tb + 2 * c + 2)
                for m in range(KT):
                    d, mm = m // 4, m % 4
                    if mm == 0:
                        pe.wait_ge(w_ready, base + d + 1)
                    pe.wait_ge(dn_ev, dn_base + 8 * c + m + 1)
                    last = linear((slot0 + d) % 2, 4 + 2 * (m % 2), lambda k: hidh[:, par_c, k],
                                  lambda k: hidl[:, par_c, k], tiles=2, blk=2 * mm)
                    last.then_inc(w_used if mm == 3 else dn_mm, 1)

            dn_base = 0
            up(0, B_FFN, first=True)
            with pe.Fori(0, FFN_T // 4) as i:
                for cc in range(2):
                    at = B_FFN + 4 + 12 * i + 6 * cc
                    up(2 * i + cc + 1, at)
                    down(2 * i + cc, cc, at + 4, slot_of(B_FFN))
            down(FFN_T // 2 - 1, 0, B_A1 - 2, slot_of(B_FFN))
            norm_sums(1, (nacc, nacc2))
            norm_spread(1)
            def a1_unit(n, panel, **kw):
                if n >= 2:
                    pe.wait_ge(a_ev, n - 1)
                return linear(slot_of(panel), 2 * (n % 2), **kw)

            def a1_panel(n, panel):
                pe.wait_ge(w_ready, panel + 1)
                a1_unit(n, panel, rhs_hi=h_hi, rhs_lo=h_lo).then_inc(w_used, 1)

            def pool_mix(g):
                pe.wait_ge(w_ready, pw_panel[g] + 1)
                pe.wait_ge(pool_lo, 2 * g + 2)
                for m in range(2):
                    a1_unit(pw_unit[g] + m, pw_panel[g], rhs_hi=lambda k: dh[:, k], rhs_lo=lambda k: dl[:, k],
                            tiles=2, blk=2 * m).then_inc(w_used if m else pw_mm, 1)

            pe.wait_ge(w_ready, B_A1 + 2)
            linear_pair(1, slot_of(B_A1), 0, 2)
            a1_panel(2, B_A1 + 2)
            norm_spread(2)
            for n in range(3, 5):
                a1_panel(n, B_A1 + n)
            a1_panel(u_unit[0], u_panel[0])
            norm_sums(3)
            a1_panel(u_unit[1], u_panel[1])
            norm_spread(3)
            a1_panel(u_unit[2], u_panel[2])
            norm_sums(4)
            norm_spread(4)
            a1_panel(u_unit[3], u_panel[3])
            pool_mix(0)
            for g in (1, 2):
                a1_panel(u_unit[2 * g + 2], u_panel[2 * g + 2])
                a1_panel(u_unit[2 * g + 3], u_panel[2 * g + 3])
                pool_mix(g)
            pool_mix(3)

            pe.sem_inc(tp_mm, 4)
            wait_split(3)
            pe.wait_ge(kr_dve, 3)
            pe.wait_ge(nm_rbs, 5)
            pe.wait_ge(a_ev, 21)

            def bank_of(a):
                if not (isinstance(a, int) and a < 2):
                    pe.wait_ge(aux_ev, a - 1)

            def project(h, b):
                a0 = proj_unit(h)
                slot = slot_of(B_A2 + b)
                pe.wait_ge(w_ready, B_A2 + 1 + h)
                for u in range(8):
                    kind, f = u // 2, u % 2
                    bank_of(a0 + u)
                    out = ps[:, 6 + u % 2]
                    tok = slice(f * HALF, (f + 1) * HALF)
                    if kind < 2:
                        for k in range(3):
                            c = slice((3 * kind + k) * P, (3 * kind + k + 1) * P)
                            last = mm3(out, wh[:, slot, c], wl[:, slot, c], cqh[:, k, tok], cql[:, k, tok],
                                       k == 0, k == 2)
                    elif kind == 2:
                        c = slice(6 * P, 7 * P)
                        last = mm3(out, wh[:, slot, c], wl[:, slot, c], ckh[:, 0, tok], ckl[:, 0, tok], True, True)
                    else:
                        c = slice(7 * P, 8 * P)
                        for t in range(4):
                            at = slice((4 * f + t) * P, (4 * f + t + 1) * P)
                            last = mm3(out[:, t * P:(t + 1) * P], ckh[:, 0, at], ckl[:, 0, at],
                                       wh[:, slot, c], wl[:, slot, c], True, True)
                    last.then_inc(w_used if u == 7 else aux_mm, 1)

            def scores(h, b, t):
                pe.wait_ge(exp_done, 8 * h + t + 1)
                q = slice(t * P, (t + 1) * P)
                for f in range(2):
                    out = ps[:, 2 * (t % 2) + f]
                    key = slice(f * HALF, (f + 1) * HALF)
                    mm3(out, qnh[:, b, q], qnl[:, b, q], knh[:, b, key], knl[:, b, key], True, False)
                    last = mm3(out, qrh[:ROPE, b, q], qrl[:ROPE, b, q], krh[:ROPE, key], krl[:ROPE, key], False, True)
                last.then_inc(sc_mm, 1)

            def turn_probs(h, t):
                pe.wait_ge(prob_ok, 8 * h + t + 1)
                pe.wait_ge(tp_lo, 8 * h + t + 1)
                for k in range(KT):
                    last = nc.tensor.transpose(ps[:, 4 + k // 4, (k % 4) * P:(k % 4 + 1) * P],
                                               prob[:, t % 4, k * P:(k + 1) * P], ident[:])
                last.then_inc(tp_mm, 1)

            def attend(h, b, j, last_head):
                pe.wait_ge(tp_lo, 8 * h + 2 * j + 3)
                bank_of(pv_unit(h, j, last_head))
                for k in range(KT):
                    v = slice(k * P, (k + 1) * P)
                    last = mm3(ps[:, 6 + j % 2, 0:256], vvh[:, b, v], vvl[:, b, v], pth[:, j % 2, k], ptl[:, j % 2, k],
                               k == 0, k == KT - 1)
                last.then_inc(aux_mm, 1)

            def head(h, b, last_head=False):
                pe.wait_ge(rope_lo, 2 * h + 2)
                pe.wait_ge(aux_ev, 12 * h + 6)
                scores(h, b, 0)
                scores(h, b, 1)
                for t in range(2, 8):
                    scores(h, b, t)
                    if t in (4, 6):
                        attend(h, b, t // 2 - 2, last_head)
                    turn_probs(h, t - 2)
                if not last_head:
                    project(h + 1, 1 - b)
                attend(h, b, 2, last_head)
                turn_probs(h, 6)
                turn_probs(h, 7)
                attend(h, b, 3, last_head)

            project(0, 0)
            pe.wait_ge(aux_ev, 8)
            with pe.Fori(0, HEADS // 2 - 1) as i:
                head(2 * i, 0)
                head(2 * i + 1, 1)
            head(HEADS - 2, 0)
            head(HEADS - 1, 1, last_head=True)

            def gate(c, base, Tb):
                for q in range(2):
                    pe.wait_ge(w_ready, base + q + 1)
                    pe.wait_ge(silu_done, Tb + 2 * c + q - 1)
                    linear(q, 2 * q, h_hi, h_lo).then_inc(w_used, 1)

            def mix(f, B):
                nonlocal dn_base
                Tb, dn_base = FFN_T + 16 * f, 8 * (FFN_T // 2 + N_MC * f)
                pe.wait_ge(w_ready, B + 2)
                linear_pair(4 + f, 0, 0, 2)
                with pe.Fori(0, N_MC // 2 - 1) as i:
                    for cc in range(2):
                        c = 2 * i + cc
                        gate(c + 1, B + 2 + 4 * c, Tb)
                        down(c, cc, B + 4 + 4 * c, 0, Tb)
                gate(N_MC - 1, B + 4 * N_MC - 6, Tb)
                down(N_MC - 2, 0, B + 4 * N_MC - 4, 0, Tb)
                down(N_MC - 1, 1, B + 4 * N_MC - 2, 0, Tb)

            pe.wait_ge(aux_ev, pv_unit(HEADS - 1, 3, True) + 1)
            norm_spread(5)
            mix(0, B_A3)
            norm_sums(5)
            norm_spread(6)
            pe.wait_ge(nm_rbs, 7)

            def r_scores(h, ib, j):
                q = slice(ib * IB, (ib + 1) * IB)
                s = ib * KT + j
                if s < 3:
                    pe.wait_ge(v_lo, 8 * h + s + 1)
                else:
                    pe.wait_ge(s_ev, 32 * h + s - 2)
                key = slice(j * P, (j + 1) * P)
                for k in range(2):
                    last = mm3(ps[:, s % 3, 0:IB], rkh[:, k, key], rkl[:, k, key], rqh[:, k, q], rql[:, k, q],
                               k == 0, k == 1)
                last.then_inc(s_mm, 1)

            def r_values(h, ib, j):
                if j == 0:
                    if ib == 0:
                        pe.wait_ge(v_lo, 8 * h + 8)
                    else:
                        pe.wait_ge(o_ev, 16 * h + 4 * ib)
                pe.wait_ge(p_lo, 32 * h + 8 * ib + j + 1)
                for m in range(4):
                    v = slice(m * P, (m + 1) * P)
                    last = mm3(ps[:, 4 + m, 0:IB], vrh[:, j, v], vrl[:, j, v], rph[:, j], rpl[:, j],
                               j == 0, j == KT - 1)
                last.then_inc(o_mm, 1)

            def r_variance(h, ib):
                pe.wait_ge(o_acc, 16 * h + 4 * ib + 4)
                nc.tensor.matmul(ps[:, 3, 0:IB], ones[:], roa[:], start=True, stop=True).then_inc(var_mm, 1)

            def r_head(h, last_head=False):
                base = B_R2 + 8 * h
                for n in range(2, 4):
                    pe.wait_ge(w_ready, base + n + 1)
                    linear(n % 2, 2 * n, h_hi, h_lo).then_inc(w_used, 1)
                for n in range(4):
                    pe.wait_ge(w_ready, base + 4 + n + 1)
                    for t in range(KT):
                        if n == 0:
                            pe.wait_ge(r_ev, 4 * h + (2 if t < 4 else 4))
                        tok = slice(t * P, (t + 1) * P)
                        for kk in range(2):
                            c = slice(kk * R_DV, (kk + 1) * R_DV)
                            last = mm3(ps[:, t], hh[:, 2 * n + kk, tok], hl[:, 2 * n + kk, tok],
                                       wh[:, n % 2, c], wl[:, n % 2, c], n + kk == 0, n + kk == 4)
                    last.then_inc(w_used, 1)
                pe.wait_ge(r_lo, 8 * h + 8)
                for j in range(KT):
                    r_scores(h, 0, j)
                for ib in range(R_BLOCKS):
                    for j in range(KT):
                        r_values(h, ib, j)
                        if ib + 1 < R_BLOCKS and j < R_AHEAD:
                            r_scores(h, ib + 1, j)
                        if ib and j == 1:
                            r_variance(h, ib - 1)
                    if ib + 1 < R_BLOCKS:
                        for j in range(R_AHEAD, KT):
                            r_scores(h, ib + 1, j)
                pe.wait_ge(s_ev, 32 * h + 32)
                if not last_head:
                    pe.wait_ge(w_ready, base + 9)
                    linear(0, 0, h_hi, h_lo).then_inc(w_used, 1)
                r_variance(h, R_BLOCKS - 1)
                pe.wait_ge(var_std, 4 * h + 4)
                if not last_head:
                    pe.wait_ge(w_ready, base + 10)
                    linear(1, 2, h_hi, h_lo).then_inc(w_used, 1)
                pe.wait_ge(o_ev, 16 * h + 16)

            pe.wait_ge(w_ready, B_R2 + 2)
            linear_pair(5, 0, 0, 2)
            with pe.Fori(0, R_HEADS - 1) as h:
                r_head(h)
            r_head(R_HEADS - 1, last_head=True)
            mix(1, B_R3)
            norm_sums(6)
            norm_spread(7)

        @block.scalar
        def _(act):
            def copy(out, in_, **kw):
                return nc.scalar.activation(out, in_, ACT.Copy, **kw)

            def norm_squares(m, src, buf=sqb, made=None, made_from=0):
                for k in range(NORM_T[m]):
                    if made is not None:
                        act.wait_ge(made, made_from + k + 1)
                    if k >= 2:
                        act.wait_ge(nm_acc, nb[m] + k - 1)
                    nc.scalar.activation(buf[:, k % 2], src[k], ACT.Square).then_inc(nm_sq, 1)

            def norm_std(m):
                act.wait_ge(nm_ss, m + 1)
                nc.scalar.activation(stat[:, 0:KT], ps[:, 7, 0:KT], ACT.Sqrt, bias=stat[:, 60:61],
                                     scale=1.0 / NORM_N[m]).then_inc(nm_std, 1)

            def norm_bring(s, dst=rb):
                act.wait_ge(nm_rb, s + 1)
                copy(dst[:].rearrange("p (a n) -> p a n", a=2), ps[:, 5:7]).then_inc(nm_rbs, 1)

            def split_hi(q, dst, shift=None):
                for k in range(SPLIT_T[q]):
                    act.wait_ge(sp_t, sb[q] + k + 1)
                    if shift is None:
                        copy(dst(k), tt[:, k % 2]).then_inc(sp_hi, 1)
                    else:
                        nc.scalar.activation(dst(k), tt[:, k % 2], ACT.Identity, bias=shift(k)).then_inc(sp_hi, 1)

            h_dst = lambda k: hh[:, k]

            act.dma_start(par[:], par_d).then_inc(par_in, 16)
            for i in range(4):
                act.dma_start(x[:, 2 * i:2 * i + 2], xt_d[:, 2 * i:2 * i + 2]).then_inc(xt_in[i], 16)
            act.dma_start(ident[:], ident_d).then_inc(ident_in, 16)
            act.wait_ge(par_in, 16)
            nc.scalar.activation(silu_c[:], col("c", 0, KT), ACT.Silu).then_inc(c_ready, 1)
            act.wait_ge(zero_set, 1)
            for i in range(KT // 2):
                act.wait_ge(xt_in[i], 16)
                for t in (2 * i, 2 * i + 1):
                    if t >= 2:
                        act.wait_ge(row_ss, t - 1)
                    nc.scalar.activation(pq[:, 2 * (t % 2):2 * (t % 2) + 2].rearrange("p a n -> p (a n)"), x[:, t],
                                         ACT.Square, accum_out=stat[:, 8 + t:9 + t]).then_inc(row_ss, 1)
                act.wait_ge(row_ss, 2 * i + 2)
                nc.scalar.activation(stat[:, 16 + 2 * i:18 + 2 * i], stat[:, 8 + 2 * i:10 + 2 * i], ACT.Sqrt,
                                     bias=stat[:, 60:61], scale=1.0 / D).then_inc(row_std, 1)
                act.wait_ge(row_inv, i + 1)
                for t in (2 * i, 2 * i + 1):
                    copy(hh[:, t], x[:, t], scale=rr[:, 7, t:t + 1]).then_inc(xh_done, 1)
            for f0 in (0, 4):
                act.wait_ge(w_used, 2 * f0 + KT)
                for f in range(4):
                    for c in range(2):
                        copy(pq[:, 2 * (f0 + f) + c], ps[:, 2 * f + c]).then_inc(pq_ev, 1)

            act.wait_ge(xl_done, KT)
            act.dma_start(x[:], x_d).then_inc(x_in, 16)

            def pq_split(f):
                act.wait_ge(pq_scaled, 3 * (f + 1))
                if f >= 4:
                    act.wait_ge(c_mm, 2 * (f // 2) - 2)
                copy(pqh[:, f // 2 % 2, f % 2], pq[:, 2 * f:2 * f + 2].rearrange("p a n -> p (a n)")).then_inc(pq_hi, 1)

            def v_copy(n):
                if n == KT - 1:
                    act.wait_ge(w_used, B_CDFT + 1)
                else:
                    act.wait_ge(c_mm, n + 1)
                if n >= 1:
                    act.wait_ge(z_ev, n)
                copy(vs[:], ps[:, 2 * (n % 3) + 1]).then_inc(v_copied, 1)

            def z_hi_copy(n):
                act.wait_ge(z_ev, n + 1)
                copy(hh[:, n], zt[:, n % 2]).then_inc(z_hi, 1)

            for f in range(2):
                pq_split(f)
            for g in range(4):
                if g < 3:
                    pq_split(2 * g + 2)
                    pq_split(2 * g + 3)
                for n in (2 * g, 2 * g + 1):
                    v_copy(n)
                    if n:
                        z_hi_copy(n - 1)
            z_hi_copy(KT - 1)
            act.wait_ge(z_lo, KT)
            act.dma_start(posi[:], pos_d).then_inc(pos_in, 16)
            act.wait_ge(trig_step, 8)
            nc.scalar.activation(trig_a[:], ang[:], ACT.Sin).then_inc(trig_sin, 1)

            norm_squares(0, x_tiles, sqb0, fnet_ev, 2)
            norm_std(0)
            norm_bring(0)
            split_hi(0, h_dst, lambda k: modc[:, 24 + k:25 + k])

            act.wait_ge(zero_set, 4)

            def ffn_act(c, base, first=False):
                for q in range(2):
                    T = 2 * c + q
                    act.wait_ge(w_used, base + 2 * q + 1)
                    if not (first and q == 0):
                        act.wait_ge(cv_step, 3 * T)
                    copy(gbuf[:, 1:L + 1].rearrange("p (a n) -> p a n", a=2), ps[:, 0:2]).then_inc(g_ev, 1)
                    act.wait_ge(cv_step, 3 * T + 3)
                    nc.scalar.activation(act_g[:], conv[:], ACT.Silu).then_inc(silu_done, 1)
                    act.wait_ge(hid_done, T + 1)
                    yield T, q

            def ffn_hi(T, q, par_c):
                copy(hidh[:, par_c, q], hid[:]).then_inc(hid_hi, 1)

            for T, q in ffn_act(0, B_FFN, first=True):
                ffn_hi(T, q, 0)
            for T, q in ffn_act(1, B_FFN + 4):
                ffn_hi(T, q, 1)
            with act.Fori(1, FFN_T // 4) as i:
                for cc in range(2):
                    at = B_FFN - 2 + 12 * i + 6 * cc
                    for T, q in ffn_act(2 * i + cc, at):
                        act.wait_ge(w_used, at)
                        ffn_hi(T, q, cc)
            at = B_FFN - 2 + 6 * (FFN_T // 2 - 1)
            for T, q in ffn_act(FFN_T // 2 - 1, at):
                act.wait_ge(w_used, at)
                ffn_hi(T, q, 0)
            for k in range(KT):
                act.wait_ge(dn_ev, 2 + 8 * (FFN_T // 2 - 1) + k + 1)
                if k >= 2:
                    act.wait_ge(nm_acc, nb[1] + 2 * k - 3)
                nc.scalar.activation(sqb[:, k % 2], x[:, k], ACT.Square).then_inc(nm_sq, 1)
                if k >= 2:
                    act.wait_ge(nm_acc, nb[1] + 2 * k - 2)
                nc.scalar.activation(sqb2[:, k % 2], x[:, k], ACT.Square, scale=col("g_final1", k)).then_inc(nm_sq, 1)
            norm_std(1)
            act.wait_ge(ga_set, 3)
            act.wait_ge(nm_r, 2)
            nc.scalar.activation(stat[:, 0:KT], stat[:, 8:8 + KT], ACT.Sqrt, bias=stat[:, 60:61],
                                 scale=1.0 / D).then_inc(nm_std, 1)
            norm_bring(1)
            split_hi(1, h_dst)

            def bring(n, panel, out, **kw):
                act.wait_ge(w_used, panel + 1)
                copy(out.rearrange("p (a n) -> p a n", a=2), ps[:, 2 * (n % 2):2 * (n % 2) + 2], **kw).then_inc(a_ev, 1)

            def bring_u(q):
                if q >= 2:
                    act.wait_ge(pool_lo, q - 1)
                bring(u_unit[q], u_panel[q], ub[q % 2][:, 8:8 + L])

            def pool_hi_copy(q):
                act.wait_ge(pool_d, q + 1)
                if q >= 2:
                    act.wait_ge(w_used, pw_panel[q // 2 - 1] + 1)
                copy(dh[:, q % 2], ub[2 + pool_out(q)][:, 8:8 + L]).then_inc(pool_hi, 1)

            def pool_store(g):
                for m in range(2):
                    if m == 0:
                        act.wait_ge(pw_mm, g + 1)
                    if g:
                        act.wait_ge(yp_out[m], 16 * g)
                    bring(pw_unit[g] + m, pw_panel[g] + m - 1, yp[:, m], scale=col("pool_scale", 2 * g + m))
                    act.wait_ge(a_ev, pw_unit[g] + m + 1)
                    act.dma_start(y_d[8 + 2 * g + m], yp[:, m]).then_inc(yp_out[m], 16)

            for n in range(2):
                bring(n, B_A1 + n, cqf[:, n])
            norm_bring(2, rb2)
            for n in range(2, 4):
                bring(n, B_A1 + n, cqf[:, n])
            act.wait_ge(x3_done, KT)
            act.dma_start(xs_d, x[:]).then_inc(spilled, 16)
            bring(4, B_A1 + 4, kt_t[:])
            act.wait_ge(spilled, 16)
            act.wait_ge(a_ev, 4)
            norm_squares(3, [cqf[:, k] for k in range(3)])
            act.wait_ge(kr_dve, 1)
            copy(ks_t[:ROPE], kt_t[ROPE:]).then_inc(kr_act, 1)
            act.wait_ge(kr_dve, 2)
            copy(krh[:ROPE], kt_t[:ROPE]).then_inc(kr_act, 1)
            act.wait_ge(zero_set, 5)
            bring_u(0)
            norm_std(3)
            bring_u(1)
            norm_bring(3)
            split_hi(2, lambda k: cqh[:, k])
            norm_squares(4, [cqf[:, 3]])
            pool_hi_copy(0)
            bring_u(2)
            norm_std(4)
            norm_bring(4)
            split_hi(3, lambda k: ckh[:, 0])
            pool_hi_copy(1)
            bring_u(3)
            pool_store(0)
            for g in (1, 2):
                pool_hi_copy(2 * g)
                bring_u(2 * g + 2)
                pool_hi_copy(2 * g + 1)
                bring_u(2 * g + 3)
                pool_store(g)
            pool_hi_copy(6)
            pool_hi_copy(7)
            pool_store(3)

            act.sem_inc(exp_done, 2)
            for s in o_out:
                act.sem_inc(s, 16)

            def project_act(h, b, m0):
                def hi(u, dst, panel=None):
                    if panel is None:
                        act.wait_ge(aux_mm, m0 + u + 1)
                    else:
                        act.wait_ge(w_used, panel)
                    copy(dst[:, b, (u % 2) * HALF:(u % 2 + 1) * HALF], ps[:, 6 + u % 2]).then_inc(ax_hi, 1)

                def shift(f):
                    act.wait_ge(aux_ev, proj_unit(h) + 3 + f)
                    copy(rs_t[:ROPE, f], rt[ROPE:, f]).then_inc(rope_shift, 1)

                def rot_hi(f):
                    act.wait_ge(rope_sum, 2 * h + f + 1)
                    copy(qrh[:ROPE, b, f * HALF:(f + 1) * HALF], rf_t[:ROPE, f]).then_inc(rope_hi, 1)

                hi(0, qnh)
                hi(1, qnh)
                shift(0)
                shift(1)
                hi(4, knh)
                rot_hi(0)
                hi(5, knh)
                rot_hi(1)
                hi(6, vvh)
                hi(7, vvh, B_A2 + 1 + h)

            def exp_row(h, t):
                act.wait_ge(row_bias, 8 * h + t + 1)
                act.wait_ge(tp_mm, 8 * h + t + 1)
                nc.scalar.activation(prob[:, t % 4].rearrange("p (a n) -> p a n", a=2),
                                     ps[:, 2 * (t % 2):2 * (t % 2) + 2], ACT.Exp, bias=stat[:, 28 + t % 4:29 + t % 4],
                                     scale=ATT_SCALE, accum_out=stat[:, 48 + t % 4:49 + t % 4]).then_inc(exp_done, 1)

            def turned_hi(h, t):
                j = t // 2
                act.wait_ge(tp_mm, 8 * h + t + 5)
                act.wait_ge(aux_mm, 11 * h + 6 + j)
                copy(pth[:, j % 2, :, (t % 2) * P:(t % 2 + 1) * P],
                     ps[:, 4:6].rearrange("p a (b n) -> p (a b) n", n=P)).then_inc(tp_hi, 1)

            def store_o(h, j, last_head):
                act.wait_ge(aux_ev, pv_unit(h, j, last_head) + 1)
                dst = y_d[h] if isinstance(h, int) else y_d[bass.ds(h, 1)].rearrange("a p n -> p (a n)")
                act.dma_start(dst[:, j * 256:(j + 1) * 256], osb[:, j % 2]).then_inc(o_out[j % 2], 16)

            def head_act(h, b, last_head=False):
                exp_row(h, 0)
                exp_row(h, 1)
                for t in range(2, 8):
                    exp_row(h, t)
                    turned_hi(h, t - 2)
                    if t in (5, 7):
                        store_o(h, (t - 5) // 2, last_head)
                if not last_head:
                    project_act(h + 1, 1 - b, 9 + 11 * h)
                turned_hi(h, 6)
                store_o(h, 2, last_head)
                turned_hi(h, 7)
                store_o(h, 3, last_head)

            for s in yp_out:
                act.wait_ge(s, 16 * POOL_G)
            project_act(0, 0, 0)
            with act.Fori(0, HEADS // 2 - 1) as i:
                head_act(2 * i, 0)
                head_act(2 * i + 1, 1)
            head_act(HEADS - 2, 0)
            act.wait_ge(w_used, B_A3)
            act.dma_start(x[:], xs_d).then_inc(x_in, 16)
            head_act(HEADS - 1, 1, last_head=True)

            for s in o_out:
                act.wait_ge(s, 16 + 16 * 2 * HEADS)
            for s in yp_out:
                act.wait_ge(s, 16 * POOL_G)
            norm_bring(5)
            split_hi(4, h_dst)

            def gate_act(c, b, base, Tb, used=None):
                if used is not None:
                    act.wait_ge(hid_done, Tb + 2 * c - 2)
                src = y_d[2 * c:2 * c + 2] if isinstance(c, int) else y_d[bass.ds(2 * c, 2)]
                act.dma_start(ybuf[:, b], src.rearrange("a p n -> p a n")).then_inc(y_in[b], 16)
                for q in range(2):
                    T = 2 * c + q
                    act.wait_ge(w_used, base + q + 1)
                    act.wait_ge(hid_done, Tb + T)
                    nc.scalar.activation(sg[:].rearrange("p (a n) -> p a n", a=2), ps[:, 2 * q:2 * q + 2],
                                         ACT.Silu).then_inc(silu_done, 1)
                    act.wait_ge(hid_done, Tb + T + 1)
                    if used is not None:
                        act.wait_ge(w_used, used)
                    copy(hidh[:, b, q], yg[:]).then_inc(hid_hi, 1)

            def mix_act(f, B):
                Tb = FFN_T + 16 * f
                gate_act(0, 0, B, Tb)
                gate_act(1, 1, B + 2, Tb)
                with act.Fori(1, N_MC // 2) as i:
                    for cc in range(2):
                        at = B - 2 + 8 * i + 4 * cc
                        gate_act(2 * i + cc, cc, at, Tb, used=at)

            def x_made(f):
                return dict(made=dn_ev, made_from=2 + 8 * (FFN_T // 2 + N_MC * (f + 1) - 1))

            mix_act(0, B_A3)
            norm_squares(5, x_tiles, **x_made(0))
            act.wait_ge(dn_ev, 2 + 8 * (FFN_T // 2 + N_MC))
            act.dma_start(posi[:], pos_d).then_inc(pos_in, 16)
            act.dma_start(xs_d, x[:]).then_inc(spilled, 16)
            norm_std(5)
            norm_bring(6)
            split_hi(5, h_dst)

            act.wait_ge(trig_step, 16)
            nc.scalar.activation(cos_r[:], ang[:], ACT.Sin).then_inc(trig_sin, 1)
            act.wait_ge(trig_step, 24)
            nc.scalar.activation(sin_r[:], ang[:], ACT.Sin).then_inc(trig_sin, 1)
            act.wait_ge(gam_step, 1)
            nc.scalar.activation(lgam[:, 8:16], lgam[:, 0:8], ACT.Exp, scale=-1.0).then_inc(gam_exp, 1)
            act.wait_ge(spilled, 32)

            def r_probs_hi(h, ib, j):
                if ib:
                    act.wait_ge(o_mm, 32 * h + 8 * (ib - 1) + j + 1)
                act.wait_ge(s_ev, 32 * h + 8 * ib + j + 1)
                copy(rph[:, j], rsm[:, j % 2]).then_inc(p_hi, 1)

            def r_head_act(h, last_head=False):
                base = B_R2 + 8 * h
                act.wait_ge(mask_step, 2 * h + 2)
                nc.scalar.activation(mask[:], mask[:], ACT.Exp).then_inc(mask_exp, 1)
                for u in range(4):
                    dst, f = (rqh, rkh)[u // 2], u % 2
                    for m in range(2):
                        act.wait_ge(r_sum, 8 * h + 2 * u + m + 1)
                        copy(dst[:, m, f * HALF:(f + 1) * HALF], rta[:, 2 * m]).then_inc(r_hi, 1)
                act.wait_ge(w_used, base + 8)
                act.wait_ge(r_lo, 8 * h + 8)
                for t in range(KT + 1):
                    if t < KT:
                        if t >= 2:
                            act.wait_ge(v_sum, 8 * h + t - 1)
                        copy(rta[:, t % 2], ps[:, t], accum_out=stat[:, 8 + t:9 + t]).then_inc(v_sum, 1)
                    if t:
                        act.wait_ge(v_mean, 8 * h + t)
                        nc.scalar.activation(vrh[:, t - 1], ps[:, t - 1], ACT.Identity,
                                             bias=stat[:, 31 + t:32 + t]).then_inc(v_hi, 1)
                for j in range(KT):
                    r_probs_hi(h, 0, j)
                for ib in range(R_BLOCKS):
                    if ib + 1 < R_BLOCKS:
                        for j in range(R_AHEAD):
                            r_probs_hi(h, ib + 1, j)
                    act.wait_ge(o_mm, 32 * h + 8 * ib + 8)
                    if ib:
                        act.wait_ge(r_out, 16 * (4 * h + ib))
                    for m in range(4):
                        copy(ro[:, m], ps[:, 4 + m, 0:IB]).then_inc(o_ev, 1)
                    if ib + 1 < R_BLOCKS:
                        for j in range(R_AHEAD, KT):
                            r_probs_hi(h, ib + 1, j)
                    for m in range(4):
                        n = 4 * ib + m
                        act.wait_ge(o_ev, 16 * h + n + 1)
                        if m >= 2:
                            act.wait_ge(o_acc, 16 * h + n - 1)
                        nc.scalar.activation(rsq[:, m % 2], ro[:, m], ACT.Square).then_inc(o_sq, 1)
                    if ib + 1 == R_BLOCKS and not last_head:
                        act.wait_ge(s_ev, 32 * h + 32)
                        act.dma_start(mask[:], diff_d).then_inc(diff_in, 16)
                    act.wait_ge(var_mm, 4 * h + ib + 1)
                    nc.scalar.activation(rstd[:], ps[:, 3, 0:IB], ACT.Sqrt, bias=stat[:, 60:61],
                                         scale=1.0 / R_DV).then_inc(var_std, 1)
                    act.wait_ge(o_normed, 16 * h + 4 * ib + 4)
                    act.dma_start(y_d[bass.ds(4 * h, 4)].rearrange("a p n -> p a n")[:, :, ib * IB:(ib + 1) * IB],
                                  ro[:]).then_inc(r_out, 16)
                act.wait_ge(r_out, 16 * (4 * h + 4))

            act.wait_ge(trig_sin, 3)
            act.dma_start(mask[:], diff_d).then_inc(diff_in, 16)
            with act.Fori(0, R_HEADS - 1) as h:
                r_head_act(h)
            r_head_act(R_HEADS - 1, last_head=True)
            act.wait_ge(w_used, B_R3)
            act.wait_ge(o_mm, 32 * R_HEADS)
            act.dma_start(x[:], xs_d).then_inc(x_in, 16)
            mix_act(1, B_R3)
            norm_squares(6, x_tiles, **x_made(1))
            norm_std(6)
            norm_bring(7)
            for k in range(KT):
                act.wait_ge(x3_done, KT + k + 1)
                act.dma_start(out_d[:, k], x[:, k]).then_inc(done, 16)

        @block.vector
        def _(dve):
            V = nc.vector

            spread = [0]

            def lo_of(out, value, hi):
                return V.tensor_tensor(out, value, hi.bitcast(F32), ALU.subtract)

            def add_square(n, j, first, acc=nacc, buf=sqb):
                dve.wait_ge(nm_sq, n + 1)
                if first:
                    V.tensor_copy(acc[:], buf[:, j]).then_inc(nm_acc, 1)
                else:
                    dve.wait_ge(nm_acc, n)
                    V.tensor_tensor(acc[:], acc[:], buf[:, j], ALU.add).then_inc(nm_acc, 1)

            def norm_add(m):
                for k in range(NORM_T[m]):
                    add_square(nb[m] + k, k % 2, k == 0)

            def add_both(k):
                add_square(nb[1] + 2 * k, k % 2, k == 0)
                add_square(nb[1] + 2 * k + 1, k % 2, k == 0, nacc2, sqb2)

            def norm_invert(m):
                dve.wait_ge(nm_std, m + 1)
                V.reciprocal(rr[:, m], stat[:, 0:KT]).then_inc(nm_r, 1)
                dve.wait_ge(nm_r, m + 1)

            def norm_diag(m):
                if spread[0]:
                    dve.wait_ge(nm_dg, KT * spread[0])
                spread[0] += 1
                for t in range(KT):
                    V.tensor_scalar(diag[:, t], ident[:], rr[:, m, t:t + 1], None, ALU.mult).then_inc(nm_dg, 1)

            def split(q, src, scale, dst, shift=None):
                for k in range(SPLIT_T[q] + 1):
                    if k < SPLIT_T[q]:
                        if sb[q] + k >= 2:
                            dve.wait_ge(sp_lo, sb[q] + k - 1)
                        V.scalar_tensor_tensor(tt[:, k % 2], src(k), scale(k), rb[:], ALU.mult,
                                               ALU.mult).then_inc(sp_t, 1)
                    if k:
                        j = k - 1
                        dve.wait_ge(sp_hi, sb[q] + j + 1)
                        if shift is None:
                            lo_of(dst(j)[1], tt[:, j % 2], dst(j)[0]).then_inc(sp_lo, 1)
                        else:
                            V.scalar_tensor_tensor(dst(j)[1], tt[:, j % 2], shift(j), dst(j)[0].bitcast(F32),
                                                   ALU.add, ALU.subtract).then_inc(sp_lo, 1)

            h_dst = lambda k: (hh[:, k], hl[:, k])

            dve.sem_inc(fnet_ev, 2)
            dve.sem_inc(dn_ev, 2)
            V.memset(stat[:, 60:61], EPS).then_inc(zero_set, 1)
            V.memset(stat[:, 61:62], 0.0).then_inc(zero_set, 1)
            V.memset(stat[:, 62:63], 0.0).then_inc(zero_set, 1)
            V.memset(ones[:], 1.0).then_inc(ones_set, 1)
            for i in range(KT // 2):
                dve.wait_ge(row_std, i + 1)
                V.reciprocal(rr[:, 7, 2 * i:2 * i + 2], stat[:, 16 + 2 * i:18 + 2 * i]).then_inc(row_inv, 1)
                dve.wait_ge(row_inv, i + 1)
                for t in (2 * i, 2 * i + 1):
                    dve.wait_ge(xh_done, t + 1)
                    V.scalar_tensor_tensor(hl[:, t], x[:, t], rr[:, 7, t:t + 1], hh[:, t].bitcast(F32), ALU.mult,
                                           ALU.subtract).then_inc(xl_done, 1)

            def mod_chunk(c, j, src, dst, at, landed):
                dve.wait_ge(wm_in[j], landed)
                out = dst[:, bass.ds(at, WMC)]
                for k in range(KT):
                    w = src[:, j, k * WMC:(k + 1) * WMC]
                    if k == 0:
                        V.tensor_scalar(out, w, silu_c[:, 0:1], None, ALU.mult).then_inc(mod_step, 1)
                    else:
                        dve.wait_ge(mod_step, c * KT + k)
                        V.scalar_tensor_tensor(out, w, silu_c[:, k:k + 1], out, ALU.mult,
                                               ALU.add).then_inc(mod_step, 1)

            dve.wait_ge(c_ready, 1)
            with dve.Fori(0, 4) as i:
                for j in range(2):
                    mod_chunk(2 * i + j, j, wm, macc, (2 * i + j) * WMC, 16 * i + 16)
            dve.wait_ge(mod_mm, 1)
            V.tensor_tensor(modc[:, 0:24], ps[:, 7, 0:24], col("b_mod", 0, 24), ALU.add).then_inc(mod_ready, 1)
            dve.wait_ge(mod_ready, 1)
            V.scalar_tensor_tensor(s1[:], modc[:, 8:16], 1.0, col("g_mix", 0, KT), ALU.add, ALU.mult).then_inc(mod_s, 1)
            V.tensor_scalar(sh2x[:], modc[:, 0:8], L / 512.0, None, ALU.mult).then_inc(mod_s, 1)
            dve.wait_ge(mod_s, 2)
            dve.wait_ge(pq_ev, 16)

            def pq_scale(f):
                for c in range(2):
                    V.tensor_scalar(pq[:, 2 * f + c], pq[:, 2 * f + c], s1[:, f:f + 1], None,
                                    ALU.mult).then_inc(pq_scaled, 1)
                dve.wait_ge(pq_scaled, 3 * f + 1)
                V.tensor_tensor(pq[:, 2 * f, 0:1], pq[:, 2 * f, 0:1], sh2x[:, f:f + 1], ALU.add).then_inc(pq_scaled, 1)

            def pq_low(f):
                dve.wait_ge(pq_hi, f + 1)
                lo_of(pql[:, f // 2 % 2, f % 2], pq[:, 2 * f:2 * f + 2].rearrange("p a n -> p (a n)"),
                      pqh[:, f // 2 % 2, f % 2]).then_inc(pq_lo, 1)

            def z_make(n):
                dve.wait_ge(v_copied, n + 1)
                if n >= 2:
                    dve.wait_ge(z_lo, n - 1)
                u, b = ps[:, 2 * (n % 3)], n % 2
                V.tensor_tensor(zt[:, b, 1:HALF], u[:, 1:HALF], vs[:, 1:HALF], ALU.subtract)
                V.tensor_tensor(zt[:, b, L - 1:HALF:-1], u[:, 1:HALF], vs[:, 1:HALF], ALU.add)
                V.tensor_copy(zt[:, b, 0:1], u[:, 0:1])
                V.tensor_copy(zt[:, b, HALF:HALF + 1], ps[:, 6 + n % 2, 0:1]).then_inc(z_ev, 1)

            def z_low(n):
                dve.wait_ge(z_hi, n + 1)
                lo_of(hl[:, n], zt[:, n % 2], hh[:, n]).then_inc(z_lo, 1)

            pq_scale(0)
            pq_scale(1)
            pq_low(0)
            pq_low(1)
            for g in range(4):
                if g < 3:
                    pq_scale(2 * g + 2)
                    pq_scale(2 * g + 3)
                    pq_low(2 * g + 2)
                    pq_low(2 * g + 3)
                for n in (2 * g, 2 * g + 1):
                    z_make(n)
                    if n:
                        z_low(n - 1)
            z_low(KT - 1)

            def angles(inv, turn, rad, s0):
                step = [s0]

                def then(ins):
                    ins.then_inc(trig_step, 1)
                    step[0] += 1
                    dve.wait_ge(trig_step, step[0])

                then(V.tensor_scalar(ang[:], posf[:], inv, None, ALU.mult))
                then(V.tensor_scalar(turns[:], ang[:], 1.0 / TWO_PI, turn, ALU.mult, ALU.add))
                then(V.tensor_scalar(turns[:], turns[:], ROUND, ROUND, ALU.add, ALU.subtract))
                then(V.scalar_tensor_tensor(ang[:], turns[:], -C1, ang[:], ALU.mult, ALU.add))
                then(V.scalar_tensor_tensor(ang[:], turns[:], -C2, ang[:], ALU.mult, ALU.add))
                then(V.scalar_tensor_tensor(ang[:], turns[:], -C3, ang[:], ALU.mult, ALU.add))
                then(V.tensor_scalar(ang[:], ang[:], rad, PI_IN, ALU.add, ALU.min))

            dve.wait_ge(pos_in, 16)
            V.tensor_copy(posf[:], posi[:]).then_inc(pos_float, 1)
            dve.wait_ge(pos_float, 1)
            angles(col("inv_a"), col("turn_a"), col("rad_a"), 0)
            V.tensor_scalar(ang[:], ang[:], -PI_IN, None, ALU.max).then_inc(trig_step, 1)

            dve.wait_ge(x_in, 16)

            def fnet_update(i, first=False):
                for j in range(2):
                    n = 2 * i + j
                    mod_chunk(8 + n, j, wm_b, macc_b, n * WMC, 16 * i + 80)
                    dve.wait_ge(w_used, B_FNET + 1 + n)
                    xm = x[:, bass.ds(n, 1)].rearrange("p a (b n) -> p (a b) n", b=2)
                    V.scalar_tensor_tensor(xm, ps[:, 2 * j:2 * j + 2], modc[:, bass.ds(16 + n, 1)], xm,
                                           ALU.mult, ALU.add).then_inc(fnet_ev, 1)
                    if not (first and j == 0):
                        add_square(n - 1, 1 - j, first, nacc0, sqb0)

            fnet_update(0, first=True)
            with dve.Fori(1, KT // 2) as i:
                fnet_update(i)
            add_square(KT - 1, 1, False, nacc0, sqb0)
            dve.wait_ge(mod_mm, 2)
            V.tensor_tensor(modc[:, 24:48], ps[:, 4, 0:24], col("b_mod", 24, 24), ALU.add).then_inc(mod_ready, 1)
            dve.wait_ge(mod_ready, 2)
            V.scalar_tensor_tensor(s2[:], modc[:, 32:40], 1.0, col("g_ffn", 0, KT), ALU.add, ALU.mult).then_inc(mod_s, 1)
            dve.wait_ge(mod_s, 3)
            V.tensor_tensor(ga[:], col("g_final1", 0, KT), col("a_norm", 0, KT), ALU.mult).then_inc(ga_set, 1)
            dve.wait_ge(ident_in, 16)
            norm_invert(0)
            norm_diag(0)
            dve.wait_ge(nm_rbs, 1)
            split(0, lambda k: x[:, k], lambda k: s2[:, k:k + 1], h_dst, lambda k: modc[:, 24 + k:25 + k])

            V.memset(gbuf[:, 0:1], 0.0)
            V.memset(gbuf[:, L + 1:L + 2], 0.0).then_inc(zero_set, 1)

            def hidden(c, base, par_c, first=False):
                for q in range(2):
                    T = 2 * c + q
                    tap = lambda j: par[:, bass.ds(COL["conv"] + j * FFN_T + T, 1)]
                    dve.wait_ge(g_ev, T + 1)
                    V.tensor_scalar(conv[:], gbuf[:, 1:L + 1], tap(1), par[:, bass.ds(COL["b_conv"] + T, 1)],
                                    ALU.mult, ALU.add).then_inc(cv_step, 1)
                    dve.wait_ge(cv_step, 3 * T + 1)
                    V.scalar_tensor_tensor(conv[:], gbuf[:, 0:L], tap(0), conv[:], ALU.mult,
                                           ALU.add).then_inc(cv_step, 1)
                    dve.wait_ge(cv_step, 3 * T + 2)
                    V.scalar_tensor_tensor(conv[:], gbuf[:, 2:L + 2], tap(2), conv[:], ALU.mult,
                                           ALU.add).then_inc(cv_step, 1)
                    dve.wait_ge(silu_done, T + 1)
                    dve.wait_ge(w_used, base + 2 * q + 2)
                    if not (first and q == 0):
                        dve.wait_ge(hid_lo, T)
                    V.tensor_tensor(hid[:].rearrange("p (a n) -> p a n", a=2), ps[:, 2:4],
                                    act_g[:].rearrange("p (a n) -> p a n", a=2), ALU.mult).then_inc(hid_done, 1)
                    dve.wait_ge(hid_hi, T + 1)
                    dve.wait_ge(hid_done, T + 1)
                    lo_of(hidl[:, par_c, q], hid[:], hidh[:, par_c, q]).then_inc(hid_lo, 1)

            def add_down(c, base, mm_base, gate=None, square=None):
                for m in range(KT):
                    d, mm = m // 4, m % 4
                    if mm == 3:
                        dve.wait_ge(w_used, base + d + 1)
                    else:
                        dve.wait_ge(dn_mm, mm_base + 6 * c + 3 * d + mm + 1)
                    dve.wait_ge(dn_ev, dn_base + 8 * c + m + 2)
                    xm = x[:, m].rearrange("p (a n) -> p a n", a=2)
                    out = ps[:, 4 + 2 * (m % 2):6 + 2 * (m % 2)]
                    if gate is None:
                        V.tensor_tensor(xm, out, xm, ALU.add).then_inc(dn_ev, 1)
                    else:
                        V.scalar_tensor_tensor(xm, out, gate(m), xm, ALU.mult, ALU.add).then_inc(dn_ev, 1)
                    if square is not None and m:
                        square(m - 1)
                if square is not None:
                    square(KT - 1)

            dn_base = 0
            gt2 = lambda m: modc[:, 40 + m:41 + m]
            hidden(0, B_FFN, 0, first=True)
            with dve.Fori(0, FFN_T // 4) as i:
                for cc in range(2):
                    at = B_FFN + 4 + 12 * i + 6 * cc
                    hidden(2 * i + cc + 1, at, 1 - cc)
                    add_down(2 * i + cc, at + 4, 0, gt2)
            add_down(FFN_T // 2 - 1, B_A1 - 2, 0, gt2, add_both)
            norm_invert(1)
            V.tensor_tensor(rr[:, 7], rr[:, 1], rr[:, 1], ALU.mult).then_inc(ga_set, 1)
            dve.wait_ge(ga_set, 2)
            V.tensor_tensor(stat[:, 8:8 + KT], ps[:, 7, KT:2 * KT], rr[:, 7], ALU.mult).then_inc(ga_set, 1)
            norm_invert(2)
            dve.wait_ge(ga_set, 3)
            V.tensor_tensor(rr[:, 7], rr[:, 1], rr[:, 2], ALU.mult).then_inc(ga_set, 1)
            dve.wait_ge(ga_set, 4)
            norm_diag(7)
            dve.wait_ge(nm_rbs, 2)
            split(1, lambda k: x[:, k], lambda k: ga[:, k:k + 1], h_dst)
            norm_diag(1)
            for i in range(2):
                V.memset(ub[i][:, 0:8], 0.0)
                last = V.memset(ub[i][:, 8 + L:PADW], 0.0)
            last.then_inc(zero_set, 1)
            dve.wait_ge(nm_rbs, 3)
            for k in range(KT):
                V.scalar_tensor_tensor(x[:, k], x[:, k], col("g_final1", k), rb2[:], ALU.mult,
                                       ALU.mult).then_inc(x3_done, 1)
            norm_add(3)
            dve.wait_ge(a_ev, 5)
            dve.wait_ge(trig_sin, 1)
            V.tensor_tensor(kt_t[:], kt_t[:], trig_a[:], ALU.mult).then_inc(kr_dve, 1)
            dve.wait_ge(kr_act, 1)
            dve.wait_ge(kr_dve, 1)
            V.tensor_tensor(kt_t[:ROPE], kt_t[:ROPE], ks_t[:ROPE], ALU.add).then_inc(kr_dve, 1)
            dve.wait_ge(kr_act, 2)
            dve.wait_ge(kr_dve, 2)
            lo_of(krl[:ROPE], kt_t[:ROPE], krh[:ROPE]).then_inc(kr_dve, 1)
            norm_invert(3)
            norm_diag(3)
            dve.wait_ge(nm_rbs, 4)
            dve.wait_ge(spilled, 16)
            split(2, lambda k: cqf[:, k], lambda k: col("q_norm", k), lambda k: (cqh[:, k], cql[:, k]))
            norm_add(4)
            pstep = [0]

            def pool_tile(q):
                g = q // 2
                w = pool_window(g)

                def then(ins):
                    ins.then_inc(pool_step, 1)
                    pstep[0] += 1
                    dve.wait_ge(pool_step, pstep[0])

                dve.wait_ge(a_ev, u_unit[q] + 1)
                if q:
                    dve.wait_ge(pool_lo, q)
                u = ub[q % 2]
                src, b = u, 0
                for left, right, lo, hi in pool_levels(g):
                    dst = ub[2 + b]
                    then(V.tensor_tensor(dst[:, 8 + lo:8 + hi], src[:, 8 + lo - left:8 + hi - left],
                                         src[:, 8 + lo + right:8 + hi + right], ALU.add))
                    src, b = dst, 1 - b
                d = ub[2 + b]
                then(V.scalar_tensor_tensor(d[:, 8:8 + L], src[:, 8:8 + L], 1.0 / w, u[:, 8:8 + L], ALU.mult,
                                            ALU.subtract))
                at, left, right = edge_cols(g)
                then(V.tensor_tensor(stat[:, 32:32 + left], src[:, 8:8 + left], par[:, at:at + left], ALU.mult))
                if right:
                    then(V.tensor_tensor(stat[:, 40:40 + right], src[:, 8 + L - right:8 + L],
                                         par[:, at + left:at + left + right], ALU.mult))
                    then(V.tensor_tensor(d[:, 8 + L - right:8 + L], stat[:, 40:40 + right],
                                         u[:, 8 + L - right:8 + L], ALU.subtract))
                V.tensor_tensor(d[:, 8:8 + left], stat[:, 32:32 + left], u[:, 8:8 + left],
                                ALU.subtract).then_inc(pool_d, 1)
                dve.wait_ge(pool_hi, q + 1)
                dve.wait_ge(pool_d, q + 1)
                lo_of(dl[:, q % 2], d[:, 8:8 + L], dh[:, q % 2]).then_inc(pool_lo, 1)

            pool_tile(0)
            norm_invert(4)
            norm_diag(4)
            dve.wait_ge(nm_rbs, 5)
            split(3, lambda k: cqf[:, 3], lambda k: col("kv_norm"), lambda k: (ckh[:, 0], ckl[:, 0]))
            for q in range(1, KT):
                pool_tile(q)

            dve.sem_inc(tp_lo, 1)

            def project_dve(h, b, m0):
                def low(u, hi_n, hi_t, lo_t):
                    dve.wait_ge(ax_hi, 6 * h + hi_n)
                    f = slice((u % 2) * HALF, (u % 2 + 1) * HALF)
                    lo_of(lo_t[:, b, f], ps[:, 6 + u % 2], hi_t[:, b, f]).then_inc(aux_ev, 1)

                low(0, 1, qnh, qnl)
                low(1, 2, qnh, qnl)
                for f in range(2):
                    dve.wait_ge(aux_mm, m0 + 3 + f)
                    if not (isinstance(h, int) and h == 0):
                        dve.wait_ge(rope_lo, 2 * h)
                    V.tensor_tensor(rt[:, f], ps[:, 6 + f], trig_a[:, f * HALF:(f + 1) * HALF],
                                    ALU.mult).then_inc(aux_ev, 1)
                for f in range(2):
                    dve.wait_ge(rope_shift, 2 * h + f + 1)
                    dve.wait_ge(aux_ev, proj_unit(h) + 3 + f)
                    V.tensor_tensor(rf_t[:ROPE, f], rt[:ROPE, f], rs_t[:ROPE, f], ALU.add).then_inc(rope_sum, 1)
                low(4, 3, knh, knl)
                low(5, 4, knh, knl)
                for f in range(2):
                    dve.wait_ge(rope_hi, 2 * h + f + 1)
                    dve.wait_ge(rope_sum, 2 * h + f + 1)
                    at = slice(f * HALF, (f + 1) * HALF)
                    lo_of(qrl[:ROPE, b, at], rf_t[:ROPE, f], qrh[:ROPE, b, at]).then_inc(rope_lo, 1)
                low(6, 5, vvh, vvl)
                low(7, 6, vvh, vvl)

            def row_maximum(h, t):
                dve.wait_ge(sc_mm, 8 * h + t + 1)
                m, n = stat[:, 24 + t % 4:25 + t % 4], stat[:, 28 + t % 4:29 + t % 4]
                V.tensor_reduce(m, ps[:, 2 * (t % 2):2 * (t % 2) + 2].rearrange("p a n -> p (a n)"), AX_X,
                                ALU.max).then_inc(row_max, 1)
                dve.wait_ge(row_max, 8 * h + t + 1)
                V.tensor_scalar(n, m, -ATT_SCALE, None, ALU.mult).then_inc(row_bias, 1)

            def normalise(h, t):
                dve.wait_ge(exp_done, 8 * h + t + 3)
                r = stat[:, 52 + t % 4:53 + t % 4]
                V.reciprocal(r, stat[:, 48 + t % 4:49 + t % 4]).then_inc(sum_inv, 1)
                dve.wait_ge(sum_inv, 8 * h + t + 1)
                V.tensor_scalar(prob[:, t % 4], prob[:, t % 4], r, None, ALU.mult).then_inc(prob_ok, 1)

            def turned_lo(h, t):
                j = t // 2
                dve.wait_ge(tp_hi, 8 * h + t + 1)
                at = slice((t % 2) * P, (t % 2 + 1) * P)
                lo_of(ptl[:, j % 2, :, at], ps[:, 4:6].rearrange("p a (b n) -> p (a b) n", n=P),
                      pth[:, j % 2, :, at]).then_inc(tp_lo, 1)

            def bring_o(h, j, last_head):
                dve.wait_ge(aux_mm, pv_count(h, j, last_head))
                dve.wait_ge(o_out[j % 2], 16 * (2 * h + j // 2 + 1))
                V.tensor_copy(osb[:, j % 2], ps[:, 6 + j % 2, 0:256]).then_inc(aux_ev, 1)

            def head_dve(h, b, last_head=False):
                row_maximum(h, 0)
                row_maximum(h, 1)
                normalise(h, 0)
                for t in range(2, 8):
                    row_maximum(h, t)
                    normalise(h, t - 1)
                    if t in (4, 6):
                        bring_o(h, t // 2 - 2, last_head)
                    turned_lo(h, t - 2)
                normalise(h, 7)
                if not last_head:
                    project_dve(h + 1, 1 - b, 9 + 11 * h)
                bring_o(h, 2, last_head)
                turned_lo(h, 6)
                turned_lo(h, 7)
                bring_o(h, 3, last_head)

            project_dve(0, 0, 0)
            with dve.Fori(0, HEADS // 2 - 1) as i:
                head_dve(2 * i, 0)
                head_dve(2 * i + 1, 1)
            head_dve(HEADS - 2, 0)
            head_dve(HEADS - 1, 1, last_head=True)

            dve.wait_ge(tp_mm, 4 + 8 * HEADS)
            norm_diag(2)
            dve.wait_ge(nm_rbs, 6)
            dve.wait_ge(x_in, 32)
            for s in o_out:
                dve.wait_ge(s, 16 + 16 * 2 * HEADS)
            dve.wait_ge(aux_mm, pv_count(HEADS - 1, 3, True))
            split(4, lambda k: x[:, k], lambda k: col("a_norm", k), h_dst)

            def gate_dve(c, b, base, Tb, y_count):
                dve.wait_ge(y_in[b], y_count)
                for q in range(2):
                    T = 2 * c + q
                    dve.wait_ge(silu_done, Tb + T + 1)
                    dve.wait_ge(hid_lo, Tb + T)
                    V.tensor_tensor(yg[:], sg[:], ybuf[:, b, q], ALU.mult).then_inc(hid_done, 1)
                    dve.wait_ge(hid_hi, Tb + T + 1)
                    dve.wait_ge(hid_done, Tb + T + 1)
                    lo_of(hidl[:, b, q], yg[:], hidh[:, b, q]).then_inc(hid_lo, 1)

            def mix_dve(f, B):
                nonlocal dn_base
                Tb, dn_base = FFN_T + 16 * f, 8 * (FFN_T // 2 + N_MC * f)
                mb, y0 = 6 * (FFN_T // 2 + N_MC * f), 16 * (N_MC // 2) * f
                gate_dve(0, 0, B, Tb, y0 + 16)
                with dve.Fori(0, N_MC // 2 - 1) as i:
                    gate_dve(2 * i + 1, 1, B, Tb, y0 + 16 * i + 16)
                    add_down(2 * i, B + 4 + 8 * i, mb)
                    gate_dve(2 * i + 2, 0, B, Tb, y0 + 16 * i + 32)
                    add_down(2 * i + 1, B + 8 + 8 * i, mb)
                gate_dve(N_MC - 1, 1, B, Tb, y0 + 16 * (N_MC // 2))
                add_down(N_MC - 2, B + 4 * N_MC - 4, mb)
                add_down(N_MC - 1, B + 4 * N_MC - 2, mb,
                         square=lambda k: add_square(nb[5 + f] + k, k % 2, k == 0))

            mix_dve(0, B_A3)
            norm_invert(5)
            norm_diag(5)
            dve.wait_ge(nm_rbs, 7)
            dve.wait_ge(dn_ev, 2 + 8 * (FFN_T // 2 + N_MC))
            split(5, lambda k: x[:, k], lambda k: col("r_norm", k), h_dst)

            dve.wait_ge(pos_in, 32)
            V.tensor_copy(posf[:], posi[:]).then_inc(pos_float, 1)
            dve.wait_ge(pos_float, 2)
            angles(col("inv_r"), 0.25, float(np.pi / 2), 8)
            V.tensor_scalar(ang[:], ang[:], -PI_IN, None, ALU.max).then_inc(trig_step, 1)
            dve.wait_ge(trig_sin, 2)
            dve.wait_ge(trig_step, 16)
            angles(col("inv_r"), 0.0, 0.0, 16)
            V.tensor_scalar(ang[:], ang[:], -PI_IN, None, ALU.max).then_inc(trig_step, 1)

            g_abs, g_e, g_z, g_z2, g_p = [lgam[:, 8 * i:8 * i + 8] for i in range(5)]
            gstep = [0]

            def then(ins):
                ins.then_inc(gam_step, 1)
                gstep[0] += 1
                dve.wait_ge(gam_step, gstep[0])

            dec = col("decay", 0, 8)
            then(V.scalar_tensor_tensor(g_abs, dec, -1.0, dec, ALU.mult, ALU.max))
            dve.wait_ge(gam_exp, 1)
            then(V.tensor_scalar(g_p, g_e, 2.0, None, ALU.add))
            then(V.reciprocal(g_z, g_p))
            then(V.tensor_tensor(g_z, g_z, g_e, ALU.mult))
            then(V.tensor_tensor(g_z2, g_z, g_z, ALU.mult))
            then(V.tensor_scalar(g_p, g_z2, 1.0 / 19, None, ALU.mult))
            for n in range(17, 1, -2):
                then(V.scalar_tensor_tensor(g_p, g_p, 1.0 / n, g_z2, ALU.add, ALU.mult))
            then(V.scalar_tensor_tensor(g_p, g_p, 1.0, g_z, ALU.add, ALU.mult))
            then(V.tensor_scalar(g_abs, dec, 0.0, None, ALU.min))
            then(V.scalar_tensor_tensor(g_abs, g_p, -2.0, g_abs, ALU.mult, ALU.add))
            then(V.tensor_scalar(g_e, g_abs, -1.0, None, ALU.mult))
            dve.wait_ge(spilled, 32)
            dve.wait_ge(trig_sin, 3)

            def r_block(h, ib, j0, j1):
                for j in range(j0, j1 + 1):
                    n = 32 * h + 8 * ib + j
                    if j < j1:
                        s = ib * KT + j
                        dve.wait_ge(s_mm, n + 1)
                        if s >= 2:
                            dve.wait_ge(p_lo, n - 1)
                        at = ib * IB - j * P + L - P
                        V.scalar_tensor_tensor(rsm[:, j % 2], ps[:, s % 3, 0:IB], R_DK ** -0.5,
                                               mask[:, at:at + IB], ALU.mult, ALU.mult).then_inc(s_ev, 1)
                    if j > j0:
                        dve.wait_ge(p_hi, n)
                        dve.wait_ge(s_ev, n)
                        lo_of(rpl[:, j - 1], rsm[:, (j - 1) % 2], rph[:, j - 1]).then_inc(p_lo, 1)

            with dve.Fori(0, R_HEADS) as h:
                dve.wait_ge(diff_in, 16 * h + 16)
                V.tensor_scalar(mtmp[:], mask[:], lgam[:, bass.ds(h + 12, 1)], None, ALU.mult).then_inc(mask_step, 1)
                dve.wait_ge(mask_step, 2 * h + 1)
                V.scalar_tensor_tensor(mask[:], mask[:], lgam[:, bass.ds(h, 1)], mtmp[:], ALU.mult,
                                       ALU.min).then_inc(mask_step, 1)
                dve.wait_ge(mask_step, 2 * h + 2)
                for u in range(4):
                    hi_t, lo_t = ((rqh, rql), (rkh, rkl))[u // 2]
                    b0, f = 4 * (u // 2), u % 2
                    dve.wait_ge(w_used, B_R2 + 8 * h + 2 * (u // 2) + 2)
                    if u:
                        dve.wait_ge(r_lo, 8 * h + 2 * u)
                    tok = slice(f * HALF, (f + 1) * HALF)
                    x1, x2 = ps[:, b0 + f], ps[:, b0 + 2 + f]
                    V.tensor_tensor(rta[:, 0], x1, cos_r[:, tok], ALU.mult)
                    V.tensor_tensor(rta[:, 1], x2, sin_r[:, tok], ALU.mult)
                    V.tensor_tensor(rta[:, 2], x2, cos_r[:, tok], ALU.mult)
                    V.tensor_tensor(rta[:, 3], x1, sin_r[:, tok], ALU.mult).then_inc(r_ev, 1)
                    dve.wait_ge(r_ev, 4 * h + u + 1)
                    V.tensor_tensor(rta[:, 0], rta[:, 0], rta[:, 1], ALU.subtract).then_inc(r_sum, 1)
                    V.tensor_tensor(rta[:, 2], rta[:, 2], rta[:, 3], ALU.add).then_inc(r_sum, 1)
                    for m in range(2):
                        dve.wait_ge(r_hi, 8 * h + 2 * u + m + 1)
                        dve.wait_ge(r_sum, 8 * h + 2 * u + m + 1)
                        lo_of(lo_t[:, m, tok], rta[:, 2 * m], hi_t[:, m, tok]).then_inc(r_lo, 1)
                for t in range(KT + 1):
                    if t < KT:
                        dve.wait_ge(v_sum, 8 * h + t + 1)
                        V.tensor_scalar(stat[:, 32 + t:33 + t], stat[:, 8 + t:9 + t], -1.0 / R_DV, None,
                                        ALU.mult).then_inc(v_mean, 1)
                    if t:
                        dve.wait_ge(v_hi, 8 * h + t)
                        dve.wait_ge(v_mean, 8 * h + t)
                        V.scalar_tensor_tensor(vrl[:, t - 1], ps[:, t - 1], stat[:, 31 + t:32 + t],
                                               vrh[:, t - 1].bitcast(F32), ALU.add, ALU.subtract).then_inc(v_lo, 1)
                dve.wait_ge(mask_exp, h + 1)
                r_block(h, 0, 0, KT)
                for ib in range(R_BLOCKS):
                    if ib + 1 < R_BLOCKS:
                        r_block(h, ib + 1, 0, R_AHEAD)
                        r_block(h, ib + 1, R_AHEAD, KT)
                    for m in range(4):
                        n = 16 * h + 4 * ib + m
                        dve.wait_ge(o_sq, n + 1)
                        if m == 0:
                            V.tensor_copy(roa[:], rsq[:, 0]).then_inc(o_acc, 1)
                        else:
                            dve.wait_ge(o_acc, n)
                            V.tensor_tensor(roa[:], roa[:], rsq[:, m % 2], ALU.add).then_inc(o_acc, 1)
                    dve.wait_ge(var_std, 4 * h + ib + 1)
                    V.reciprocal(rinv[:], rstd[:]).then_inc(var_inv, 1)
                    dve.wait_ge(var_inv, 4 * h + ib + 1)
                    for m in range(4):
                        V.scalar_tensor_tensor(ro[:, m], ro[:, m], par[:, bass.ds(COL["gn"] + m + 4 * h, 1)], rinv[:],
                                               ALU.mult, ALU.mult).then_inc(o_normed, 1)
            dve.wait_ge(x_in, 48)
            mix_dve(1, B_R3)
            norm_invert(6)
            norm_diag(6)
            dve.wait_ge(nm_rbs, 8)
            dve.wait_ge(dn_ev, 2 + 8 * (FFN_T // 2 + 2 * N_MC))
            for k in range(KT):
                V.scalar_tensor_tensor(x[:, k], x[:, k], col("final", k), rb[:], ALU.mult,
                                       ALU.mult).then_inc(x3_done, 1)


def host_panels(a):
    pan = np.zeros((N_PANELS, P, D), np.float32)
    at = [0]

    def put(*parts):
        pan[at[0]] = np.concatenate(parts, axis=1)
        at[0] += 1

    def cols(w, c0, k0=0, kn=KT, width=P):
        return np.concatenate([w[(k0 + k) * P:(k0 + k + 1) * P, c0:c0 + width] for k in range(kn)], axis=1)

    def down(w, c):
        for d in range(2):
            put(*[cols(w, (4 * d + m) * P, 2 * c, 2) for m in range(4)])

    n = np.arange(L)
    turn = np.outer(n, np.arange(HALF)) % L
    cos = (np.cos(2 * np.pi * turn / L) / 512).astype(np.float32)
    sin = (np.sin(2 * np.pi * turn / L) / 512).astype(np.float32)
    sin[:, 0] = np.where(n % 2 == 0, 1.0, -1.0) / 512
    for _ in range(2):
        for t in range(KT):
            put(cos[t * P:(t + 1) * P], sin[t * P:(t + 1) * P])
    m = np.arange(FNET_C)
    turn = np.outer(m, m) % FNET_C
    cc = np.cos(2 * np.pi * turn / FNET_C).astype(np.float32)
    ss = np.sin(2 * np.pi * turn / FNET_C).astype(np.float32)
    put(*[cols(w, q * P, 0, 2) for w in (cc, ss) for q in range(2)])
    w = a["w_fnet_out"][0]
    for q in range(KT):
        put(cols(w, q * P))
    assert at[0] == B_FFN
    w, wd = a["w_ffn_up"][0], a["w_ffn_down"][0]

    def up(c):
        for q in range(2):
            put(cols(w, (2 * c + q) * P))
            put(cols(w, FFN + (2 * c + q) * P))

    up(0)
    for c in range(FFN_T // 2 - 1):
        up(c + 1)
        down(wd, c)
    down(wd, FFN_T // 2 - 1)
    assert at[0] == B_A1
    w = a["a_w_in_2"][0]
    o_kv, o_kr = Q_LORA, Q_LORA + KV_LORA
    o_u = o_kr + ROPE
    o_g = o_u + POOL_G * POOL_C
    for q in range(3):
        put(cols(w, q * P))
    put(cols(w, o_kv))
    kr = w[:, o_kr:o_kr + ROPE]
    put(cols(np.concatenate([kr, kr[:, 32:], kr[:, :32]], axis=1), 0))
    pw = a["a_pool_w_2"][0]

    def put_pool(g):
        put(cols(pw[g], 0, 0, 2), cols(pw[g], P, 0, 2), np.zeros((P, HALF), np.float32))

    for q in range(KT):
        put(cols(w, o_u + q * P))
        if q in (3, 5):
            put_pool((q - 3) // 2)
    put_pool(2)
    put_pool(3)
    assert at[0] == B_A2
    wq, wkv = a["a_w_uq_2"][0], a["a_w_ukv_2"][0]
    for h in range(HEADS):
        q = wq[:, h * 192:(h + 1) * 192]
        r = q[:, NOPE:]
        put(cols(q, 0, 0, 3), cols(np.concatenate([r, r[:, 32:], r[:, :32]], axis=1), 0, 0, 3),
            wkv[:, h * 256:(h + 1) * 256])
    assert at[0] == B_A3

    def mix(w_gate, w_out):
        def gate(c):
            for q in range(2):
                put(cols(w_gate, (2 * c + q) * P))

        gate(0)
        for c in range(MIX // P // 2 - 1):
            gate(c + 1)
            down(w_out, c)
        down(w_out, MIX // P // 2 - 1)

    mix(w[:, o_g:], a["a_w_out_2"][0])
    assert at[0] == B_R2
    w = a["r_w_in_2"][0]
    for h in range(R_HEADS):
        for o in (0, R_HEADS * R_DK):
            for q in range(2):
                put(cols(w, o + h * R_DK + q * P))
        v = w[:, 2 * R_HEADS * R_DK + h * R_DV:2 * R_HEADS * R_DK + (h + 1) * R_DV]
        for k in range(0, KT, 2):
            put(v[k * P:(k + 1) * P], v[(k + 1) * P:(k + 2) * P])
    assert at[0] == B_R3
    mix(w[:, 2 * R_HEADS * R_DK + R_HEADS * R_DV:], a["r_w_out_2"][0])
    assert at[0] == N_PANELS
    return pan


def host_params(a):
    t = np.zeros((P, N_COL), np.float32)

    def put(name, v, i=0):
        v = np.asarray(v, np.float32).reshape(-1, P).T
        t[:, COL[name] + i:COL[name] + i + v.shape[1]] = v

    put("c", a["c"][0])
    put("b_mod", a["b_mod"][0])
    put("g_mix", a["g_norm_mix"][0])
    put("g_ffn", a["g_norm_ffn"][0])
    put("conv", a["w_ffn_conv"][0].reshape(-1))
    put("b_conv", a["b_ffn_conv"][0])
    put("g_final1", a["g_final"])
    put("a_norm", a["a_norm_g_2"][0])
    put("q_norm", a["a_q_norm_g_2"][0])
    put("kv_norm", a["a_kv_norm_g_2"][0])
    put("pool_scale", a["a_pool_scale_2"][0])
    put("r_norm", a["r_norm_g_2"][0])
    put("gn", a["r_gn_g_2"][0])
    put("final", a["final_norm_g_2"])
    t[:, COL["decay"]:COL["decay"] + 4] = a["r_decay_fwd_2"]
    t[:, COL["decay"] + 4:COL["decay"] + 8] = a["r_decay_bwd_2"]
    f32 = np.float32
    inv_a = f32(1.0) / (10000.0 ** (np.arange(0, ROPE, 2) / ROPE)).astype(f32)
    inv_r = f32(1.0) / (10000.0 ** (np.arange(0, R_DK, 2) / R_DK)).astype(f32)
    t[:, COL["inv_a"]] = np.concatenate([inv_a, inv_a, -inv_a, inv_a])
    t[:64, COL["turn_a"]] = 0.25
    t[:64, COL["rad_a"]] = np.pi / 2
    t[:, COL["inv_r"]] = inv_r
    for g in range(POOL_G):
        at, left, right = edge_cols(g)
        n = np.concatenate([np.arange(left) + left, left * 2 - 1 - np.arange(right)])
        t[:, at:at + left + right] = (1.0 / n).astype(f32)
    return t


def kernel(**inputs):
    import concourse.bacc as bacc
    from concourse.bass_utils import run_bass_kernel_spmd

    a = {k: np.asarray(v) for k, v in inputs.items()}
    xm = a["x"][0]
    wm = a["w_mod"][0].reshape(KT, P, 16, 384).transpose(2, 1, 0, 3).reshape(16, P, KT * 384)
    arrays = {
        "xt": np.ascontiguousarray(xm.reshape(KT, P, D).transpose(1, 0, 2)),
        "xf": np.ascontiguousarray(xm.T.reshape(KT, P, L).transpose(1, 0, 2)),
        "panels": host_panels(a),
        "w_mod_chunks": np.ascontiguousarray(wm),
        "params": host_params(a),
        "positions": np.ascontiguousarray(np.broadcast_to(a["positions_2"].reshape(1, L), (P, L))),
        "ident_c": np.eye(P, dtype=np.float32),
        "diff_c": (np.arange(MASK_W)[None, :] - (L - P) - np.arange(P)[:, None]).astype(np.float32),
    }
    nc = bacc.Bacc("TRN2", target_bir_lowering=False, num_devices=1)
    args = [nc.dram_tensor(k, v.shape, mybir.dt.from_np(v.dtype), kind="ExternalInput").ap() for k, v in arrays.items()]
    out = nc.dram_tensor("out", (P, KT, L), F32, kind="ExternalOutput").ap()
    build(nc, *args, out)
    r = run_bass_kernel_spmd(nc, [arrays], core_ids=[0])
    y = r.results[0]["out"]
    return np.ascontiguousarray(y.transpose(1, 0, 2).reshape(D, L).T).reshape(1, L, D)
```

```python
from contextlib import ExitStack

import numpy as np

import concourse.bass as bass
from concourse import mybir

F32 = mybir.dt.float32
F32R = mybir.dt.float32r
I32 = mybir.dt.int32
ALU = mybir.AluOpType
ACT = mybir.ActivationFunctionType
AX_X = mybir.AxisListType.X

P = 128
D = 1024
L = 1024
KT = D // P
HALF = 512
EPS = 1e-6

FNET_G, FNET_C = 4, 256
FFN = 2816
FFN_T = FFN // P
Q_LORA, KV_LORA = 384, 128
HEADS, NOPE, ROPE, VDIM = 8, 128, 64, 128
ATT_SCALE = float((NOPE + ROPE) ** -0.5)
POOL_G, POOL_C = 4, 256
MIX = 2048
R_HEADS, R_DK, R_DV = 4, 256, 512
IB = 256
R_BLOCKS = L // IB
V_ORDER = (0, 1, 2, 3, 4, 6, 5, 7)
R_AHEAD = KT - 2
MASK_W = 2 * L - P

N_DFT, N_CDFT, N_FNET = 16, 1, KT
N_FFN = FFN_T // 2 * 6
N_A1 = 5 + KT + POOL_G
N_A2 = HEADS
N_MIX = MIX // P * 2
N_R2 = R_HEADS * 8
COUNTS = [N_DFT, N_CDFT, N_FNET, N_FFN, N_A1, N_A2, N_MIX, N_R2, N_MIX]
B_DFT, B_CDFT, B_FNET, B_FFN, B_A1, B_A2, B_A3, B_R2, B_R3, N_PANELS = [sum(COUNTS[:i]) for i in range(10)]

_COLS = [("c", KT), ("b_mod", 48), ("g_mix", KT), ("g_ffn", KT), ("conv", 3 * FFN_T), ("b_conv", FFN_T),
         ("g_final1", KT), ("a_norm", KT), ("q_norm", 3), ("kv_norm", 1), ("pool_scale", KT),
         ("r_norm", KT), ("gn", 16), ("final", KT), ("decay", 8),
         ("inv_a", 1), ("turn_a", 1), ("rad_a", 1), ("inv_r", 1), ("edge", 26)]
COL = {}
N_COL = 0
for _name, _n in _COLS:
    COL[_name] = N_COL
    N_COL += _n

TWO_PI = 2.0 * np.pi
C1 = 6.28125
C2 = float(np.float32(np.round((TWO_PI - C1) * 2.0 ** 21) / 2.0 ** 21))
C3 = float(np.float32(TWO_PI - C1 - C2))
ROUND = 1.5 * 2.0 ** 23
PI_IN = float(np.nextafter(np.float32(np.pi), np.float32(0)))

NORM_T = [KT, KT, KT, 3, 1, KT, KT]
NORM_N = [D, D, D, Q_LORA, KV_LORA, D, D]
SPLIT_T = [KT, KT, 3, 1, KT, KT]


def pool_window(g):
    return 2 << g


def pool_levels(g):
    out, lo, hi = [], 0, L
    for lv in range(g, -1, -1):
        a, b = (1, 0) if lv == 0 else (1 << (lv - 1), 1 << (lv - 1))
        out.append((a, b, lo, hi))
        lo, hi = lo - a, hi + b
    return out[::-1]


def edge_cols(g):
    at = COL["edge"] + sum(pool_window(q) - 1 for q in range(g))
    w = pool_window(g)
    return at, w // 2, w // 2 - 1


POOL_ORDER = (3, 2, 1, 0)


def pool_out(q):
    return (POOL_ORDER[q // 2] + 1) % 2


def build(nc, xt_d, x_d, pan_d, wm_d, par_d, pos_d, ident_d, diff_d, out_d):
    ctx = ExitStack()
    with ctx:
        def place(name, shape, dt, at):
            with ExitStack() as s:
                if at:
                    s.enter_context(nc.sbuf_tensor(f"under_{name}", [P, at // 4], F32))
                return s.enter_context(nc.sbuf_tensor(name, shape, dt))

        def sem(name):
            return ctx.enter_context(nc.semaphore(name))

        K = 1024
        stage = place("stage", [P, 2, D], F32, 0)
        wh = place("wh", [P, 2, D], F32R, 8 * K)
        wl = place("wl", [P, 2, D], F32R, 16 * K)
        x = place("x", [P, KT, L], F32, 24 * K)
        hh = place("hh", [P, KT, L], F32R, 56 * K)
        hl = place("hl", [P, KT, L], F32R, 88 * K)
        par = place("par", [P, N_COL], F32, 120 * K)
        modc = place("modc", [P, 48], F32, 120 * K + 1200)
        s1 = place("s1", [P, KT], F32, 120 * K + 1392)
        s2 = place("s2", [P, KT], F32, 120 * K + 1424)
        sh2x = place("sh2x", [P, KT], F32, 120 * K + 1456)
        silu_c = place("silu_c", [P, KT], F32, 120 * K + 1488)
        rr = place("rr", [P, 8, KT], F32, 120 * K + 1520)
        stat = place("stat", [P, 64], F32, 120 * K + 1776)
        lgam = place("lgam", [P, 40], F32, 120 * K + 2032)
        nothing = place("nothing", [P, 1], F32, 120 * K + 3232)
        ga = place("ga", [P, KT], F32, 120 * K + 3264)
        ident = place("ident", [P, P], F32, 120 * K + 2192)
        ones = place("ones", [P, P], F32, 120 * K + 2704)
        rb = place("rb", [P, L], F32, 124 * K)
        trig_a = place("trig_a", [P, L], F32, 128 * K)
        sqb = place("sqb", [P, 2, L], F32, 132 * K)
        nacc = place("nacc", [P, L], F32, 140 * K)
        diag = place("diag", [P, KT, P], F32, 144 * K)
        sqb0 = place("sqb0", [P, 2, L], F32, 188 * K)
        nacc0 = place("nacc0", [P, L], F32, 196 * K)
        sqb2 = place("sqb2", [P, 2, L], F32, 148 * K)
        nacc2 = place("nacc2", [P, L], F32, 156 * K)
        rb2 = place("rb2", [P, L], F32, 160 * K)
        tt = place("tt", [P, 2, L], F32, 148 * K)
        WMC = 384
        wm = place("wm", [P, 2, KT * WMC], F32, 124 * K)
        macc = place("macc", [P, 3 * D], F32, 148 * K)
        wm_b = place("wm_b", [P, 2, KT * WMC], F32, 132 * K)
        macc_b = place("macc_b", [P, 3 * D], F32, 156 * K)
        pq = place("pq", [P, 16, HALF], F32, 172 * K)
        pqh = place("pqh", [P, 2, 2, D], F32R, 124 * K)
        pql = place("pql", [P, 2, 2, D], F32R, 140 * K)
        zt = place("zt", [P, 2, L], F32, 156 * K)
        vs = place("vs", [P, HALF], F32, 164 * K)
        posi = place("posi", [P, L], I32, 172 * K)
        posf = place("posf", [P, L], F32, 176 * K)
        ang = place("ang", [P, L], F32, 180 * K)
        turns = place("turns", [P, L], F32, 203 * K + 512)
        hidh = place("hidh", [P, 2, 2, L], F32R, 164 * K)
        hidl = place("hidl", [P, 2, 2, L], F32R, 180 * K)
        gbuf = place("gbuf", [P, L + 2], F32, 132 * K)
        conv = place("conv", [P, L], F32, 137 * K)
        act_g = place("act_g", [P, L], F32, 141 * K)
        hid = place("hid", [P, L], F32, 145 * K)
        cqh = place("cqh", [P, 3, L], F32R, 24 * K)
        cql = place("cql", [P, 3, L], F32R, 36 * K)
        ckh = place("ckh", [P, 1, L], F32R, 48 * K)
        ckl = place("ckl", [P, 1, L], F32R, 52 * K)
        krh = place("krh", [P, L], F32R, 156 * K)
        krl = place("krl", [P, L], F32R, 160 * K)
        cqf = place("cqf", [P, 4, L], F32, 164 * K)
        dh = place("dh", [P, 2, L], F32R, 164 * K)
        dl = place("dl", [P, 2, L], F32R, 172 * K)
        dh_b = place("dh_b", [P, 2, L], F32R, 132 * K)
        dl_b = place("dl_b", [P, 2, L], F32R, 140 * K)
        d_hi, d_lo = (dh, dh_b), (dl, dl_b)
        PADW = L + 16
        ub = [place(f"ub{i}", [P, PADW], F32, 180 * K + i * 4160) for i in range(4)]
        kt_t = place("kt_t", [P, L], F32, 180 * K + 4 * 4160)
        ks_t = place("ks_t", [P, L], F32, 180 * K + 4 * 4160 + 4096)
        yp = place("yp", [P, 2, L], F32, 180 * K + 4 * 4160)
        qnh = place("qnh", [P, 2, L], F32R, 56 * K)
        qnl = place("qnl", [P, 2, L], F32R, 64 * K)
        qr = place("qr", [P, 2, L], F32R, 72 * K)
        knh = place("knh", [P, 2, L], F32R, 88 * K)
        knl = place("knl", [P, 2, L], F32R, 96 * K)
        vvh = place("vvh", [P, 2, L], F32R, 104 * K)
        vvl = place("vvl", [P, 2, L], F32R, 112 * K)
        prob = place("prob", [P, 4, L], F32, 132 * K)
        osb = place("osb", [P, 2, 256], F32, 205 * K)
        rt = place("rt", [P, 2, HALF], F32, 150 * K)
        pth = place("pth", [P, 2, KT, 256], F32R, 164 * K)
        ptl = place("ptl", [P, 2, KT, 256], F32R, 180 * K)
        rs_t = place("rs_t", [P, 2, HALF], F32, 196 * K)
        rf_t = place("rf_t", [P, 2, HALF], F32, 200 * K)
        ybuf = place("ybuf", [P, 2, 2, L], F32, 132 * K)
        sg = place("sg", [P, L], F32, 196 * K)
        yg = place("yg", [P, L], F32, 200 * K)
        vrh = place("vrh", [P, KT, R_DV], F32R, 24 * K)
        vrl = place("vrl", [P, KT, R_DV], F32R, 40 * K)
        rqh = place("rqh", [P, 2, L], F32R, 132 * K)
        rql = place("rql", [P, 2, L], F32R, 140 * K)
        rkh = place("rkh", [P, 2, L], F32R, 148 * K)
        rkl = place("rkl", [P, 2, L], F32R, 156 * K)
        rph = place("rph", [P, KT, IB], F32R, 164 * K)
        rpl = place("rpl", [P, KT, IB], F32R, 172 * K)
        cos_r = place("cos_r", [P, L], F32, 187 * K + 512)
        sin_r = place("sin_r", [P, L], F32, 191 * K + 512)
        mask = place("mask", [P, MASK_W], F32, 180 * K)
        rta = place("rta", [P, 4, HALF], F32, 195 * K + 512)
        mtmp = place("mtmp", [P, MASK_W], F32, 195 * K + 512)
        rsm = place("rsm", [P, 2, IB], F32, 124 * K)
        roa = place("roa", [P, IB], F32, 126 * K)
        rinv = place("rinv", [P, IB], F32, 127 * K)
        rsq = place("rsq", [P, 2, IB], F32, 128 * K)
        rstd = place("rstd", [P, IB], F32, 130 * K)
        ro = place("ro", [P, 4, IB], F32, 203 * K + 512)

        ps = ctx.enter_context(nc.psum_tensor("ps", [P, 8, HALF], F32))
        xs_d = nc.dram_tensor("x_spill", (P, KT, L), F32).ap()
        y_d = nc.dram_tensor("y_spill", (16, P, L), F32).ap()

        panel_in = [sem("panel_in0"), sem("panel_in1")]
        nothing_set, w_hi, w_ready, w_used = sem("nothing_set"), sem("w_hi"), sem("w_ready"), sem("w_used")
        wm_in = [sem("wm_in0"), sem("wm_in1")]
        xt_in = [sem(f"xt_in{i}") for i in range(4)]
        par_in, ident_in, x_in, pos_in = sem("par_in"), sem("ident_in"), sem("x_in"), sem("pos_in")
        ones_set, filled, c_ready = sem("ones_set"), sem("filled"), sem("c_ready")
        row_ss, row_std, row_inv, xh_done, xl_done = [sem(n) for n in ("row_ss", "row_std", "row_inv", "xh_done", "xl_done")]
        mod_step, pq_ev, mod_mm, mod_ready, mod_s = [sem(n) for n in ("mod_step", "pq_ev", "mod_mm", "mod_ready", "mod_s")]
        ga_set = sem("ga_set")
        pq_scaled, pq_hi, pq_lo, c_mm, v_copied, z_ev, z_hi, z_lo = [
            sem(n) for n in ("pq_scaled", "pq_hi", "pq_lo", "c_mm", "v_copied", "z_ev", "z_hi", "z_lo")]
        pos_float, trig_step, trig_sin = sem("pos_float"), sem("trig_step"), sem("trig_sin")
        fnet_ev = sem("fnet_ev")
        nm_sq, nm_acc, nm_ss, nm_std, nm_r, nm_dg, nm_rb, nm_rbs = [
            sem(n) for n in ("nm_sq", "nm_acc", "nm_ss", "nm_std", "nm_r", "nm_dg", "nm_rb", "nm_rbs")]
        sp_t, sp_hi, sp_lo = sem("sp_t"), sem("sp_hi"), sem("sp_lo")
        g_ev, cv_step, silu_done, hid_done, hid_hi, hid_lo, dn_mm, dn_ev = [
            sem(n) for n in ("g_ev", "cv_step", "silu_done", "hid_done", "hid_hi", "hid_lo", "dn_mm", "dn_ev")]
        x3_done, spilled = sem("x3_done"), sem("spilled")
        a_ev, pw_mm, kr_dve, kr_act, pool_step, pool_d, pool_hi, pool_lo = [
            sem(n) for n in ("a_ev", "pw_mm", "kr_dve", "kr_act", "pool_step", "pool_d", "pool_hi", "pool_lo")]
        yp_out = [sem("yp_out0"), sem("yp_out1")]
        aux_mm, aux_ev, ax_hi, rope_shift, rope_sum, rope_hi, rope_lo = [
            sem(n) for n in ("aux_mm", "aux_ev", "ax_hi", "rope_shift", "rope_sum", "rope_hi", "rope_lo")]
        sc_mm, row_max, row_bias, exp_done, sum_inv, prob_ok, tp_mm, tp_hi, tp_lo = [
            sem(n) for n in ("sc_mm", "row_max", "row_bias", "exp_done", "sum_inv", "prob_ok", "tp_mm", "tp_hi", "tp_lo")]
        o_out = [sem("o_out0"), sem("o_out1")]
        y_in = [sem("y_in0"), sem("y_in1")]
        diff_in, gam_step, gam_exp, mask_step, mask_exp = [
            sem(n) for n in ("diff_in", "gam_step", "gam_exp", "mask_step", "mask_exp")]
        r_ev, r_sum, r_hi, r_lo, v_mm, v_sum, v_mean, v_hi, v_lo = [
            sem(n) for n in ("r_ev", "r_sum", "r_hi", "r_lo", "v_mm", "v_sum", "v_mean", "v_hi", "v_lo")]
        s_mm, s_ev, p_hi, p_lo, o_mm, o_ev, o_sq, o_acc, var_mm, var_std, var_inv, o_normed, r_out = [
            sem(n) for n in ("s_mm", "s_ev", "p_hi", "p_lo", "o_mm", "o_ev", "o_sq", "o_acc", "var_mm", "var_std",
                             "var_inv", "o_normed", "r_out")]
        done = sem("done")
        block = ctx.enter_context(nc.Block())

        def col(name, i=0, n=1):
            return par[:, COL[name] + i:COL[name] + i + n]

        def slot_of(panel):
            return panel % 2

        @block.sync
        def _(sp):
            for n in range(B_FFN + 1):
                if n >= 2:
                    sp.wait_ge(w_ready, n - 1)
                sp.dma_start(stage[:, n % 2], pan_d[n]).then_inc(panel_in[n % 2], 16)
                if n < N_DFT and n % 2:
                    c, dst = n // 2, wm
                elif n >= B_FNET:
                    c, dst = 8 + n - B_FNET, wm_b
                else:
                    continue
                if c == 8:
                    sp.wait_ge(w_used, B_FNET)
                if c >= 2:
                    sp.wait_ge(mod_step, KT * (c - 1))
                if c < 16:
                    sp.dma_start(dst[:, c % 2], wm_d[c]).then_inc(wm_in[c % 2], 16)
            with sp.Fori((B_FFN + 1) // 2, N_PANELS // 2) as i:
                for j in range(2):
                    sp.wait_ge(w_ready, 2 * i + j - 1)
                    sp.dma_start(stage[:, j], pan_d[bass.ds(2 * i + j, 1)].rearrange("a p n -> p (a n)")
                                 ).then_inc(panel_in[j], 16)
            sp.wait_ge(done, 16 * KT)

        @block.gpsimd
        def _(pool):
            def split(n, j, landed):
                pool.wait_ge(panel_in[j], landed)
                nc.gpsimd.tensor_tensor(wh[:, j], stage[:, j], nothing[:].to_broadcast([P, D]), ALU.add).then_inc(w_hi, 1)
                pool.wait_ge(w_hi, n + 1)
                nc.gpsimd.tensor_tensor(wl[:, j], stage[:, j], wh[:, j].bitcast(F32),
                                        ALU.subtract).then_inc(w_ready, 1)

            nc.gpsimd.memset(nothing[:], 0.0).then_inc(nothing_set, 1)
            pool.wait_ge(nothing_set, 1)
            for j in range(2):
                split(j, j, 16)
            with pool.Fori(1, N_PANELS // 2) as i:
                for j in range(2):
                    pool.wait_ge(w_used, 2 * i + j - 1)
                    split(2 * i + j, j, 16 * i + 16)

        nb = [sum(NORM_T[:m]) for m in range(len(NORM_T))]
        sb = [sum(SPLIT_T[:q]) for q in range(len(SPLIT_T))]
        x_tiles = [x[:, k] for k in range(KT)]

        u_panel = [B_A1 + 5 + q + (q >= 6) for q in range(KT)]
        u_unit = [5 + q + 2 * (q >= 6) for q in range(KT)]
        pw_panel = [B_A1 + n for n in (11, 14, 15, 16)]
        pw_unit = [11, 15, 17, 19]

        UNITS_P = [1, 3, 4, 6, 7, 8, 10, 11]
        STEP_P = [[], [0], [1], [2], [3], [4, 5], [6], [7]]
        UNITS_O = [5, 9, 12, 14]

        def unit(h, i):
            if isinstance(h, int) and h == 0:
                return 6 + i + (i == 1)
            if isinstance(h, int) and h == HEADS - 1:
                return 12 * h + 6 + [0, 2, 5, 9, 12, 14].index(i)
            return 12 * h + 6 + i

        def unit_bank(h, i):
            return unit(h, i) % 2 if isinstance(h, int) and h == HEADS - 1 else i % 2

        def unit_mm(h, i):
            return unit(h, i) - h if isinstance(h, int) else 11 * h + 6 + i

        def pair_at(h, j):
            return (h, UNITS_O[j]) if j < 2 or (isinstance(h, int) and h == HEADS - 1) else (h + 1, UNITS_O[j] - 12)

        N_MC = MIX // P // 2

        @block.tensor
        def _(pe):
            def mm3(out, a_hi, a_lo, b_hi, b_lo, first, last):
                nc.tensor.matmul(out, a_hi, b_lo, start=first, stop=False)
                nc.tensor.matmul(out, a_lo, b_hi, start=False, stop=False)
                return nc.tensor.matmul(out, a_hi, b_hi, start=False, stop=last)

            def linear(slot, bank, rhs_hi, rhs_lo, tiles=KT, blk=0, width=P):
                for h in range(2):
                    for k in range(tiles):
                        c = (blk + k) * P
                        last = mm3(ps[:width, bank + h], wh[:, slot, c:c + width], wl[:, slot, c:c + width],
                                   rhs_hi(k)[:, h * HALF:(h + 1) * HALF], rhs_lo(k)[:, h * HALF:(h + 1) * HALF],
                                   k == 0, k == tiles - 1)
                return last

            def linear_early(panel, slot, bank):
                for h in range(2):
                    out, at = ps[:, bank + h], slice(h * HALF, (h + 1) * HALF)
                    for k in range(KT):
                        w = wh[:, slot, k * P:(k + 1) * P]
                        nc.tensor.matmul(out, w, hl[:, k, at], start=k == 0, stop=False)
                        nc.tensor.matmul(out, w, hh[:, k, at], start=False, stop=False)
                    if h == 0:
                        pe.wait_ge(w_ready, panel + 1)
                    for k in range(KT):
                        last = nc.tensor.matmul(out, wl[:, slot, k * P:(k + 1) * P], hh[:, k, at],
                                                start=False, stop=k == KT - 1)
                return last

            def norm_sums(m, src=(nacc,)):
                n = m + len(src) - 1
                pe.wait_ge(nm_acc, nb[n] + NORM_T[n])
                for i, acc in enumerate(src):
                    for t in range(KT):
                        last = nc.tensor.matmul(ps[:, 7, i * KT + t:i * KT + t + 1], acc[:, t * P:(t + 1) * P],
                                                ones[:, 0:1], start=True, stop=True)
                last.then_inc(nm_ss, len(src))

            def norm_spread(s):
                pe.wait_ge(nm_dg, KT * (s + 1))
                if s:
                    pe.wait_ge(nm_rbs, s)
                for t in range(KT):
                    last = nc.tensor.matmul(ps[:, 5 + t // 4, (t % 4) * P:(t % 4 + 1) * P], ones[:], diag[:, t],
                                            start=True, stop=True)
                last.then_inc(nm_rb, 1)

            def wait_split(q):
                pe.wait_ge(sp_lo, sb[q] + SPLIT_T[q])

            def linear_pair(q, slot0, bank0, bank1):
                for k in range(KT):
                    pe.wait_ge(sp_lo, sb[q] + k + 1)
                    for n, bank in enumerate((bank0, bank1)):
                        slot, c = (slot0 + n) % 2, k * P
                        for h in range(2):
                            at = slice(h * HALF, (h + 1) * HALF)
                            last = mm3(ps[:, bank + h], wh[:, slot, c:c + P], wl[:, slot, c:c + P],
                                       hh[:, k, at], hl[:, k, at], k == 0, k == KT - 1)
                        if k == KT - 1:
                            last.then_inc(w_used, 1)

            h_hi, h_lo = (lambda k: hh[:, k]), (lambda k: hl[:, k])

            for f0 in (0, 4):
                for t in range(KT):
                    n = f0 * 2 + t
                    pe.wait_ge(w_ready, n + 1)
                    if f0 == 0:
                        pe.wait_ge(xl_done, t + 1)
                    for f in range(4):
                        for c in range(2):
                            if f0 and t == 0:
                                pe.wait_ge(pq_ev, 2 * f + c + 1)
                            a = slice((f0 + f) * P, (f0 + f + 1) * P)
                            b = slice(c * HALF, (c + 1) * HALF)
                            last = mm3(ps[:, 2 * f + c], hh[:, t, a], hl[:, t, a], wh[:, n % 2, b], wl[:, n % 2, b],
                                       t == 0, t == KT - 1)
                    last.then_inc(w_used, 1)
            def mod_sums(half, bank, src):
                pe.wait_ge(mod_step, 8 * KT * (half + 1))
                for c in range(24):
                    last = nc.tensor.matmul(ps[:, bank, c:c + 1], src[:, c * P:(c + 1) * P], ones[:, 0:1],
                                            start=True, stop=True)
                last.then_inc(mod_mm, 1)

            pe.wait_ge(ones_set, 1)
            pe.wait_ge(pq_ev, 9)
            mod_sums(0, 0, macc)
            sc = slot_of(B_CDFT)
            pe.wait_ge(w_ready, B_CDFT + 1)
            for n in range(KT):
                g, m = n // 2, n % 2
                pe.wait_ge(pq_lo, 4 * g + 4)
                if n >= 3:
                    pe.wait_ge(z_ev, n - 2)
                if n == 0:
                    pe.wait_ge(mod_ready, 1)
                for c in range(2):
                    for k in range(2):
                        blk = slice((c * 4 + m * 2 + k) * P, (c * 4 + m * 2 + k + 1) * P)
                        mm3(ps[:, 2 * (n % 3) + c], wh[:, sc, blk], wl[:, sc, blk],
                            pqh[:, g % 2, k, c * HALF:(c + 1) * HALF], pql[:, g % 2, k, c * HALF:(c + 1) * HALF],
                            k == 0, k == 1)
                if n >= 2:
                    pe.wait_ge(z_ev, n - 1)
                for k in range(2):
                    blk = slice((m * 2 + k) * P, (m * 2 + k + 1) * P)
                    last = mm3(ps[:, 6 + n % 2, 0:2], wh[:, sc, blk], wl[:, sc, blk],
                               pqh[:, g % 2, k, HALF:HALF + 2], pql[:, g % 2, k, HALF:HALF + 2], k == 0, k == 1)
                last.then_inc(w_used if n == KT - 1 else c_mm, 1)
            pe.wait_ge(z_lo, KT)
            with pe.Fori(0, KT // 2) as i:
                for j in range(2):
                    pe.wait_ge(w_ready, B_FNET + 1 + 2 * i + j)
                    pe.wait_ge(fnet_ev, 2 * i + j + 1)
                    linear(slot_of(B_FNET + j), 2 * j, h_hi, h_lo).then_inc(w_used, 1)
            mod_sums(1, 4, macc_b)
            norm_sums(0, (nacc0,))
            norm_spread(0)
            def up(c, base, first=False):
                if first:
                    pe.wait_ge(w_ready, base + 2)
                    linear_pair(0, slot_of(B_FFN), 0, 2)
                for q in range(1 if first else 0, 2):
                    T = 2 * c + q
                    for v in range(2):
                        pe.wait_ge(w_hi, base + 2 * q + v + 1)
                        pe.wait_ge(hid_done if v else g_ev, T)
                        linear_early(base + 2 * q + v, slot_of(B_FFN + 2 * q + v), 2 * v).then_inc(w_used, 1)

            def down(c, par_c, base, slot0, Tb=0):
                pe.wait_ge(hid_lo, Tb + 2 * c + 2)
                for m in range(KT):
                    d, mm = m // 4, m % 4
                    if mm == 0:
                        pe.wait_ge(w_ready, base + d + 1)
                    pe.wait_ge(dn_ev, dn_base + 8 * c + m + 1)
                    last = linear((slot0 + d) % 2, 4 + 2 * (m % 2), lambda k: hidh[:, par_c, k],
                                  lambda k: hidl[:, par_c, k], tiles=2, blk=2 * mm)
                    last.then_inc(w_used if mm == 3 else dn_mm, 1)

            dn_base = 0
            up(0, B_FFN, first=True)
            with pe.Fori(0, FFN_T // 4) as i:
                for cc in range(2):
                    at = B_FFN + 4 + 12 * i + 6 * cc
                    up(2 * i + cc + 1, at)
                    down(2 * i + cc, cc, at + 4, slot_of(B_FFN))
            down(FFN_T // 2 - 1, 0, B_A1 - 2, slot_of(B_FFN))
            norm_sums(1, (nacc, nacc2))
            norm_spread(1)
            def a1_unit(n, panel, **kw):
                if n >= 2:
                    pe.wait_ge(a_ev, n - 1)
                return linear(slot_of(panel), 2 * (n % 2), **kw)

            def a1_panel(n, panel):
                pe.wait_ge(w_hi, panel + 1)
                pe.wait_ge(a_ev, n - 1)
                linear_early(panel, slot_of(panel), 2 * (n % 2)).then_inc(w_used, 1)

            def pool_mix(g):
                pe.wait_ge(w_ready, pw_panel[g] + 1)
                pe.wait_ge(pool_lo, 2 * g + 2)
                for m in range(2):
                    a1_unit(pw_unit[g] + m, pw_panel[g], rhs_hi=lambda k: d_hi[g % 2][:, k], rhs_lo=lambda k: d_lo[g % 2][:, k],
                            tiles=2, blk=2 * m).then_inc(w_used if m else pw_mm, 1)

            pe.wait_ge(w_ready, B_A1 + 2)
            linear_pair(1, slot_of(B_A1), 0, 2)
            a1_panel(2, B_A1 + 2)
            norm_spread(2)
            for n in range(3, 5):
                a1_panel(n, B_A1 + n)
            a1_panel(u_unit[0], u_panel[0])
            norm_sums(3, (nacc, tt[:, 0]))
            a1_panel(u_unit[1], u_panel[1])
            norm_spread(3)
            a1_panel(u_unit[2], u_panel[2])
            norm_spread(4)
            a1_panel(u_unit[3], u_panel[3])
            for q in range(4, KT):
                a1_panel(u_unit[q], u_panel[q])
                if q % 2:
                    pool_mix((q - 5) // 2)
            pool_mix(2)
            pool_mix(3)

            pe.sem_inc(tp_mm, 4)
            wait_split(3)
            pe.wait_ge(kr_dve, 3)
            pe.wait_ge(kr_act, 3)
            pe.wait_ge(nm_rbs, 5)
            pe.wait_ge(a_ev, 21)

            def project(u, b, bank):
                slot = slot_of(B_A2 + b)
                kind, f = u // 2, u % 2
                out = ps[:, 6 + bank]
                tok = slice(f * HALF, (f + 1) * HALF)
                if kind < 2:
                    for k in range(3):
                        c = slice((3 * kind + k) * P, (3 * kind + k + 1) * P)
                        last = mm3(out, wh[:, slot, c], wl[:, slot, c], cqh[:, k, tok], cql[:, k, tok],
                                   k == 0, k == 2)
                elif kind == 2:
                    c = slice(6 * P, 7 * P)
                    last = mm3(out, wh[:, slot, c], wl[:, slot, c], ckh[:, 0, tok], ckl[:, 0, tok], True, True)
                else:
                    c = slice(7 * P, 8 * P)
                    for t in range(4):
                        at = slice((4 * f + t) * P, (4 * f + t + 1) * P)
                        last = mm3(out[:, t * P:(t + 1) * P], ckh[:, 0, at], ckl[:, 0, at],
                                   wh[:, slot, c], wl[:, slot, c], True, True)
                last.then_inc(w_used if u == 7 else aux_mm, 1)

            def scores(h, b, t):
                pe.wait_ge(exp_done, 8 * h + t + 1)
                q = slice(t * P, (t + 1) * P)
                for f in range(2):
                    out = ps[:, 2 * (t % 2) + f]
                    key = slice(f * HALF, (f + 1) * HALF)
                    mm3(out, qnh[:, b, q], qnl[:, b, q], knh[:, b, key], knl[:, b, key], True, False)
                    nc.tensor.matmul(out, qr[:ROPE, b, q], krl[:ROPE, key], start=False, stop=False)
                    last = nc.tensor.matmul(out, qr[:, b, q], krh[:, key], start=False, stop=True)
                last.then_inc(sc_mm, 1)

            def turn_probs(h, t):
                pe.wait_ge(prob_ok, 8 * h + t + 1)
                pe.wait_ge(tp_lo, 8 * h + t + 1)
                for k in range(KT):
                    last = nc.tensor.transpose(ps[:, 4 + k // 4, (k % 4) * P:(k % 4 + 1) * P],
                                               prob[:, t % 4, k * P:(k + 1) * P], ident[:])
                last.then_inc(tp_mm, 1)

            def attend(h, b, j):
                at, i = pair_at(h, j)
                pe.wait_ge(tp_lo, 8 * h + 2 * j + 3)
                pe.wait_ge(aux_ev, unit(at, i) - 1)
                for k in range(KT):
                    v = slice(k * P, (k + 1) * P)
                    last = mm3(ps[:, 6 + unit_bank(at, i), 0:256], vvh[:, b, v], vvl[:, b, v],
                               pth[:, j % 2, k], ptl[:, j % 2, k], k == 0, k == KT - 1)
                last.then_inc(aux_mm, 1)

            def head(h, b, first=False, last_head=False):
                pe.wait_ge(rope_lo, 2 * h + 2)
                pe.wait_ge(aux_ev, 6 if first else 12 * h + 4)
                for t in range(KT):
                    scores(h, b, t)
                    if t in (0, 2) and not first:
                        attend(h - 1, 1 - b, 2 + t // 2)
                    if t == 4:
                        pe.wait_ge(aux_ev, 8 if first else 12 * h + 6)
                    if t in (4, 6):
                        attend(h, b, t // 2 - 2)
                    if t >= 2:
                        turn_probs(h, t - 2)
                    elif not first:
                        turn_probs(h - 1, t + 6)
                    if not last_head:
                        for u in STEP_P[t]:
                            if u == 0:
                                pe.wait_ge(w_ready, B_A2 + 2 + h)
                            n = unit(h, UNITS_P[u])
                            pe.wait_ge(aux_ev, n if first and u < 2 else n - 1)
                            project(u, 1 - b, UNITS_P[u] % 2)
                if last_head:
                    turn_probs(h, 6)
                    attend(h, b, 2)
                    turn_probs(h, 7)
                    attend(h, b, 3)

            pe.wait_ge(w_ready, B_A2 + 1)
            for u in range(8):
                if u >= 2:
                    pe.wait_ge(aux_ev, u - 1)
                project(u, 0, u % 2)
            head(0, 0, first=True)
            with pe.Fori(0, HEADS // 2 - 1) as i:
                head(2 * i + 1, 1)
                head(2 * i + 2, 0)
            head(HEADS - 1, 1, last_head=True)

            def gate(c, base, Tb):
                for q in range(2):
                    pe.wait_ge(w_hi, base + q + 1)
                    pe.wait_ge(silu_done, Tb + 2 * c + q - 1)
                    linear_early(base + q, q, 2 * q).then_inc(w_used, 1)

            def mix(f, B):
                nonlocal dn_base
                Tb, dn_base = FFN_T + 16 * f, 8 * (FFN_T // 2 + N_MC * f)
                pe.wait_ge(w_ready, B + 2)
                linear_pair(4 + f, 0, 0, 2)
                with pe.Fori(0, N_MC // 2 - 1) as i:
                    for cc in range(2):
                        c = 2 * i + cc
                        gate(c + 1, B + 2 + 4 * c, Tb)
                        down(c, cc, B + 4 + 4 * c, 0, Tb)
                gate(N_MC - 1, B + 4 * N_MC - 6, Tb)
                down(N_MC - 2, 0, B + 4 * N_MC - 4, 0, Tb)
                down(N_MC - 1, 1, B + 4 * N_MC - 2, 0, Tb)

            pe.wait_ge(aux_ev, unit(HEADS - 1, 12) + 1)
            pe.wait_ge(tp_lo, 1 + 8 * HEADS)
            norm_spread(5)
            pe.wait_ge(aux_ev, unit(HEADS - 1, 14) + 1)
            mix(0, B_A3)
            norm_sums(5)
            norm_spread(6)
            pe.wait_ge(nm_rbs, 7)

            def r_scores(h, ib, j):
                q = slice(ib * IB, (ib + 1) * IB)
                s = ib * KT + j
                if s < 3:
                    pe.wait_ge(v_lo, 8 * h + s + 1)
                else:
                    pe.wait_ge(s_ev, 32 * h + s - 2)
                key = slice(j * P, (j + 1) * P)
                for k in range(2):
                    last = mm3(ps[:, s % 3, 0:IB], rkh[:, k, key], rkl[:, k, key], rqh[:, k, q], rql[:, k, q],
                               k == 0, k == 1)
                last.then_inc(s_mm, 1)

            def r_values(h, ib, j):
                if j == 0:
                    if ib == 0:
                        pe.wait_ge(v_lo, 8 * h + 8)
                    else:
                        pe.wait_ge(o_ev, 16 * h + 4 * ib)
                pe.wait_ge(p_lo, 32 * h + 8 * ib + j + 1)
                for m in range(4):
                    v = slice(m * P, (m + 1) * P)
                    last = mm3(ps[:, 4 + m, 0:IB], vrh[:, j, v], vrl[:, j, v], rph[:, j], rpl[:, j],
                               j == 0, j == KT - 1)
                last.then_inc(o_mm, 1)

            def r_variance(h, ib):
                pe.wait_ge(o_acc, 16 * h + 4 * ib + 4)
                nc.tensor.matmul(ps[:, 3, 0:IB], ones[:], roa[:], start=True, stop=True).then_inc(var_mm, 1)

            def r_head(h, last_head=False):
                base = B_R2 + 8 * h
                for n in range(2, 4):
                    pe.wait_ge(w_hi, base + n + 1)
                    linear_early(base + n, n % 2, 2 * n).then_inc(w_used, 1)
                for n in range(4):
                    pe.wait_ge(w_ready, base + 4 + n + 1)
                    for t in V_ORDER:
                        if n == 0:
                            pe.wait_ge(r_ev, 4 * h + (2 if t < 4 else 3 + t % 2))
                        tok = slice(t * P, (t + 1) * P)
                        for kk in range(2):
                            c = slice(kk * R_DV, (kk + 1) * R_DV)
                            last = mm3(ps[:, t], hh[:, 2 * n + kk, tok], hl[:, 2 * n + kk, tok],
                                       wh[:, n % 2, c], wl[:, n % 2, c], n + kk == 0, n + kk == 4)
                        if n == 3 and t != 7:
                            last.then_inc(v_mm, 1)
                    last.then_inc(w_used, 1)
                pe.wait_ge(r_lo, 8 * h + 8)
                for j in range(KT):
                    r_scores(h, 0, j)
                for ib in range(R_BLOCKS):
                    for j in range(KT):
                        r_values(h, ib, j)
                        if ib + 1 < R_BLOCKS and j < R_AHEAD:
                            r_scores(h, ib + 1, j)
                        if ib and j == 1:
                            r_variance(h, ib - 1)
                    if ib + 1 < R_BLOCKS:
                        for j in range(R_AHEAD, KT):
                            r_scores(h, ib + 1, j)
                pe.wait_ge(s_ev, 32 * h + 32)
                if not last_head:
                    pe.wait_ge(w_hi, base + 9)
                    linear_early(base + 8, 0, 0).then_inc(w_used, 1)
                r_variance(h, R_BLOCKS - 1)
                pe.wait_ge(var_std, 4 * h + 4)
                if not last_head:
                    pe.wait_ge(w_hi, base + 10)
                    linear_early(base + 9, 1, 2).then_inc(w_used, 1)
                pe.wait_ge(o_ev, 16 * h + 16)

            pe.wait_ge(w_ready, B_R2 + 2)
            linear_pair(5, 0, 0, 2)
            with pe.Fori(0, R_HEADS - 1) as h:
                r_head(h)
            r_head(R_HEADS - 1, last_head=True)
            mix(1, B_R3)
            norm_sums(6)
            norm_spread(7)

        @block.scalar
        def _(act):
            def copy(out, in_, **kw):
                return nc.scalar.activation(out, in_, ACT.Copy, **kw)

            def norm_squares(m, src, buf=sqb, made=None, made_from=0):
                for k in range(NORM_T[m]):
                    if made is not None:
                        act.wait_ge(made, made_from + k + 1)
                    if k >= 2:
                        act.wait_ge(nm_acc, nb[m] + k - 1)
                    nc.scalar.activation(buf[:, k % 2], src[k], ACT.Square).then_inc(nm_sq, 1)

            def norm_std(m, at=0):
                act.wait_ge(nm_ss, m + 1)
                nc.scalar.activation(stat[:, at:at + KT], ps[:, 7, at:at + KT], ACT.Sqrt, bias=stat[:, 60:61],
                                     scale=1.0 / NORM_N[m]).then_inc(nm_std, 1)

            def norm_bring(s, dst=rb):
                act.wait_ge(nm_rb, s + 1)
                copy(dst[:].rearrange("p (a n) -> p a n", a=2), ps[:, 5:7]).then_inc(nm_rbs, 1)

            def split_hi(q, dst, shift=None):
                for k in range(SPLIT_T[q]):
                    act.wait_ge(sp_t, sb[q] + k + 1)
                    if shift is None:
                        copy(dst(k), tt[:, k % 2]).then_inc(sp_hi, 1)
                    else:
                        nc.scalar.activation(dst(k), tt[:, k % 2], ACT.Identity, bias=shift(k)).then_inc(sp_hi, 1)

            h_dst = lambda k: hh[:, k]

            act.dma_start(par[:], par_d).then_inc(par_in, 16)
            for i in range(4):
                act.dma_start(x[:, 2 * i:2 * i + 2], xt_d[:, 2 * i:2 * i + 2]).then_inc(xt_in[i], 16)
            act.dma_start(ident[:], ident_d).then_inc(ident_in, 16)
            act.wait_ge(par_in, 16)
            nc.scalar.activation(silu_c[:], col("c", 0, KT), ACT.Silu).then_inc(c_ready, 1)
            act.wait_ge(filled, 1)
            for i in range(KT // 2):
                act.wait_ge(xt_in[i], 16)
                for t in (2 * i, 2 * i + 1):
                    if t >= 2:
                        act.wait_ge(row_ss, t - 1)
                    nc.scalar.activation(pq[:, 2 * (t % 2):2 * (t % 2) + 2].rearrange("p a n -> p (a n)"), x[:, t],
                                         ACT.Square, accum_out=stat[:, 8 + t:9 + t]).then_inc(row_ss, 1)
                act.wait_ge(row_ss, 2 * i + 2)
                nc.scalar.activation(stat[:, 16 + 2 * i:18 + 2 * i], stat[:, 8 + 2 * i:10 + 2 * i], ACT.Sqrt,
                                     bias=stat[:, 60:61], scale=1.0 / D).then_inc(row_std, 1)
                act.wait_ge(row_inv, i + 1)
                for t in (2 * i, 2 * i + 1):
                    copy(hh[:, t], x[:, t], scale=rr[:, 7, t:t + 1]).then_inc(xh_done, 1)
            for f0 in (0, 4):
                act.wait_ge(w_used, 2 * f0 + KT)
                for f in range(4):
                    for c in range(2):
                        copy(pq[:, 2 * (f0 + f) + c], ps[:, 2 * f + c]).then_inc(pq_ev, 1)

            act.wait_ge(xl_done, KT)
            act.dma_start(x[:], x_d).then_inc(x_in, 16)

            def pq_split(f):
                act.wait_ge(pq_scaled, 2 * (f // 4) + 2)
                if f >= 4:
                    act.wait_ge(c_mm, 2 * (f // 2) - 2)
                dst = pqh[:, f // 2 % 2, f % 2]
                copy(dst, pq[:, 2 * f:2 * f + 2].rearrange("p a n -> p (a n)"), scale=s1[:, f:f + 1]).then_inc(pq_hi, 1)
                act.wait_ge(pq_hi, 2 * f + 1)
                copy(dst[:, 0:1], stat[:, 24 + f:25 + f]).then_inc(pq_hi, 1)

            def v_copy(n):
                if n == KT - 1:
                    act.wait_ge(w_used, B_CDFT + 1)
                else:
                    act.wait_ge(c_mm, n + 1)
                if n >= 1:
                    act.wait_ge(z_ev, n)
                copy(vs[:], ps[:, 2 * (n % 3) + 1]).then_inc(v_copied, 1)

            def z_hi_copy(n):
                act.wait_ge(z_ev, n + 1)
                copy(hh[:, n], zt[:, n % 2]).then_inc(z_hi, 1)

            act.wait_ge(pq_ev, 16)
            for f in range(2):
                pq_split(f)
            for g in range(4):
                if g < 3:
                    pq_split(2 * g + 2)
                    pq_split(2 * g + 3)
                for n in (2 * g, 2 * g + 1):
                    v_copy(n)
                    if n:
                        z_hi_copy(n - 1)
            z_hi_copy(KT - 1)
            act.wait_ge(z_lo, KT)
            act.dma_start(posi[:], pos_d).then_inc(pos_in, 16)
            act.wait_ge(trig_step, 8)
            nc.scalar.activation(trig_a[:], ang[:], ACT.Sin).then_inc(trig_sin, 1)

            norm_squares(0, x_tiles, sqb0, fnet_ev, 2)
            norm_std(0)
            norm_bring(0)
            split_hi(0, h_dst, lambda k: modc[:, 24 + k:25 + k])

            act.wait_ge(filled, 2)

            def ffn_act(c, base, first=False):
                for q in range(2):
                    T = 2 * c + q
                    act.wait_ge(w_used, base + 2 * q + 1)
                    if not (first and q == 0):
                        act.wait_ge(cv_step, 3 * T)
                    copy(gbuf[:, 1:L + 1].rearrange("p (a n) -> p a n", a=2), ps[:, 0:2]).then_inc(g_ev, 1)
                    act.wait_ge(cv_step, 3 * T + 3)
                    nc.scalar.activation(act_g[:], conv[:], ACT.Silu).then_inc(silu_done, 1)
                    act.wait_ge(hid_done, T + 1)
                    yield T, q

            def ffn_hi(T, q, par_c):
                copy(hidh[:, par_c, q], hid[:]).then_inc(hid_hi, 1)

            for T, q in ffn_act(0, B_FFN, first=True):
                ffn_hi(T, q, 0)
            for T, q in ffn_act(1, B_FFN + 4):
                ffn_hi(T, q, 1)
            with act.Fori(1, FFN_T // 4) as i:
                for cc in range(2):
                    at = B_FFN - 2 + 12 * i + 6 * cc
                    for T, q in ffn_act(2 * i + cc, at):
                        act.wait_ge(w_used, at)
                        ffn_hi(T, q, cc)
            at = B_FFN - 2 + 6 * (FFN_T // 2 - 1)
            for T, q in ffn_act(FFN_T // 2 - 1, at):
                act.wait_ge(w_used, at)
                ffn_hi(T, q, 0)
            for k in range(KT):
                act.wait_ge(dn_ev, 2 + 8 * (FFN_T // 2 - 1) + k + 1)
                if k >= 2:
                    act.wait_ge(nm_acc, nb[1] + 2 * k - 3)
                nc.scalar.activation(sqb[:, k % 2], x[:, k], ACT.Square).then_inc(nm_sq, 1)
                if k >= 2:
                    act.wait_ge(nm_acc, nb[1] + 2 * k - 2)
                nc.scalar.activation(sqb2[:, k % 2], x[:, k], ACT.Square, scale=col("g_final1", k)).then_inc(nm_sq, 1)
            norm_std(1)
            act.wait_ge(ga_set, 3)
            act.wait_ge(nm_r, 2)
            nc.scalar.activation(stat[:, 0:KT], stat[:, 8:8 + KT], ACT.Sqrt, bias=stat[:, 60:61],
                                 scale=1.0 / D).then_inc(nm_std, 1)
            norm_bring(1)
            split_hi(1, h_dst)

            def bring(n, panel, out, **kw):
                act.wait_ge(w_used, panel + 1)
                copy(out.rearrange("p (a n) -> p a n", a=2), ps[:, 2 * (n % 2):2 * (n % 2) + 2], **kw).then_inc(a_ev, 1)

            def bring_u(q):
                if q >= 2:
                    act.wait_ge(pool_lo, q - 1)
                bring(u_unit[q], u_panel[q], ub[q % 2][:, 8:8 + L])

            def pool_hi_copy(q):
                act.wait_ge(pool_d, q + 1)
                if q >= 4:
                    act.wait_ge(w_used, pw_panel[q // 2 - 2] + 1)
                copy(d_hi[q // 2 % 2][:, q % 2], ub[2 + pool_out(q)][:, 8:8 + L]).then_inc(pool_hi, 1)

            def pool_store(g):
                for m in range(2):
                    if m == 0:
                        act.wait_ge(pw_mm, g + 1)
                    if g:
                        act.wait_ge(yp_out[m], 16 * g)
                    bring(pw_unit[g] + m, pw_panel[g] + m - 1, yp[:, m], scale=col("pool_scale", 2 * POOL_ORDER[g] + m))
                    act.wait_ge(a_ev, pw_unit[g] + m + 1)
                    act.dma_start(y_d[8 + 2 * POOL_ORDER[g] + m], yp[:, m]).then_inc(yp_out[m], 16)

            for n in range(2):
                bring(n, B_A1 + n, cqf[:, n])
            norm_bring(2, rb2)
            for n in range(2, 4):
                bring(n, B_A1 + n, cqf[:, n])
            act.wait_ge(x3_done, KT)
            act.dma_start(xs_d, x[:]).then_inc(spilled, 16)
            bring(4, B_A1 + 4, kt_t[:])
            act.wait_ge(spilled, 16)
            act.wait_ge(a_ev, 4)
            norm_squares(3, [cqf[:, k] for k in range(3)])
            act.wait_ge(nm_acc, nb[4])
            norm_squares(4, [cqf[:, 3]])
            act.wait_ge(kr_dve, 1)
            copy(ks_t[:ROPE], kt_t[ROPE:]).then_inc(kr_act, 1)
            act.wait_ge(kr_dve, 2)
            copy(krh[:ROPE], kt_t[:ROPE]).then_inc(kr_act, 1)
            copy(krh[ROPE:], kt_t[:ROPE]).then_inc(kr_act, 1)
            act.wait_ge(filled, 3)
            bring_u(0)
            norm_std(3)
            norm_std(4, KT)
            bring_u(1)
            norm_bring(3)
            split_hi(2, lambda k: cqh[:, k])
            pool_hi_copy(0)
            bring_u(2)
            norm_bring(4)
            split_hi(3, lambda k: ckh[:, 0])
            pool_hi_copy(1)
            bring_u(3)
            for q in range(4, KT):
                pool_hi_copy(q - 2)
                bring_u(q)
                if q % 2:
                    pool_store((q - 5) // 2)
            pool_hi_copy(6)
            pool_store(2)
            pool_hi_copy(7)
            pool_store(3)

            act.sem_inc(exp_done, 2)
            for s in o_out:
                act.sem_inc(s, 16)

            def project_hi(h, u, b, bank, n_mm):
                if u == 7:
                    act.wait_ge(w_used, B_A2 + 1 + h)
                else:
                    act.wait_ge(aux_mm, n_mm)
                dst = (qnh, None, knh, vvh)[u // 2]
                copy(dst[:, b, (u % 2) * HALF:(u % 2 + 1) * HALF], ps[:, 6 + bank]).then_inc(ax_hi, 1)

            def rope_move(f, n_ev):
                act.wait_ge(aux_ev, n_ev)
                copy(rs_t[:ROPE, f], rt[ROPE:, f]).then_inc(rope_shift, 1)

            def rope_hi_copy(h, f, b):
                act.wait_ge(rope_sum, 2 * h + f + 1)
                copy(qr[:ROPE, b, f * HALF:(f + 1) * HALF], rf_t[:ROPE, f]).then_inc(rope_hi, 1)

            def exp_row(h, t):
                act.wait_ge(row_bias, 8 * h + t + 1)
                act.wait_ge(tp_mm, 8 * h + t + 1)
                nc.scalar.activation(prob[:, t % 4].rearrange("p (a n) -> p a n", a=2),
                                     ps[:, 2 * (t % 2):2 * (t % 2) + 2], ACT.Exp, bias=stat[:, 28 + t % 4:29 + t % 4],
                                     scale=ATT_SCALE, accum_out=stat[:, 48 + t % 4:49 + t % 4]).then_inc(exp_done, 1)

            def turned_hi(h, t):
                j = t // 2
                act.wait_ge(tp_mm, 8 * h + t + 5)
                if not (isinstance(h, int) and h == 0 and j < 2):
                    act.wait_ge(aux_mm, unit_mm(*(pair_at(h, j - 2) if j >= 2 else (h, 2 * j))))
                copy(pth[:, j % 2, :, (t % 2) * P:(t % 2 + 1) * P],
                     ps[:, 4:6].rearrange("p a (b n) -> p (a b) n", n=P)).then_inc(tp_hi, 1)

            def store_o(h, j):
                act.wait_ge(aux_ev, unit(*pair_at(h, j)) + 1)
                dst = y_d[h] if isinstance(h, int) else y_d[bass.ds(h, 1)].rearrange("a p n -> p (a n)")
                act.dma_start(dst[:, j * 256:(j + 1) * 256], osb[:, j % 2]).then_inc(o_out[j % 2], 16)

            def head_act(h, b, first=False, last_head=False):
                for t in range(KT):
                    exp_row(h, t)
                    if t >= 2:
                        turned_hi(h, t - 2)
                    elif not first:
                        turned_hi(h - 1, t + 6)
                    if not last_head:
                        if t == 3:
                            rope_move(0, unit(h, UNITS_P[2]) + 1)
                        if t == 4:
                            rope_move(1, unit(h, UNITS_P[3]) + 1)
                            rope_hi_copy(h + 1, 0, 1 - b)
                        for u in STEP_P[t]:
                            if u not in (2, 3):
                                i = UNITS_P[u]
                                project_hi(h + 1, u, 1 - b, i % 2, unit_mm(h, i))
                        if t == 5:
                            rope_hi_copy(h + 1, 1, 1 - b)
                    if t in (1, 3) and not first:
                        store_o(h - 1, 2 + t // 2)
                    if t in (5, 7):
                        store_o(h, t // 2 - 2)
                if last_head:
                    turned_hi(h, 6)
                    store_o(h, 2)
                    turned_hi(h, 7)
                    norm_bring(5)
                    store_o(h, 3)

            for s in yp_out:
                act.wait_ge(s, 16 * POOL_G)
            for u in (0, 1):
                project_hi(0, u, 0, u, u + 1)
            rope_move(0, 3)
            rope_move(1, 4)
            project_hi(0, 4, 0, 0, 5)
            rope_hi_copy(0, 0, 0)
            project_hi(0, 5, 0, 1, 6)
            rope_hi_copy(0, 1, 0)
            for u in (6, 7):
                project_hi(0, u, 0, u - 6, u + 1)
            head_act(0, 0, first=True)
            with act.Fori(0, HEADS // 2 - 1) as i:
                head_act(2 * i + 1, 1)
                head_act(2 * i + 2, 0)
            act.wait_ge(w_used, B_A3)
            act.dma_start(x[:], xs_d).then_inc(x_in, 16)
            head_act(HEADS - 1, 1, last_head=True)

            split_hi(4, h_dst)
            act.wait_ge(gam_step, 1)
            nc.scalar.activation(lgam[:, 8:16], lgam[:, 0:8], ACT.Exp, scale=-1.0).then_inc(gam_exp, 1)
            for s in o_out:
                act.wait_ge(s, 16 + 16 * 2 * HEADS)
            for s in yp_out:
                act.wait_ge(s, 16 * POOL_G)

            def gate_act(c, b, base, Tb, used=None):
                if used is not None:
                    act.wait_ge(hid_done, Tb + 2 * c - 2)
                src = y_d[2 * c:2 * c + 2] if isinstance(c, int) else y_d[bass.ds(2 * c, 2)]
                act.dma_start(ybuf[:, b], src.rearrange("a p n -> p a n")).then_inc(y_in[b], 16)
                for q in range(2):
                    T = 2 * c + q
                    act.wait_ge(w_used, base + q + 1)
                    act.wait_ge(hid_done, Tb + T)
                    nc.scalar.activation(sg[:].rearrange("p (a n) -> p a n", a=2), ps[:, 2 * q:2 * q + 2],
                                         ACT.Silu).then_inc(silu_done, 1)
                    act.wait_ge(hid_done, Tb + T + 1)
                    if used is not None:
                        act.wait_ge(w_used, used)
                    copy(hidh[:, b, q], yg[:]).then_inc(hid_hi, 1)

            def mix_act(f, B):
                Tb = FFN_T + 16 * f
                gate_act(0, 0, B, Tb)
                gate_act(1, 1, B + 2, Tb)
                with act.Fori(1, N_MC // 2) as i:
                    for cc in range(2):
                        at = B - 2 + 8 * i + 4 * cc
                        gate_act(2 * i + cc, cc, at, Tb, used=at)

            def x_made(f):
                return dict(made=dn_ev, made_from=2 + 8 * (FFN_T // 2 + N_MC * (f + 1) - 1))

            mix_act(0, B_A3)
            norm_squares(5, x_tiles, **x_made(0))
            act.wait_ge(dn_ev, 2 + 8 * (FFN_T // 2 + N_MC))
            act.dma_start(posi[:], pos_d).then_inc(pos_in, 16)
            act.dma_start(xs_d, x[:]).then_inc(spilled, 16)
            norm_std(5)
            norm_bring(6)
            split_hi(5, h_dst)

            act.wait_ge(trig_step, 16)
            nc.scalar.activation(cos_r[:], ang[:], ACT.Sin).then_inc(trig_sin, 1)
            act.wait_ge(trig_step, 24)
            nc.scalar.activation(sin_r[:], ang[:], ACT.Sin).then_inc(trig_sin, 1)
            act.wait_ge(spilled, 32)

            def r_probs_hi(h, ib, j):
                if ib:
                    act.wait_ge(o_mm, 32 * h + 8 * (ib - 1) + j + 1)
                act.wait_ge(s_ev, 32 * h + 8 * ib + j + 1)
                copy(rph[:, j], rsm[:, j % 2]).then_inc(p_hi, 1)

            def r_head_act(h, last_head=False):
                base = B_R2 + 8 * h
                for u in range(4):
                    dst, f = (rqh, rkh)[u // 2], u % 2
                    for m in range(2):
                        act.wait_ge(r_sum, 8 * h + 2 * u + m + 1)
                        copy(dst[:, m, f * HALF:(f + 1) * HALF], rta[:, 2 * m]).then_inc(r_hi, 1)
                act.wait_ge(mask_step, 2 * h + 2)
                nc.scalar.activation(mask[:], mask[:], ACT.Exp).then_inc(mask_exp, 1)
                act.wait_ge(r_lo, 8 * h + 8)
                for n in range(KT + 1):
                    if n < KT:
                        t = V_ORDER[n]
                        if n < KT - 1:
                            act.wait_ge(v_mm, 7 * h + n + 1)
                        else:
                            act.wait_ge(w_used, base + 8)
                        if n >= 2:
                            act.wait_ge(v_sum, 8 * h + n - 1)
                        copy(rta[:, n % 2], ps[:, t], accum_out=stat[:, 8 + t:9 + t]).then_inc(v_sum, 1)
                    if n:
                        t = V_ORDER[n - 1]
                        act.wait_ge(v_mean, 8 * h + n)
                        nc.scalar.activation(vrh[:, t], ps[:, t], ACT.Identity,
                                             bias=stat[:, 32 + t:33 + t]).then_inc(v_hi, 1)

                def deviation(ib):
                    act.wait_ge(var_mm, 4 * h + ib + 1)
                    nc.scalar.activation(rstd[:], ps[:, 3, 0:IB], ACT.Sqrt, bias=stat[:, 60:61],
                                         scale=1.0 / R_DV).then_inc(var_std, 1)

                def store(ib):
                    act.wait_ge(o_normed, 16 * h + 4 * ib + 4)
                    act.dma_start(y_d[bass.ds(4 * h, 4)].rearrange("a p n -> p a n")[:, :, ib * IB:(ib + 1) * IB],
                                  ro[:]).then_inc(r_out, 16)

                for j in range(KT):
                    r_probs_hi(h, 0, j)
                for ib in range(R_BLOCKS):
                    ahead = ib + 1 < R_BLOCKS
                    for j in range(R_AHEAD if ahead else 0):
                        r_probs_hi(h, ib + 1, j)
                        if ib and j == 1:
                            deviation(ib - 1)
                        if ib and j == 3:
                            store(ib - 1)
                    if not ahead:
                        deviation(ib - 1)
                        store(ib - 1)
                    act.wait_ge(o_mm, 32 * h + 8 * ib + 8)
                    if ib:
                        act.wait_ge(r_out, 16 * (4 * h + ib))
                    for m in range(4):
                        copy(ro[:, m], ps[:, 4 + m, 0:IB]).then_inc(o_ev, 1)
                    if ahead:
                        for j in range(R_AHEAD, KT):
                            r_probs_hi(h, ib + 1, j)
                    for m in range(4):
                        n = 4 * ib + m
                        act.wait_ge(o_ev, 16 * h + n + 1)
                        if m >= 2:
                            act.wait_ge(o_acc, 16 * h + n - 1)
                        nc.scalar.activation(rsq[:, m % 2], ro[:, m], ACT.Square).then_inc(o_sq, 1)
                if not last_head:
                    act.wait_ge(s_ev, 32 * h + 32)
                    act.dma_start(mask[:], diff_d).then_inc(diff_in, 16)
                deviation(R_BLOCKS - 1)
                store(R_BLOCKS - 1)
                act.wait_ge(r_out, 16 * (4 * h + 4))

            act.wait_ge(trig_sin, 3)
            act.dma_start(mask[:], diff_d).then_inc(diff_in, 16)
            with act.Fori(0, R_HEADS - 1) as h:
                r_head_act(h)
            r_head_act(R_HEADS - 1, last_head=True)
            act.wait_ge(w_used, B_R3)
            act.wait_ge(o_mm, 32 * R_HEADS)
            act.dma_start(x[:], xs_d).then_inc(x_in, 16)
            mix_act(1, B_R3)
            norm_squares(6, x_tiles, **x_made(1))
            norm_std(6)
            norm_bring(7)
            for k in range(KT):
                act.wait_ge(x3_done, KT + k + 1)
                act.dma_start(out_d[:, k], x[:, k]).then_inc(done, 16)

        @block.vector
        def _(dve):
            V = nc.vector

            spread = [0]

            def lo_of(out, value, hi):
                return V.tensor_tensor(out, value, hi.bitcast(F32), ALU.subtract)

            def add_square(n, j, first, acc=nacc, buf=sqb):
                dve.wait_ge(nm_sq, n + 1)
                if first:
                    V.tensor_copy(acc[:], buf[:, j]).then_inc(nm_acc, 1)
                else:
                    dve.wait_ge(nm_acc, n)
                    V.tensor_tensor(acc[:], acc[:], buf[:, j], ALU.add).then_inc(nm_acc, 1)

            def norm_add(m):
                for k in range(NORM_T[m]):
                    add_square(nb[m] + k, k % 2, k == 0)

            def add_both(k):
                add_square(nb[1] + 2 * k, k % 2, k == 0)
                add_square(nb[1] + 2 * k + 1, k % 2, k == 0, nacc2, sqb2)

            def norm_invert(m, at=0):
                dve.wait_ge(nm_std, m + 1)
                V.reciprocal(rr[:, m], stat[:, at:at + KT]).then_inc(nm_r, 1)
                dve.wait_ge(nm_r, m + 1)

            def norm_diag(m):
                if spread[0]:
                    dve.wait_ge(nm_dg, KT * spread[0])
                spread[0] += 1
                for t in range(KT):
                    V.tensor_scalar(diag[:, t], ident[:], rr[:, m, t:t + 1], None, ALU.mult).then_inc(nm_dg, 1)

            def split(q, src, scale, dst, shift=None):
                for k in range(SPLIT_T[q] + 1):
                    if k < SPLIT_T[q]:
                        if sb[q] + k >= 2:
                            dve.wait_ge(sp_lo, sb[q] + k - 1)
                        V.scalar_tensor_tensor(tt[:, k % 2], src(k), scale(k), rb[:], ALU.mult,
                                               ALU.mult).then_inc(sp_t, 1)
                    if k:
                        j = k - 1
                        dve.wait_ge(sp_hi, sb[q] + j + 1)
                        if shift is None:
                            lo_of(dst(j)[1], tt[:, j % 2], dst(j)[0]).then_inc(sp_lo, 1)
                        else:
                            V.scalar_tensor_tensor(dst(j)[1], tt[:, j % 2], shift(j), dst(j)[0].bitcast(F32),
                                                   ALU.add, ALU.subtract).then_inc(sp_lo, 1)

            h_dst = lambda k: (hh[:, k], hl[:, k])

            dve.sem_inc(fnet_ev, 2)
            dve.sem_inc(dn_ev, 2)
            V.memset(stat[:, 60:61], EPS).then_inc(filled, 1)
            V.memset(ones[:], 1.0).then_inc(ones_set, 1)
            for i in range(KT // 2):
                dve.wait_ge(row_std, i + 1)
                V.reciprocal(rr[:, 7, 2 * i:2 * i + 2], stat[:, 16 + 2 * i:18 + 2 * i]).then_inc(row_inv, 1)
                dve.wait_ge(row_inv, i + 1)
                for t in (2 * i, 2 * i + 1):
                    dve.wait_ge(xh_done, t + 1)
                    V.scalar_tensor_tensor(hl[:, t], x[:, t], rr[:, 7, t:t + 1], hh[:, t].bitcast(F32), ALU.mult,
                                           ALU.subtract).then_inc(xl_done, 1)

            def mod_chunk(c, j, src, dst, at, landed):
                dve.wait_ge(wm_in[j], landed)
                out = dst[:, bass.ds(at, WMC)]
                for k in range(KT):
                    w = src[:, j, k * WMC:(k + 1) * WMC]
                    if k == 0:
                        V.tensor_scalar(out, w, silu_c[:, 0:1], None, ALU.mult).then_inc(mod_step, 1)
                    else:
                        dve.wait_ge(mod_step, c * KT + k)
                        V.scalar_tensor_tensor(out, w, silu_c[:, k:k + 1], out, ALU.mult,
                                               ALU.add).then_inc(mod_step, 1)

            dve.wait_ge(c_ready, 1)
            with dve.Fori(0, 4) as i:
                for j in range(2):
                    mod_chunk(2 * i + j, j, wm, macc, (2 * i + j) * WMC, 16 * i + 16)
            dve.wait_ge(mod_mm, 1)
            V.tensor_tensor(modc[:, 0:24], ps[:, 0, 0:24], col("b_mod", 0, 24), ALU.add).then_inc(mod_ready, 1)
            dve.wait_ge(mod_ready, 1)
            V.scalar_tensor_tensor(s1[:], modc[:, 8:16], 1.0, col("g_mix", 0, KT), ALU.add, ALU.mult).then_inc(mod_s, 1)
            V.tensor_scalar(sh2x[:], modc[:, 0:8], L / 512.0, None, ALU.mult).then_inc(mod_s, 1)
            dve.wait_ge(mod_s, 2)

            def first_columns(i):
                z, f = stat[:, 24 + 4 * i:28 + 4 * i], slice(4 * i, 4 * i + 4)
                dve.wait_ge(pq_ev, 8 * i + 8)
                V.tensor_tensor(z, pq[:, 8 * i:8 * i + 8:2, 0], s1[:, f], ALU.mult).then_inc(pq_scaled, 1)
                dve.wait_ge(pq_scaled, 2 * i + 1)
                V.tensor_tensor(z, z, sh2x[:, f], ALU.add).then_inc(pq_scaled, 1)

            def pq_low(f):
                dve.wait_ge(pq_hi, 2 * f + 2)
                hi, lo = pqh[:, f // 2 % 2, f % 2], pql[:, f // 2 % 2, f % 2]
                V.scalar_tensor_tensor(lo, pq[:, 2 * f:2 * f + 2].rearrange("p a n -> p (a n)"), s1[:, f:f + 1],
                                       hi.bitcast(F32), ALU.mult, ALU.subtract).then_inc(pq_lo, 1)
                dve.wait_ge(pq_lo, 2 * f + 1)
                lo_of(lo[:, 0:1], stat[:, 24 + f:25 + f], hi[:, 0:1]).then_inc(pq_lo, 1)

            def z_make(n):
                dve.wait_ge(v_copied, n + 1)
                if n >= 2:
                    dve.wait_ge(z_lo, n - 1)
                u, b = ps[:, 2 * (n % 3)], n % 2
                V.tensor_tensor(zt[:, b, 1:HALF], u[:, 1:HALF], vs[:, 1:HALF], ALU.subtract)
                V.tensor_tensor(zt[:, b, L - 1:HALF:-1], u[:, 1:HALF], vs[:, 1:HALF], ALU.add)
                V.tensor_copy(zt[:, b, 0:1], u[:, 0:1])
                V.tensor_copy(zt[:, b, HALF:HALF + 1], ps[:, 6 + n % 2, 0:1]).then_inc(z_ev, 1)

            def z_low(n):
                dve.wait_ge(z_hi, n + 1)
                lo_of(hl[:, n], zt[:, n % 2], hh[:, n]).then_inc(z_lo, 1)

            first_columns(0)
            first_columns(1)
            pq_low(0)
            pq_low(1)
            for g in range(4):
                if g < 3:
                    pq_low(2 * g + 2)
                    pq_low(2 * g + 3)
                for n in (2 * g, 2 * g + 1):
                    z_make(n)
                    if n:
                        z_low(n - 1)
            z_low(KT - 1)

            def angles(inv, turn, rad, s0):
                step = [s0]

                def then(ins):
                    ins.then_inc(trig_step, 1)
                    step[0] += 1
                    dve.wait_ge(trig_step, step[0])

                then(V.tensor_scalar(ang[:], posf[:], inv, None, ALU.mult))
                then(V.tensor_scalar(turns[:], ang[:], 1.0 / TWO_PI, turn, ALU.mult, ALU.add))
                then(V.tensor_scalar(turns[:], turns[:], ROUND, ROUND, ALU.add, ALU.subtract))
                then(V.scalar_tensor_tensor(ang[:], turns[:], -C1, ang[:], ALU.mult, ALU.add))
                then(V.scalar_tensor_tensor(ang[:], turns[:], -C2, ang[:], ALU.mult, ALU.add))
                then(V.scalar_tensor_tensor(ang[:], turns[:], -C3, ang[:], ALU.mult, ALU.add))
                then(V.tensor_scalar(ang[:], ang[:], rad, PI_IN, ALU.add, ALU.min))

            dve.wait_ge(pos_in, 16)
            V.tensor_copy(posf[:], posi[:]).then_inc(pos_float, 1)
            dve.wait_ge(pos_float, 1)
            angles(col("inv_a"), col("turn_a"), col("rad_a"), 0)
            V.tensor_scalar(ang[:], ang[:], -PI_IN, None, ALU.max).then_inc(trig_step, 1)

            dve.wait_ge(x_in, 16)

            def fnet_update(i, first=False):
                for j in range(2):
                    n = 2 * i + j
                    mod_chunk(8 + n, j, wm_b, macc_b, n * WMC, 16 * i + 80)
                    dve.wait_ge(w_used, B_FNET + 1 + n)
                    xm = x[:, bass.ds(n, 1)].rearrange("p a (b n) -> p (a b) n", b=2)
                    V.scalar_tensor_tensor(xm, ps[:, 2 * j:2 * j + 2], modc[:, bass.ds(16 + n, 1)], xm,
                                           ALU.mult, ALU.add).then_inc(fnet_ev, 1)
                    if not (first and j == 0):
                        add_square(n - 1, 1 - j, first, nacc0, sqb0)

            fnet_update(0, first=True)
            with dve.Fori(1, KT // 2) as i:
                fnet_update(i)
            add_square(KT - 1, 1, False, nacc0, sqb0)
            dve.wait_ge(mod_mm, 2)
            V.tensor_tensor(modc[:, 24:48], ps[:, 4, 0:24], col("b_mod", 24, 24), ALU.add).then_inc(mod_ready, 1)
            dve.wait_ge(mod_ready, 2)
            V.scalar_tensor_tensor(s2[:], modc[:, 32:40], 1.0, col("g_ffn", 0, KT), ALU.add, ALU.mult).then_inc(mod_s, 1)
            dve.wait_ge(mod_s, 3)
            V.tensor_tensor(ga[:], col("g_final1", 0, KT), col("a_norm", 0, KT), ALU.mult).then_inc(ga_set, 1)
            dve.wait_ge(ident_in, 16)
            norm_invert(0)
            norm_diag(0)
            dve.wait_ge(nm_rbs, 1)
            split(0, lambda k: x[:, k], lambda k: s2[:, k:k + 1], h_dst, lambda k: modc[:, 24 + k:25 + k])

            V.memset(gbuf[:, 0:1], 0.0)
            V.memset(gbuf[:, L + 1:L + 2], 0.0).then_inc(filled, 1)

            def hidden(c, base, par_c, first=False):
                for q in range(2):
                    T = 2 * c + q
                    tap = lambda j: par[:, bass.ds(COL["conv"] + j * FFN_T + T, 1)]
                    dve.wait_ge(g_ev, T + 1)
                    V.tensor_scalar(conv[:], gbuf[:, 1:L + 1], tap(1), par[:, bass.ds(COL["b_conv"] + T, 1)],
                                    ALU.mult, ALU.add).then_inc(cv_step, 1)
                    dve.wait_ge(cv_step, 3 * T + 1)
                    V.scalar_tensor_tensor(conv[:], gbuf[:, 0:L], tap(0), conv[:], ALU.mult,
                                           ALU.add).then_inc(cv_step, 1)
                    dve.wait_ge(cv_step, 3 * T + 2)
                    V.scalar_tensor_tensor(conv[:], gbuf[:, 2:L + 2], tap(2), conv[:], ALU.mult,
                                           ALU.add).then_inc(cv_step, 1)
                    dve.wait_ge(silu_done, T + 1)
                    dve.wait_ge(w_used, base + 2 * q + 2)
                    if not (first and q == 0):
                        dve.wait_ge(hid_lo, T)
                    V.tensor_tensor(hid[:].rearrange("p (a n) -> p a n", a=2), ps[:, 2:4],
                                    act_g[:].rearrange("p (a n) -> p a n", a=2), ALU.mult).then_inc(hid_done, 1)
                    dve.wait_ge(hid_hi, T + 1)
                    dve.wait_ge(hid_done, T + 1)
                    lo_of(hidl[:, par_c, q], hid[:], hidh[:, par_c, q]).then_inc(hid_lo, 1)

            def add_down(c, base, mm_base, gate=None, square=None):
                for m in range(KT):
                    d, mm = m // 4, m % 4
                    if mm == 3:
                        dve.wait_ge(w_used, base + d + 1)
                    else:
                        dve.wait_ge(dn_mm, mm_base + 6 * c + 3 * d + mm + 1)
                    dve.wait_ge(dn_ev, dn_base + 8 * c + m + 2)
                    xm = x[:, m].rearrange("p (a n) -> p a n", a=2)
                    out = ps[:, 4 + 2 * (m % 2):6 + 2 * (m % 2)]
                    if gate is None:
                        V.tensor_tensor(xm, out, xm, ALU.add).then_inc(dn_ev, 1)
                    else:
                        V.scalar_tensor_tensor(xm, out, gate(m), xm, ALU.mult, ALU.add).then_inc(dn_ev, 1)
                    if square is not None and m:
                        square(m - 1)
                if square is not None:
                    square(KT - 1)

            dn_base = 0
            gt2 = lambda m: modc[:, 40 + m:41 + m]
            hidden(0, B_FFN, 0, first=True)
            with dve.Fori(0, FFN_T // 4) as i:
                for cc in range(2):
                    at = B_FFN + 4 + 12 * i + 6 * cc
                    hidden(2 * i + cc + 1, at, 1 - cc)
                    add_down(2 * i + cc, at + 4, 0, gt2)
            add_down(FFN_T // 2 - 1, B_A1 - 2, 0, gt2, add_both)
            norm_invert(1)
            V.tensor_tensor(rr[:, 7], rr[:, 1], rr[:, 1], ALU.mult).then_inc(ga_set, 1)
            dve.wait_ge(ga_set, 2)
            V.tensor_tensor(stat[:, 8:8 + KT], ps[:, 7, KT:2 * KT], rr[:, 7], ALU.mult).then_inc(ga_set, 1)
            norm_invert(2)
            dve.wait_ge(ga_set, 3)
            V.tensor_tensor(rr[:, 7], rr[:, 1], rr[:, 2], ALU.mult).then_inc(ga_set, 1)
            dve.wait_ge(ga_set, 4)
            norm_diag(7)
            dve.wait_ge(nm_rbs, 2)
            split(1, lambda k: x[:, k], lambda k: ga[:, k:k + 1], h_dst)
            norm_diag(1)
            for i in range(2):
                V.memset(ub[i][:, 0:8], 0.0)
                last = V.memset(ub[i][:, 8 + L:PADW], 0.0)
            last.then_inc(filled, 1)
            dve.wait_ge(nm_rbs, 3)
            for k in range(KT):
                V.scalar_tensor_tensor(x[:, k], x[:, k], col("g_final1", k), rb2[:], ALU.mult,
                                       ALU.mult).then_inc(x3_done, 1)
            norm_add(3)
            add_square(nb[4], 0, True, tt[:, 0])
            dve.wait_ge(a_ev, 5)
            dve.wait_ge(trig_sin, 1)
            V.tensor_tensor(kt_t[:], kt_t[:], trig_a[:], ALU.mult).then_inc(kr_dve, 1)
            dve.wait_ge(kr_act, 1)
            dve.wait_ge(kr_dve, 1)
            V.tensor_tensor(kt_t[:ROPE], kt_t[:ROPE], ks_t[:ROPE], ALU.add).then_inc(kr_dve, 1)
            dve.wait_ge(kr_act, 2)
            dve.wait_ge(kr_dve, 2)
            lo_of(krl[:ROPE], kt_t[:ROPE], krh[:ROPE]).then_inc(kr_dve, 1)
            norm_invert(3)
            norm_invert(4, KT)
            norm_diag(3)
            dve.wait_ge(nm_rbs, 4)
            norm_diag(4)
            dve.wait_ge(spilled, 16)
            split(2, lambda k: cqf[:, k], lambda k: col("q_norm", k), lambda k: (cqh[:, k], cql[:, k]))
            pstep = [0]

            def pool_tile(q):
                g = POOL_ORDER[q // 2]
                w = pool_window(g)

                def then(ins):
                    ins.then_inc(pool_step, 1)
                    pstep[0] += 1
                    dve.wait_ge(pool_step, pstep[0])

                dve.wait_ge(a_ev, u_unit[q] + 1)
                if q:
                    dve.wait_ge(pool_lo, q)
                u = ub[q % 2]
                src, b = u, 0
                for left, right, lo, hi in pool_levels(g):
                    dst = ub[2 + b]
                    then(V.tensor_tensor(dst[:, 8 + lo:8 + hi], src[:, 8 + lo - left:8 + hi - left],
                                         src[:, 8 + lo + right:8 + hi + right], ALU.add))
                    src, b = dst, 1 - b
                d = ub[2 + b]
                then(V.scalar_tensor_tensor(d[:, 8:8 + L], src[:, 8:8 + L], 1.0 / w, u[:, 8:8 + L], ALU.mult,
                                            ALU.subtract))
                at, left, right = edge_cols(g)
                then(V.tensor_tensor(stat[:, 32:32 + left], src[:, 8:8 + left], par[:, at:at + left], ALU.mult))
                if right:
                    then(V.tensor_tensor(stat[:, 40:40 + right], src[:, 8 + L - right:8 + L],
                                         par[:, at + left:at + left + right], ALU.mult))
                    then(V.tensor_tensor(d[:, 8 + L - right:8 + L], stat[:, 40:40 + right],
                                         u[:, 8 + L - right:8 + L], ALU.subtract))
                V.tensor_tensor(d[:, 8:8 + left], stat[:, 32:32 + left], u[:, 8:8 + left],
                                ALU.subtract).then_inc(pool_d, 1)
                dve.wait_ge(pool_hi, q + 1)
                dve.wait_ge(pool_d, q + 1)
                lo_of(d_lo[q // 2 % 2][:, q % 2], d[:, 8:8 + L], d_hi[q // 2 % 2][:, q % 2]).then_inc(pool_lo, 1)

            pool_tile(0)
            dve.wait_ge(nm_rbs, 5)
            split(3, lambda k: cqf[:, 3], lambda k: col("kv_norm"), lambda k: (ckh[:, 0], ckl[:, 0]))
            for q in range(1, KT):
                pool_tile(q)

            dve.sem_inc(tp_lo, 1)

            def project_lo(h, u, b, bank):
                dve.wait_ge(ax_hi, 6 * h + (1, 2, 0, 0, 3, 4, 5, 6)[u])
                hi_t, lo_t = ((qnh, qnl), None, (knh, knl), (vvh, vvl))[u // 2]
                f = slice((u % 2) * HALF, (u % 2 + 1) * HALF)
                lo_of(lo_t[:, b, f], ps[:, 6 + bank], hi_t[:, b, f]).then_inc(aux_ev, 1)

            def rope_turn(h, f, bank, n_mm):
                dve.wait_ge(aux_mm, n_mm)
                if not (isinstance(h, int) and h == 0):
                    dve.wait_ge(rope_lo, 2 * h + f - 1)
                V.tensor_tensor(rt[:, f], ps[:, 6 + bank], trig_a[:, f * HALF:(f + 1) * HALF],
                                ALU.mult).then_inc(aux_ev, 1)

            def rope_add(h, f, n_ev):
                dve.wait_ge(rope_shift, 2 * h + f + 1)
                dve.wait_ge(aux_ev, n_ev)
                V.tensor_tensor(rf_t[:ROPE, f], rt[:ROPE, f], rs_t[:ROPE, f], ALU.add).then_inc(rope_sum, 1)

            def rope_low(h, f, b):
                dve.wait_ge(rope_hi, 2 * h + f + 1)
                dve.wait_ge(rope_sum, 2 * h + f + 1)
                at = slice(f * HALF, (f + 1) * HALF)
                lo_of(qr[ROPE:, b, at], rf_t[:ROPE, f], qr[:ROPE, b, at]).then_inc(rope_lo, 1)

            def row_maximum(h, t):
                dve.wait_ge(sc_mm, 8 * h + t + 1)
                m, n = stat[:, 24 + t % 4:25 + t % 4], stat[:, 28 + t % 4:29 + t % 4]
                V.tensor_reduce(m, ps[:, 2 * (t % 2):2 * (t % 2) + 2].rearrange("p a n -> p (a n)"), AX_X,
                                ALU.max).then_inc(row_max, 1)
                dve.wait_ge(row_max, 8 * h + t + 1)
                V.tensor_scalar(n, m, -ATT_SCALE, None, ALU.mult).then_inc(row_bias, 1)

            def normalise(h, t):
                dve.wait_ge(exp_done, 8 * h + t + 3)
                r = stat[:, 52 + t % 4:53 + t % 4]
                V.reciprocal(r, stat[:, 48 + t % 4:49 + t % 4]).then_inc(sum_inv, 1)
                dve.wait_ge(sum_inv, 8 * h + t + 1)
                V.tensor_scalar(prob[:, t % 4], prob[:, t % 4], r, None, ALU.mult).then_inc(prob_ok, 1)

            def turned_lo(h, t):
                j = t // 2
                dve.wait_ge(tp_hi, 8 * h + t + 1)
                at = slice((t % 2) * P, (t % 2 + 1) * P)
                lo_of(ptl[:, j % 2, :, at], ps[:, 4:6].rearrange("p a (b n) -> p (a b) n", n=P),
                      pth[:, j % 2, :, at]).then_inc(tp_lo, 1)

            def bring_o(h, j):
                at, i = pair_at(h, j)
                dve.wait_ge(aux_mm, unit_mm(at, i))
                dve.wait_ge(o_out[j % 2], 16 * (2 * h + j // 2 + 1))
                V.tensor_copy(osb[:, j % 2], ps[:, 6 + unit_bank(at, i), 0:256]).then_inc(aux_ev, 1)

            def head_dve(h, b, first=False, last_head=False):
                for t in range(KT):
                    row_maximum(h, t)
                    if t:
                        normalise(h, t - 1)
                    elif not first:
                        normalise(h - 1, 7)
                    if t in (0, 2) and not first:
                        bring_o(h - 1, 2 + t // 2)
                    if t in (4, 6):
                        bring_o(h, t // 2 - 2)
                    if t >= 2:
                        turned_lo(h, t - 2)
                    elif not first:
                        turned_lo(h - 1, t + 6)
                    if not last_head:
                        for u in STEP_P[t]:
                            i = UNITS_P[u]
                            if u in (2, 3):
                                rope_turn(h + 1, u - 2, i % 2, unit_mm(h, i))
                            else:
                                project_lo(h + 1, u, 1 - b, i % 2)
                        if t == 4:
                            rope_add(h + 1, 0, unit(h, UNITS_P[2]) + 1)
                        if t == 5:
                            rope_add(h + 1, 1, unit(h, UNITS_P[3]) + 1)
                            rope_low(h + 1, 0, 1 - b)
                        if t == 6:
                            rope_low(h + 1, 1, 1 - b)
                if last_head:
                    normalise(h, 7)
                    bring_o(h, 2)
                    turned_lo(h, 6)
                    turned_lo(h, 7)
                    dve.wait_ge(tp_mm, 4 + 8 * HEADS)
                    norm_diag(2)
                    bring_o(h, 3)

            for u in (0, 1):
                project_lo(0, u, 0, u)
            for f in range(2):
                rope_turn(0, f, f, 3 + f)
            for f in range(2):
                rope_add(0, f, 3 + f)
            for u in (4, 5):
                project_lo(0, u, 0, u - 4)
            for f in range(2):
                rope_low(0, f, 0)
            for u in (6, 7):
                project_lo(0, u, 0, u - 6)
            head_dve(0, 0, first=True)
            with dve.Fori(0, HEADS // 2 - 1) as i:
                head_dve(2 * i + 1, 1)
                head_dve(2 * i + 2, 0)
            head_dve(HEADS - 1, 1, last_head=True)

            dve.wait_ge(nm_rbs, 6)
            dve.wait_ge(x_in, 32)
            dve.wait_ge(aux_mm, unit_mm(HEADS - 1, 14))
            split(4, lambda k: x[:, k], lambda k: col("a_norm", k), h_dst)

            g_abs, g_e, g_z, g_z2, g_p = [lgam[:, 8 * i:8 * i + 8] for i in range(5)]
            gstep = [0]

            def then(ins):
                ins.then_inc(gam_step, 1)
                gstep[0] += 1
                dve.wait_ge(gam_step, gstep[0])

            dec = col("decay", 0, 8)
            then(V.scalar_tensor_tensor(g_abs, dec, -1.0, dec, ALU.mult, ALU.max))
            dve.wait_ge(gam_exp, 1)
            then(V.tensor_scalar(g_p, g_e, 2.0, None, ALU.add))
            then(V.reciprocal(g_z, g_p))
            then(V.tensor_tensor(g_z, g_z, g_e, ALU.mult))
            then(V.tensor_tensor(g_z2, g_z, g_z, ALU.mult))
            then(V.tensor_scalar(g_p, g_z2, 1.0 / 19, None, ALU.mult))
            for n in range(17, 1, -2):
                then(V.scalar_tensor_tensor(g_p, g_p, 1.0 / n, g_z2, ALU.add, ALU.mult))
            then(V.scalar_tensor_tensor(g_p, g_p, 1.0, g_z, ALU.add, ALU.mult))
            then(V.tensor_scalar(g_abs, dec, 0.0, None, ALU.min))
            then(V.scalar_tensor_tensor(g_abs, g_p, -2.0, g_abs, ALU.mult, ALU.add))
            then(V.tensor_scalar(g_e, g_abs, -1.0, None, ALU.mult))
            def gate_dve(c, b, base, Tb, y_count):
                dve.wait_ge(y_in[b], y_count)
                for q in range(2):
                    T = 2 * c + q
                    dve.wait_ge(silu_done, Tb + T + 1)
                    dve.wait_ge(hid_lo, Tb + T)
                    V.tensor_tensor(yg[:], sg[:], ybuf[:, b, q], ALU.mult).then_inc(hid_done, 1)
                    dve.wait_ge(hid_hi, Tb + T + 1)
                    dve.wait_ge(hid_done, Tb + T + 1)
                    lo_of(hidl[:, b, q], yg[:], hidh[:, b, q]).then_inc(hid_lo, 1)

            def mix_dve(f, B):
                nonlocal dn_base
                Tb, dn_base = FFN_T + 16 * f, 8 * (FFN_T // 2 + N_MC * f)
                mb, y0 = 6 * (FFN_T // 2 + N_MC * f), 16 * (N_MC // 2) * f
                gate_dve(0, 0, B, Tb, y0 + 16)
                with dve.Fori(0, N_MC // 2 - 1) as i:
                    gate_dve(2 * i + 1, 1, B, Tb, y0 + 16 * i + 16)
                    add_down(2 * i, B + 4 + 8 * i, mb)
                    gate_dve(2 * i + 2, 0, B, Tb, y0 + 16 * i + 32)
                    add_down(2 * i + 1, B + 8 + 8 * i, mb)
                gate_dve(N_MC - 1, 1, B, Tb, y0 + 16 * (N_MC // 2))
                add_down(N_MC - 2, B + 4 * N_MC - 4, mb)
                add_down(N_MC - 1, B + 4 * N_MC - 2, mb,
                         square=lambda k: add_square(nb[5 + f] + k, k % 2, k == 0))

            mix_dve(0, B_A3)
            norm_invert(5)
            norm_diag(5)
            dve.wait_ge(nm_rbs, 7)
            dve.wait_ge(dn_ev, 2 + 8 * (FFN_T // 2 + N_MC))
            split(5, lambda k: x[:, k], lambda k: col("r_norm", k), h_dst)

            dve.wait_ge(pos_in, 32)
            V.tensor_copy(posf[:], posi[:]).then_inc(pos_float, 1)
            dve.wait_ge(pos_float, 2)
            angles(col("inv_r"), 0.25, float(np.pi / 2), 8)
            V.tensor_scalar(ang[:], ang[:], -PI_IN, None, ALU.max).then_inc(trig_step, 1)
            dve.wait_ge(trig_sin, 2)
            dve.wait_ge(trig_step, 16)
            angles(col("inv_r"), 0.0, 0.0, 16)
            V.tensor_scalar(ang[:], ang[:], -PI_IN, None, ALU.max).then_inc(trig_step, 1)

            dve.wait_ge(spilled, 32)
            dve.wait_ge(trig_sin, 3)

            def r_block(h, ib, j0, j1):
                for j in range(j0, j1 + 1):
                    n = 32 * h + 8 * ib + j
                    if j < j1:
                        s = ib * KT + j
                        dve.wait_ge(s_mm, n + 1)
                        if s >= 2:
                            dve.wait_ge(p_lo, n - 1)
                        at = ib * IB - j * P + L - P
                        V.scalar_tensor_tensor(rsm[:, j % 2], ps[:, s % 3, 0:IB], R_DK ** -0.5,
                                               mask[:, at:at + IB], ALU.mult, ALU.mult).then_inc(s_ev, 1)
                    if j > j0:
                        dve.wait_ge(p_hi, n)
                        dve.wait_ge(s_ev, n)
                        lo_of(rpl[:, j - 1], rsm[:, (j - 1) % 2], rph[:, j - 1]).then_inc(p_lo, 1)

            with dve.Fori(0, R_HEADS) as h:
                for u in range(4):
                    hi_t, lo_t = ((rqh, rql), (rkh, rkl))[u // 2]
                    b0, f = 4 * (u // 2), u % 2
                    dve.wait_ge(w_used, B_R2 + 8 * h + 2 * (u // 2) + 2)
                    if u:
                        dve.wait_ge(r_lo, 8 * h + 2 * u)
                    tok = slice(f * HALF, (f + 1) * HALF)
                    x1, x2 = ps[:, b0 + f], ps[:, b0 + 2 + f]
                    V.tensor_tensor(rta[:, 0], x1, cos_r[:, tok], ALU.mult)
                    V.tensor_tensor(rta[:, 1], x2, sin_r[:, tok], ALU.mult)
                    V.tensor_tensor(rta[:, 2], x2, cos_r[:, tok], ALU.mult)
                    V.tensor_tensor(rta[:, 3], x1, sin_r[:, tok], ALU.mult).then_inc(r_ev, 1)
                    dve.wait_ge(r_ev, 4 * h + u + 1)
                    V.tensor_tensor(rta[:, 0], rta[:, 0], rta[:, 1], ALU.subtract).then_inc(r_sum, 1)
                    V.tensor_tensor(rta[:, 2], rta[:, 2], rta[:, 3], ALU.add).then_inc(r_sum, 1)
                    for m in range(2):
                        dve.wait_ge(r_hi, 8 * h + 2 * u + m + 1)
                        dve.wait_ge(r_sum, 8 * h + 2 * u + m + 1)
                        lo_of(lo_t[:, m, tok], rta[:, 2 * m], hi_t[:, m, tok]).then_inc(r_lo, 1)
                dve.wait_ge(diff_in, 16 * h + 16)
                dve.wait_ge(r_lo, 8 * h + 8)
                V.tensor_scalar(mtmp[:], mask[:], lgam[:, bass.ds(h + 12, 1)], None, ALU.mult).then_inc(mask_step, 1)
                dve.wait_ge(mask_step, 2 * h + 1)
                V.scalar_tensor_tensor(mask[:], mask[:], lgam[:, bass.ds(h, 1)], mtmp[:], ALU.mult,
                                       ALU.min).then_inc(mask_step, 1)
                dve.wait_ge(mask_step, 2 * h + 2)
                for n in range(KT + 1):
                    if n < KT:
                        t = V_ORDER[n]
                        dve.wait_ge(v_sum, 8 * h + n + 1)
                        V.tensor_scalar(stat[:, 32 + t:33 + t], stat[:, 8 + t:9 + t], -1.0 / R_DV, None,
                                        ALU.mult).then_inc(v_mean, 1)
                    if n:
                        t = V_ORDER[n - 1]
                        dve.wait_ge(v_hi, 8 * h + n)
                        dve.wait_ge(v_mean, 8 * h + n)
                        V.scalar_tensor_tensor(vrl[:, t], ps[:, t], stat[:, 32 + t:33 + t],
                                               vrh[:, t].bitcast(F32), ALU.add, ALU.subtract).then_inc(v_lo, 1)
                dve.wait_ge(mask_exp, h + 1)

                def normalise_outputs(ib):
                    dve.wait_ge(var_std, 4 * h + ib + 1)
                    V.reciprocal(rinv[:], rstd[:]).then_inc(var_inv, 1)
                    dve.wait_ge(var_inv, 4 * h + ib + 1)
                    for m in range(4):
                        V.scalar_tensor_tensor(ro[:, m], ro[:, m], par[:, bass.ds(COL["gn"] + m + 4 * h, 1)], rinv[:],
                                               ALU.mult, ALU.mult).then_inc(o_normed, 1)

                r_block(h, 0, 0, KT)
                for ib in range(R_BLOCKS):
                    if ib + 1 < R_BLOCKS:
                        r_block(h, ib + 1, 0, 2)
                        if ib:
                            normalise_outputs(ib - 1)
                        r_block(h, ib + 1, 2, R_AHEAD)
                        r_block(h, ib + 1, R_AHEAD, KT)
                    else:
                        normalise_outputs(ib - 1)
                    for m in range(4):
                        n = 16 * h + 4 * ib + m
                        dve.wait_ge(o_sq, n + 1)
                        if m == 0:
                            V.tensor_copy(roa[:], rsq[:, 0]).then_inc(o_acc, 1)
                        else:
                            dve.wait_ge(o_acc, n)
                            V.tensor_tensor(roa[:], roa[:], rsq[:, m % 2], ALU.add).then_inc(o_acc, 1)
                normalise_outputs(R_BLOCKS - 1)
            dve.wait_ge(x_in, 48)
            mix_dve(1, B_R3)
            norm_invert(6)
            norm_diag(6)
            dve.wait_ge(nm_rbs, 8)
            dve.wait_ge(dn_ev, 2 + 8 * (FFN_T // 2 + 2 * N_MC))
            for k in range(KT):
                V.scalar_tensor_tensor(x[:, k], x[:, k], col("final", k), rb[:], ALU.mult,
                                       ALU.mult).then_inc(x3_done, 1)


def host_panels(a):
    pan = np.zeros((N_PANELS, P, D), np.float32)
    at = [0]

    def put(*parts):
        pan[at[0]] = np.concatenate(parts, axis=1)
        at[0] += 1

    def cols(w, c0, k0=0, kn=KT, width=P):
        return np.concatenate([w[(k0 + k) * P:(k0 + k + 1) * P, c0:c0 + width] for k in range(kn)], axis=1)

    def down(w, c):
        for d in range(2):
            put(*[cols(w, (4 * d + m) * P, 2 * c, 2) for m in range(4)])

    n = np.arange(L)
    turn = np.outer(n, np.arange(HALF)) % L
    cos = (np.cos(2 * np.pi * turn / L) / 512).astype(np.float32)
    sin = (np.sin(2 * np.pi * turn / L) / 512).astype(np.float32)
    sin[:, 0] = np.where(n % 2 == 0, 1.0, -1.0) / 512
    for _ in range(2):
        for t in range(KT):
            put(cos[t * P:(t + 1) * P], sin[t * P:(t + 1) * P])
    m = np.arange(FNET_C)
    turn = np.outer(m, m) % FNET_C
    cc = np.cos(2 * np.pi * turn / FNET_C).astype(np.float32)
    ss = np.sin(2 * np.pi * turn / FNET_C).astype(np.float32)
    put(*[cols(w, q * P, 0, 2) for w in (cc, ss) for q in range(2)])
    w = a["w_fnet_out"][0]
    for q in range(KT):
        put(cols(w, q * P))
    assert at[0] == B_FFN
    w, wd = a["w_ffn_up"][0], a["w_ffn_down"][0]

    def up(c):
        for q in range(2):
            put(cols(w, (2 * c + q) * P))
            put(cols(w, FFN + (2 * c + q) * P))

    up(0)
    for c in range(FFN_T // 2 - 1):
        up(c + 1)
        down(wd, c)
    down(wd, FFN_T // 2 - 1)
    assert at[0] == B_A1
    w = a["a_w_in_2"][0]
    o_kv, o_kr = Q_LORA, Q_LORA + KV_LORA
    o_u = o_kr + ROPE
    o_g = o_u + POOL_G * POOL_C
    for q in range(3):
        put(cols(w, q * P))
    put(cols(w, o_kv))
    kr = w[:, o_kr:o_kr + ROPE]
    put(cols(np.concatenate([kr, kr[:, 32:], kr[:, :32]], axis=1), 0))
    pw = a["a_pool_w_2"][0]

    def put_pool(g):
        w_g = pw[POOL_ORDER[g]]
        put(cols(w_g, 0, 0, 2), cols(w_g, P, 0, 2), np.zeros((P, HALF), np.float32))

    for q in range(KT):
        put(cols(w, o_u + (2 * POOL_ORDER[q // 2] + q % 2) * P))
        if q in (5, 7):
            put_pool((q - 5) // 2)
    put_pool(2)
    put_pool(3)
    assert at[0] == B_A2
    wq, wkv = a["a_w_uq_2"][0], a["a_w_ukv_2"][0]
    for h in range(HEADS):
        q = wq[:, h * 192:(h + 1) * 192]
        r = q[:, NOPE:]
        put(cols(q, 0, 0, 3), cols(np.concatenate([r, r[:, 32:], r[:, :32]], axis=1), 0, 0, 3),
            wkv[:, h * 256:(h + 1) * 256])
    assert at[0] == B_A3

    def mix(w_gate, w_out):
        def gate(c):
            for q in range(2):
                put(cols(w_gate, (2 * c + q) * P))

        gate(0)
        for c in range(MIX // P // 2 - 1):
            gate(c + 1)
            down(w_out, c)
        down(w_out, MIX // P // 2 - 1)

    mix(w[:, o_g:], a["a_w_out_2"][0])
    assert at[0] == B_R2
    w = a["r_w_in_2"][0]
    for h in range(R_HEADS):
        for o in (0, R_HEADS * R_DK):
            for q in range(2):
                put(cols(w, o + h * R_DK + q * P))
        v = w[:, 2 * R_HEADS * R_DK + h * R_DV:2 * R_HEADS * R_DK + (h + 1) * R_DV]
        for k in range(0, KT, 2):
            put(v[k * P:(k + 1) * P], v[(k + 1) * P:(k + 2) * P])
    assert at[0] == B_R3
    mix(w[:, 2 * R_HEADS * R_DK + R_HEADS * R_DV:], a["r_w_out_2"][0])
    assert at[0] == N_PANELS
    return pan


def host_params(a):
    t = np.zeros((P, N_COL), np.float32)

    def put(name, v, i=0):
        v = np.asarray(v, np.float32).reshape(-1, P).T
        t[:, COL[name] + i:COL[name] + i + v.shape[1]] = v

    put("c", a["c"][0])
    put("b_mod", a["b_mod"][0])
    put("g_mix", a["g_norm_mix"][0])
    put("g_ffn", a["g_norm_ffn"][0])
    put("conv", a["w_ffn_conv"][0].reshape(-1))
    put("b_conv", a["b_ffn_conv"][0])
    put("g_final1", a["g_final"])
    put("a_norm", a["a_norm_g_2"][0])
    put("q_norm", a["a_q_norm_g_2"][0])
    put("kv_norm", a["a_kv_norm_g_2"][0])
    put("pool_scale", a["a_pool_scale_2"][0])
    put("r_norm", a["r_norm_g_2"][0])
    put("gn", a["r_gn_g_2"][0])
    put("final", a["final_norm_g_2"])
    t[:, COL["decay"]:COL["decay"] + 4] = a["r_decay_fwd_2"]
    t[:, COL["decay"] + 4:COL["decay"] + 8] = a["r_decay_bwd_2"]
    f32 = np.float32
    inv_a = f32(1.0) / (10000.0 ** (np.arange(0, ROPE, 2) / ROPE)).astype(f32)
    inv_r = f32(1.0) / (10000.0 ** (np.arange(0, R_DK, 2) / R_DK)).astype(f32)
    t[:, COL["inv_a"]] = np.concatenate([inv_a, inv_a, -inv_a, inv_a])
    t[:64, COL["turn_a"]] = 0.25
    t[:64, COL["rad_a"]] = np.pi / 2
    t[:, COL["inv_r"]] = inv_r
    for g in range(POOL_G):
        at, left, right = edge_cols(g)
        n = np.concatenate([np.arange(left) + left, left * 2 - 1 - np.arange(right)])
        t[:, at:at + left + right] = (1.0 / n).astype(f32)
    return t


def kernel(**inputs):
    import concourse.bacc as bacc
    from concourse.bass_utils import run_bass_kernel_spmd

    a = {k: np.asarray(v) for k, v in inputs.items()}
    xm = a["x"][0]
    wm = a["w_mod"][0].reshape(KT, P, 16, 384).transpose(2, 1, 0, 3).reshape(16, P, KT * 384)
    arrays = {
        "xt": np.ascontiguousarray(xm.reshape(KT, P, D).transpose(1, 0, 2)),
        "xf": np.ascontiguousarray(xm.T.reshape(KT, P, L).transpose(1, 0, 2)),
        "panels": host_panels(a),
        "w_mod_chunks": np.ascontiguousarray(wm),
        "params": host_params(a),
        "positions": np.ascontiguousarray(np.broadcast_to(a["positions_2"].reshape(1, L), (P, L))),
        "ident_c": np.eye(P, dtype=np.float32),
        "diff_c": (np.arange(MASK_W)[None, :] - (L - P) - np.arange(P)[:, None]).astype(np.float32),
    }
    nc = bacc.Bacc("TRN2", target_bir_lowering=False, num_devices=1)
    args = [nc.dram_tensor(k, v.shape, mybir.dt.from_np(v.dtype), kind="ExternalInput").ap() for k, v in arrays.items()]
    out = nc.dram_tensor("out", (P, KT, L), F32, kind="ExternalOutput").ap()
    build(nc, *args, out)
    r = run_bass_kernel_spmd(nc, [arrays], core_ids=[0])
    y = r.results[0]["out"]
    return np.ascontiguousarray(y.transpose(1, 0, 2).reshape(D, L).T).reshape(1, L, D)
```
